# Optimizing a Trainium2 kernel written in Bass

```python
import math
import jax, jax.numpy as jnp
from jax import lax
import numpy as np

D_MODEL = 1024
BATCH = 1
SEQ = 512
DEPTH = 2

N_MIXERS = 4
EPS = 1e-6
Q_BLOCK = 128
D_FF = 4 * D_MODEL

DSA_HEADS = 8
DSA_HEAD_DIM = D_MODEL // DSA_HEADS
IDX_HEADS = 8
IDX_DIM = 64
TOPK_MAX = 256
DSA_IN = 3 * D_MODEL + IDX_HEADS * IDX_DIM + IDX_DIM + IDX_HEADS

CONV_WIDTH = 31

MLA_HEADS = 16
MLA_Q_LORA = 384
MLA_KV_LORA = 256
MLA_NOPE = 64
MLA_ROPE = 32
MLA_V = 64
ROPE_THETA = 10000.0
MLA_IN = MLA_Q_LORA + MLA_KV_LORA + MLA_ROPE

GDN_HEADS = 8
GDN_DK = 128
GDN_DV = 128
GDN_CONV = 4
GDN_CHUNK = 64
GDN_HK = GDN_HEADS * GDN_DK
GDN_HV = GDN_HEADS * GDN_DV
GDN_IN = 2 * GDN_HK + 2 * GDN_HV + 2 * GDN_HEADS


def rmsnorm(x, g):
    xf = x.astype(jnp.float32)
    y = xf * lax.rsqrt(jnp.mean(xf * xf, axis=-1, keepdims=True) + EPS)
    return (y * g.astype(jnp.float32)).astype(x.dtype)

def layernorm(x, g, b):
    xf = x.astype(jnp.float32)
    mu = jnp.mean(xf, axis=-1, keepdims=True)
    var = jnp.mean(jnp.square(xf - mu), axis=-1, keepdims=True)
    y = (xf - mu) * lax.rsqrt(var + EPS) * g.astype(jnp.float32) + b.astype(jnp.float32)
    return y.astype(x.dtype)

def l2norm(x):
    return x * lax.rsqrt(jnp.sum(x * x, axis=-1, keepdims=True) + EPS)

def causal_depthwise_conv(x, w):
    width = w.shape[0]
    xp = jnp.pad(x, ((0, 0), (width - 1, 0), (0, 0)))
    return lax.conv_general_dilated(xp, w[:, None, :].astype(x.dtype), window_strides=(1,), padding='VALID',
                                    dimension_numbers=('NWC', 'WIO', 'NWC'), feature_group_count=x.shape[-1])

def rope_tables(length, dim):
    pos = jnp.arange(length, dtype=jnp.float32)
    inv_freq = ROPE_THETA ** (-jnp.arange(0, dim, 2, dtype=jnp.float32) / dim)
    ang = pos[:, None] * inv_freq[None, :]
    return jnp.cos(ang), jnp.sin(ang)

def apply_rope(x, cos, sin):
    xf = x.astype(jnp.float32)
    half = x.shape[-1] // 2
    x1, x2 = xf[..., :half], xf[..., half:]
    return jnp.concatenate([x1 * cos - x2 * sin, x2 * cos + x1 * sin], axis=-1).astype(x.dtype)

def blocked_queries(fn, *qs):
    b, length = qs[0].shape[0], qs[0].shape[1]
    nb = length // Q_BLOCK
    blks = [jnp.moveaxis(q.reshape(b, nb, Q_BLOCK, *q.shape[2:]), 1, 0) for q in qs]
    t0 = jnp.arange(nb, dtype=jnp.int32) * Q_BLOCK
    out = lax.map(lambda a: fn(*a), (t0, *blks))
    out = jnp.moveaxis(out, 0, 1)
    return out.reshape(b, length, *out.shape[3:])

def dsa_mixer(h, w_in, idx_k_g, idx_k_b, w_out):
    b, length, _ = h.shape
    topk = min(TOPK_MAX, length // 4)
    proj = h @ w_in
    o1 = D_MODEL; o2 = 2 * D_MODEL; o3 = 3 * D_MODEL
    o4 = o3 + IDX_HEADS * IDX_DIM; o5 = o4 + IDX_DIM
    q = proj[..., :o1].reshape(b, length, DSA_HEADS, DSA_HEAD_DIM)
    k = proj[..., o1:o2].reshape(b, length, DSA_HEADS, DSA_HEAD_DIM)
    v = proj[..., o2:o3].reshape(b, length, DSA_HEADS, DSA_HEAD_DIM)
    qi = proj[..., o3:o4].reshape(b, length, IDX_HEADS, IDX_DIM).astype(jnp.float32)
    ki = layernorm(proj[..., o4:o5], idx_k_g, idx_k_b).astype(jnp.float32)
    wi = proj[..., o5:].astype(jnp.float32) * (IDX_HEADS ** -0.5 * IDX_DIM ** -0.5)
    key_pos = jnp.arange(length, dtype=jnp.int32)
    scale = DSA_HEAD_DIM ** -0.5

    def block(t0, qb, qib, wib):
        qpos = t0 + jnp.arange(Q_BLOCK, dtype=jnp.int32)
        causal = key_pos[None, :] <= qpos[:, None]
        s = jax.nn.relu(jnp.einsum('bqhd,bsd->bqhs', qib, ki))
        score = jnp.einsum('bqh,bqhs->bqs', wib, s)
        score = jnp.where(causal[None], score, -jnp.inf)
        _, sel = lax.top_k(score, topk)
        valid = sel <= qpos[None, :, None]
        k_sel = jax.vmap(lambda kk, ii: kk[ii])(k, sel)
        v_sel = jax.vmap(lambda vv, ii: vv[ii])(v, sel)
        logits = jnp.einsum('bqhd,bqkhd->bqhk', qb, k_sel).astype(jnp.float32) * scale
        logits = jnp.where(valid[:, :, None, :], logits, -jnp.inf)
        p = jax.nn.softmax(logits, axis=-1)
        return jnp.einsum('bqhk,bqkhd->bqhd', p.astype(v.dtype), v_sel)

    o = blocked_queries(block, q, qi, wi)
    return o.reshape(b, length, D_MODEL) @ w_out

def conv_mixer(h, w_pw1, b_pw1, w_dw, b_dw, ln_g, ln_b, w_pw2, b_pw2):
    a = h @ w_pw1 + b_pw1
    u = a[..., :D_MODEL] * jax.nn.sigmoid(a[..., D_MODEL:])
    u = causal_depthwise_conv(u, w_dw) + b_dw
    u = jax.nn.silu(layernorm(u, ln_g, ln_b))
    return u @ w_pw2 + b_pw2

def mla_mixer(h, w_in, q_norm_g, w_uq, kv_norm_g, w_ukv, w_out):
    b, length, _ = h.shape
    proj = h @ w_in
    cq = rmsnorm(proj[..., :MLA_Q_LORA], q_norm_g)
    ckv = rmsnorm(proj[..., MLA_Q_LORA:MLA_Q_LORA + MLA_KV_LORA], kv_norm_g)
    kr = proj[..., MLA_Q_LORA + MLA_KV_LORA:]
    q = (cq @ w_uq).reshape(b, length, MLA_HEADS, MLA_NOPE + MLA_ROPE)
    kv = (ckv @ w_ukv).reshape(b, length, MLA_HEADS, MLA_NOPE + MLA_V)
    q_nope, q_rope = q[..., :MLA_NOPE], q[..., MLA_NOPE:]
    k_nope, v = kv[..., :MLA_NOPE], kv[..., MLA_NOPE:]
    cos, sin = rope_tables(length, MLA_ROPE)
    q_rope = apply_rope(q_rope, cos[None, :, None, :], sin[None, :, None, :])
    kr = apply_rope(kr, cos[None], sin[None])
    key_pos = jnp.arange(length, dtype=jnp.int32)
    scale = (MLA_NOPE + MLA_ROPE) ** -0.5

    def block(t0, qn, qr):
        qpos = t0 + jnp.arange(Q_BLOCK, dtype=jnp.int32)
        causal = key_pos[None, :] <= qpos[:, None]
        logits = (jnp.einsum('bqhd,bshd->bhqs', qn, k_nope)
                  + jnp.einsum('bqhr,bsr->bhqs', qr, kr)).astype(jnp.float32) * scale
        logits = jnp.where(causal[None, None], logits, -jnp.inf)
        p = jax.nn.softmax(logits, axis=-1)
        return jnp.einsum('bhqs,bshd->bqhd', p.astype(v.dtype), v)

    o = blocked_queries(block, q_nope, q_rope)
    return o.reshape(b, length, MLA_HEADS * MLA_V) @ w_out

def chunk_gated_delta_rule(q, k, v, g, beta):
    b, length, nh, dk = q.shape
    dv = v.shape[-1]
    c = GDN_CHUNK
    n = length // c

    def to_chunks(x):
        return jnp.moveaxis(x.reshape(b, n, c, nh, *x.shape[3:]), 3, 1)

    q, k, v, g, beta = to_chunks(q), to_chunks(k), to_chunks(v), to_chunks(g), to_chunks(beta)
    gc = jnp.cumsum(g, axis=-1)
    tril = jnp.tril(jnp.ones((c, c), dtype=bool))
    tril_strict = jnp.tril(jnp.ones((c, c), dtype=bool), -1)
    diff = gc[..., :, None] - gc[..., None, :]
    decay_mat = jnp.where(tril, jnp.exp(jnp.where(tril, diff, 0.0)), 0.0)
    kk = jnp.einsum('bhncd,bhnsd->bhncs', k, k)
    a_mat = jnp.where(tril_strict, beta[..., :, None] * kk * decay_mat, 0.0)
    eye = jnp.eye(c, dtype=jnp.float32)
    rhs = jnp.concatenate([v * beta[..., None], k * (beta * jnp.exp(gc))[..., None]], axis=-1)
    sol = lax.linalg.triangular_solve(eye + a_mat, rhs, left_side=True, lower=True, unit_diagonal=True)
    u, w = sol[..., :dv], sol[..., dv:]
    qk = jnp.einsum('bhncd,bhnsd->bhncs', q, k) * decay_mat
    q_dec = q * jnp.exp(gc)[..., None]
    k_dec = k * jnp.exp(gc[..., -1:] - gc)[..., None]
    g_last = jnp.exp(gc[..., -1])

    xs = (jnp.moveaxis(u, 2, 0), jnp.moveaxis(w, 2, 0), jnp.moveaxis(qk, 2, 0),
          jnp.moveaxis(q_dec, 2, 0), jnp.moveaxis(k_dec, 2, 0), jnp.moveaxis(g_last, 2, 0))

    def step(s, inp):
        u_c, w_c, qk_c, qd_c, kd_c, gl_c = inp
        v_new = u_c - jnp.einsum('bhcd,bhdv->bhcv', w_c, s)
        o_c = jnp.einsum('bhcd,bhdv->bhcv', qd_c, s) + jnp.einsum('bhcs,bhsv->bhcv', qk_c, v_new)
        s = s * gl_c[..., None, None] + jnp.einsum('bhcd,bhcv->bhdv', kd_c, v_new)
        return s, o_c

    s0 = jnp.zeros((b, nh, dk, dv), dtype=jnp.float32)
    _, o = lax.scan(step, s0, xs)
    return jnp.transpose(o, (1, 0, 3, 2, 4)).reshape(b, length, nh, dv)

def gdn_mixer(h, w_in, conv_w, a_log, dt_bias, o_norm_g, w_out):
    b, length, _ = h.shape
    proj = h @ w_in
    n_qkv = 2 * GDN_HK + GDN_HV
    qkv = jax.nn.silu(causal_depthwise_conv(proj[..., :n_qkv], conv_w))
    gate = proj[..., n_qkv:n_qkv + GDN_HV].reshape(b, length, GDN_HEADS, GDN_DV).astype(jnp.float32)
    b_raw = proj[..., n_qkv + GDN_HV:n_qkv + GDN_HV + GDN_HEADS].astype(jnp.float32)
    a_raw = proj[..., n_qkv + GDN_HV + GDN_HEADS:].astype(jnp.float32)
    q = l2norm(qkv[..., :GDN_HK].reshape(b, length, GDN_HEADS, GDN_DK).astype(jnp.float32))
    k = l2norm(qkv[..., GDN_HK:2 * GDN_HK].reshape(b, length, GDN_HEADS, GDN_DK).astype(jnp.float32))
    v = qkv[..., 2 * GDN_HK:].reshape(b, length, GDN_HEADS, GDN_DV).astype(jnp.float32)
    beta = jax.nn.sigmoid(b_raw)
    g = -jnp.exp(a_log.astype(jnp.float32)) * jax.nn.softplus(a_raw + dt_bias.astype(jnp.float32))
    o = chunk_gated_delta_rule(q * GDN_DK ** -0.5, k, v, g, beta)
    o = rmsnorm(o, o_norm_g) * jax.nn.silu(gate)
    return o.reshape(b, length, GDN_HV).astype(h.dtype) @ w_out

def sq_relu_mlp(h, w1, w2):
    return jnp.square(jax.nn.relu(h @ w1)) @ w2

def _num_layers_of(m):
    return len(range(m, DEPTH, N_MIXERS))

def first_inputs(seed: int = 0) -> dict:
    key = jax.random.key(seed)
    keys = jax.random.split(key, 64)
    counter = [0]

    def nxt():
        kk = keys[counter[0]]
        counter[0] += 1
        return kk

    def nrm(shape, fan_in):
        return jax.random.normal(nxt(), shape, jnp.float32) * fan_in ** -0.5

    def gain(shape):
        return 1.0 + 0.02 * jax.random.normal(nxt(), shape, jnp.float32)

    def bias(shape):
        return 0.02 * jax.random.normal(nxt(), shape, jnp.float32)

    na, nb, nc, nd = (_num_layers_of(m) for m in range(N_MIXERS))
    x = jax.random.normal(nxt(), (BATCH, SEQ, D_MODEL), jnp.float32)
    dt = jnp.exp(jax.random.uniform(nxt(), (nd, GDN_HEADS), jnp.float32, math.log(1e-3), math.log(1e-1)))
    return {
        'x': x,
        'norm_mix_g': gain((DEPTH, D_MODEL)),
        'norm_mlp_g': gain((DEPTH, D_MODEL)),
        'final_g': gain((D_MODEL,)),
        'mlp_w1': nrm((DEPTH, D_MODEL, D_FF), D_MODEL),
        'mlp_w2': nrm((DEPTH, D_FF, D_MODEL), D_FF),
        'dsa_w_in': nrm((na, D_MODEL, DSA_IN), D_MODEL),
        'dsa_idx_k_g': gain((na, IDX_DIM)),
        'dsa_idx_k_b': bias((na, IDX_DIM)),
        'dsa_w_out': nrm((na, D_MODEL, D_MODEL), D_MODEL),
        'conv_w_pw1': nrm((nb, D_MODEL, 2 * D_MODEL), D_MODEL),
        'conv_b_pw1': bias((nb, 2 * D_MODEL)),
        'conv_w_dw': nrm((nb, CONV_WIDTH, D_MODEL), CONV_WIDTH),
        'conv_b_dw': bias((nb, D_MODEL)),
        'conv_ln_g': gain((nb, D_MODEL)),
        'conv_ln_b': bias((nb, D_MODEL)),
        'conv_w_pw2': nrm((nb, D_MODEL, D_MODEL), D_MODEL),
        'conv_b_pw2': bias((nb, D_MODEL)),
        'mla_w_in': nrm((nc, D_MODEL, MLA_IN), D_MODEL),
        'mla_q_norm_g': gain((nc, MLA_Q_LORA)),
        'mla_w_uq': nrm((nc, MLA_Q_LORA, MLA_HEADS * (MLA_NOPE + MLA_ROPE)), MLA_Q_LORA),
        'mla_kv_norm_g': gain((nc, MLA_KV_LORA)),
        'mla_w_ukv': nrm((nc, MLA_KV_LORA, MLA_HEADS * (MLA_NOPE + MLA_V)), MLA_KV_LORA),
        'mla_w_out': nrm((nc, MLA_HEADS * MLA_V, D_MODEL), MLA_HEADS * MLA_V),
        'gdn_w_in': nrm((nd, D_MODEL, GDN_IN), D_MODEL),
        'gdn_conv_w': nrm((nd, GDN_CONV, 2 * GDN_HK + GDN_HV), GDN_CONV),
        'gdn_a_log': jnp.log(jax.random.uniform(nxt(), (nd, GDN_HEADS), jnp.float32, 1.0, 16.0)),
        'gdn_dt_bias': dt + jnp.log(-jnp.expm1(-dt)),
        'gdn_o_norm_g': gain((nd, GDN_DV)),
        'gdn_w_out': nrm((nd, GDN_HV, D_MODEL), GDN_HV),
    }

def first_block(x, norm_mix_g, norm_mlp_g, final_g, mlp_w1, mlp_w2,
              dsa_w_in, dsa_idx_k_g, dsa_idx_k_b, dsa_w_out,
              conv_w_pw1, conv_b_pw1, conv_w_dw, conv_b_dw, conv_ln_g, conv_ln_b, conv_w_pw2, conv_b_pw2,
              mla_w_in, mla_q_norm_g, mla_w_uq, mla_kv_norm_g, mla_w_ukv, mla_w_out,
              gdn_w_in, gdn_conv_w, gdn_a_log, gdn_dt_bias, gdn_o_norm_g, gdn_w_out):
    h = x
    for i in range(DEPTH):
        m = i % N_MIXERS
        j = i // N_MIXERS
        hn = rmsnorm(h, norm_mix_g[i])
        if m == 0:
            y = dsa_mixer(hn, dsa_w_in[j], dsa_idx_k_g[j], dsa_idx_k_b[j], dsa_w_out[j])
        elif m == 1:
            y = conv_mixer(hn, conv_w_pw1[j], conv_b_pw1[j], conv_w_dw[j], conv_b_dw[j],
                           conv_ln_g[j], conv_ln_b[j], conv_w_pw2[j], conv_b_pw2[j])
        elif m == 2:
            y = mla_mixer(hn, mla_w_in[j], mla_q_norm_g[j], mla_w_uq[j], mla_kv_norm_g[j],
                          mla_w_ukv[j], mla_w_out[j])
        else:
            y = gdn_mixer(hn, gdn_w_in[j], gdn_conv_w[j], gdn_a_log[j], gdn_dt_bias[j],
                          gdn_o_norm_g[j], gdn_w_out[j])
        h = h + y
        h = h + sq_relu_mlp(rmsnorm(h, norm_mlp_g[i]), mlp_w1[i], mlp_w2[i])
    return rmsnorm(h, final_g)


_first_inputs = first_inputs


def first_inputs(seed=0):
    import zlib

    import numpy as np

    out = dict(_first_inputs(seed))
    spreads = {}
    factors = {'final_g': 2.844,
     'dsa_idx_k_g': 3.565,
     'dsa_idx_k_b': 3.8,
     'conv_b_pw1': 7.099,
     'conv_b_dw': 3.928,
     'conv_ln_g': 6.54,
     'conv_ln_b': 7.662,
     'conv_b_pw2': 4.534}
    for name, (base, spread) in spreads.items():
        noise = np.random.default_rng([zlib.crc32(name.encode()), seed]).standard_normal(out[name].shape)
        drawn = base * np.exp(spread * noise) if base else spread * noise
        out[name] = __import__('jax').numpy.asarray(drawn.astype(out[name].dtype))
    for name, factor in factors.items():
        out[name] = (out[name] * factor).astype(out[name].dtype)
    return out


_narrow_inputs = first_inputs


def first_inputs(seed=0):

    out = dict(_narrow_inputs(seed))
    wider = {'norm_mlp_g': 3.32,
     'final_g': 3.25,
     'dsa_idx_k_g': 4.04,
     'dsa_idx_k_b': 4.22,
     'conv_ln_g': 3.44,
     'conv_b_pw2': 3.4}
    for name, times in wider.items():
        mean = out[name].mean()
        out[name] = (mean + times * (out[name] - mean)).astype(out[name].dtype)
    return out


N_EVEN = (DEPTH + 1) // 2
N_ODD = DEPTH // 2
NORM_EPS = 1e-6

RG_WIDTH = D_MODEL
RG_HEADS = 8
RG_HEAD_DIM = RG_WIDTH // RG_HEADS
RG_CONV = 4
RG_C = 8.0
RG_CONV_LEFT = 2
SC_WIDTH = D_MODEL
SC_CONV = 3
SC_CONV_LEFT = 1
EVEN_IN = 2 * RG_WIDTH + 4 * SC_WIDTH
EVEN_MIX = RG_WIDTH + SC_WIDTH
GLA_HEADS = 4
GLA_KEY = D_MODEL // 2
GLA_VAL = D_MODEL
GLA_DK = GLA_KEY // GLA_HEADS
GLA_DV = GLA_VAL // GLA_HEADS
GLA_RANK = 16
GLA_NORMALIZER = 16.0
GLA_CHUNK = 64
ODD_IN = 2 * GLA_KEY + 2 * GLA_VAL + 2 * GLA_RANK


def rmsnorm_2(x, g):
    xf = x.astype(jnp.float32)
    y = xf * lax.rsqrt(jnp.mean(xf * xf, axis=-1, keepdims=True) + NORM_EPS)
    return (y * g.astype(jnp.float32)).astype(x.dtype)

def centred_dwconv(u, w, left):
    seq = u.shape[1]
    width = w.shape[0]
    up = jnp.pad(u, ((0, 0), (left, width - 1 - left), (0, 0)))
    out = up[:, 0:seq] * w[0]
    for k in range(1, width):
        out = out + up[:, k:k + seq] * w[k]
    return out

def rg_lru(u, gate_w, gate_b, lam, reverse):
    bsz, seq, width = u.shape
    uf = u.astype(jnp.float32)
    uh = uf.reshape(bsz, seq, RG_HEADS, RG_HEAD_DIM)
    gates = jax.nn.sigmoid(
        jnp.einsum('bshi,ghij->gbshj', uh, gate_w.astype(jnp.float32))
        + gate_b[:, None, None].astype(jnp.float32))
    r = gates[0].reshape(bsz, seq, width)
    i = gates[1].reshape(bsz, seq, width)
    log_a = -RG_C * r * jax.nn.softplus(-lam.astype(jnp.float32))
    a = jnp.exp(log_a)
    b = jnp.sqrt(-jnp.expm1(2.0 * log_a)) * (i * uf)

    def combine(left, right):
        a_l, b_l = left
        a_r, b_r = right
        return (a_l * a_r, a_r * b_l + b_r)

    _, h = lax.associative_scan(combine, (a, b), reverse=reverse, axis=1)
    return h

def gla_chunked(q, k, v, g):
    bsz, nh, seq, dk = q.shape
    dv = v.shape[-1]
    nc = seq // GLA_CHUNK
    qc = q.astype(jnp.float32).reshape(bsz, nh, nc, GLA_CHUNK, dk) * (dk ** -0.5)
    kc = k.astype(jnp.float32).reshape(bsz, nh, nc, GLA_CHUNK, dk)
    vc = v.astype(jnp.float32).reshape(bsz, nh, nc, GLA_CHUNK, dv)
    gc = g.reshape(bsz, nh, nc, GLA_CHUNK, dk)
    bcum = jnp.cumsum(gc, axis=3)
    btot = bcum[..., -1:, :]
    q_in = qc * jnp.exp(bcum)
    k_in = kc * jnp.exp(-bcum)
    k_st = kc * jnp.exp(btot - bcum)
    mask = jnp.tril(jnp.ones((GLA_CHUNK, GLA_CHUNK), dtype=bool))
    scores = jnp.einsum('bhnid,bhnjd->bhnij', q_in, k_in)
    scores = jnp.where(mask, scores, 0.0)
    o_intra = jnp.einsum('bhnij,bhnje->bhnie', scores, vc)
    decay = jnp.exp(btot[..., 0, :])

    def step(state, xs):
        q_n, k_n, v_n, dec_n = xs
        o_n = jnp.einsum('bhcd,bhde->bhce', q_n, state)
        state = dec_n[..., None] * state + jnp.einsum('bhcd,bhce->bhde', k_n, v_n)
        return state, o_n

    xs = (jnp.moveaxis(q_in, 2, 0), jnp.moveaxis(k_st, 2, 0),
          jnp.moveaxis(vc, 2, 0), jnp.moveaxis(decay, 2, 0))
    state0 = jnp.zeros((bsz, nh, dk, dv), jnp.float32)
    _, o_inter = lax.scan(step, state0, xs)
    o_inter = jnp.moveaxis(o_inter, 0, 2)
    return (o_intra + o_inter).reshape(bsz, nh, seq, dv)

def even_layer(x, norm_pre, norm_post, w_in, conv_w, conv_b, gate_w, gate_b, lam, sc_w, w_out):
    h = rmsnorm_2(x, norm_pre)
    proj = h @ w_in
    xa, za, xb, gb, gc, zb = jnp.split(
        proj, [RG_WIDTH, 2 * RG_WIDTH, 2 * RG_WIDTH + SC_WIDTH,
               2 * RG_WIDTH + 2 * SC_WIDTH, 2 * RG_WIDTH + 3 * SC_WIDTH], axis=-1)
    ua = centred_dwconv(xa, conv_w, RG_CONV_LEFT) + conv_b
    ya = rg_lru(ua, gate_w[0], gate_b[0], lam[0], False) + rg_lru(ua, gate_w[1], gate_b[1], lam[1], True)
    ya = ya * jax.nn.silu(za.astype(jnp.float32))
    yb = gb * centred_dwconv(gc * xb, sc_w, SC_CONV_LEFT)
    yb = yb * jax.nn.silu(zb)
    y = jnp.concatenate([ya, yb.astype(jnp.float32)], axis=-1) @ w_out
    return (x + rmsnorm_2(y, norm_post)).astype(x.dtype)

def odd_layer(x, norm_pre, norm_post, w_in, w_gate_lr, b_gate, head_norm_g, w_out):
    bsz, seq, _ = x.shape
    h = rmsnorm_2(x, norm_pre)
    proj = h @ w_in
    q, k, v, r, lr = jnp.split(
        proj, [GLA_KEY, 2 * GLA_KEY, 2 * GLA_KEY + GLA_VAL, 2 * GLA_KEY + 2 * GLA_VAL], axis=-1)
    lr = lr.reshape(bsz, seq, 2, GLA_RANK).astype(jnp.float32)
    z = jnp.einsum('bsdr,drk->dbsk', lr, w_gate_lr.astype(jnp.float32)) + b_gate[:, None, None].astype(jnp.float32)
    log_alpha = jax.nn.log_sigmoid(z) / GLA_NORMALIZER

    def heads(t, dh):
        return jnp.transpose(t.reshape(bsz, seq, GLA_HEADS, dh), (0, 2, 1, 3))

    qh, kh, vh = heads(q, GLA_DK), heads(k, GLA_DK), heads(v, GLA_DV)
    g_f, g_b = heads(log_alpha[0], GLA_DK), heads(log_alpha[1], GLA_DK)
    o_f = gla_chunked(qh, kh, vh, g_f)
    o_b = jnp.flip(gla_chunked(jnp.flip(qh, 2), jnp.flip(kh, 2), jnp.flip(vh, 2), jnp.flip(g_b, 2)), 2)
    o = rmsnorm_2(o_f + o_b, head_norm_g)
    o = jnp.transpose(o, (0, 2, 1, 3)).reshape(bsz, seq, GLA_VAL)
    y = (o * jax.nn.silu(r.astype(jnp.float32))) @ w_out
    return (x + rmsnorm_2(y, norm_post)).astype(x.dtype)

def second_inputs(seed: int = 0) -> dict:
    key = jax.random.key(seed)
    ks = jax.random.split(key, 20)
    nrm = jax.random.normal
    f32 = jnp.float32
    lam_a = jax.random.uniform(ks[8], (N_EVEN, 2, RG_WIDTH), f32, minval=0.9, maxval=0.999)
    lam_s = lam_a ** (1.0 / RG_C)
    rg_lambda = jnp.log(lam_s) - jnp.log1p(-lam_s)
    return {
        'x': nrm(ks[0], (BATCH, SEQ, D_MODEL), f32),
        'even_norm_pre': 1.0 + 0.05 * nrm(ks[1], (N_EVEN, D_MODEL), f32),
        'even_norm_post': 1.0 + 0.05 * nrm(ks[2], (N_EVEN, D_MODEL), f32),
        'even_w_in': nrm(ks[3], (N_EVEN, D_MODEL, EVEN_IN), f32) * D_MODEL ** -0.5,
        'rg_conv_w': nrm(ks[4], (N_EVEN, RG_CONV, RG_WIDTH), f32) * RG_CONV ** -0.5,
        'rg_conv_b': 0.01 * nrm(ks[5], (N_EVEN, RG_WIDTH), f32),
        'rg_gate_w': nrm(ks[6], (N_EVEN, 2, 2, RG_HEADS, RG_HEAD_DIM, RG_HEAD_DIM), f32) * RG_HEAD_DIM ** -0.5,
        'rg_gate_b': 0.01 * nrm(ks[7], (N_EVEN, 2, 2, RG_HEADS, RG_HEAD_DIM), f32),
        'rg_lambda': rg_lambda,
        'sc_conv_w': nrm(ks[9], (N_EVEN, SC_CONV, SC_WIDTH), f32) * SC_CONV ** -0.5,
        'even_w_out': nrm(ks[10], (N_EVEN, EVEN_MIX, D_MODEL), f32) * EVEN_MIX ** -0.5,
        'odd_norm_pre': 1.0 + 0.05 * nrm(ks[11], (N_ODD, D_MODEL), f32),
        'odd_norm_post': 1.0 + 0.05 * nrm(ks[12], (N_ODD, D_MODEL), f32),
        'odd_w_in': nrm(ks[13], (N_ODD, D_MODEL, ODD_IN), f32) * D_MODEL ** -0.5,
        'gla_w_gate_lr': nrm(ks[14], (N_ODD, 2, GLA_RANK, GLA_KEY), f32) * GLA_RANK ** -0.5,
        'gla_b_gate': 1.0 + 0.3 * nrm(ks[15], (N_ODD, 2, GLA_KEY), f32),
        'gla_norm_g': 1.0 + 0.05 * nrm(ks[16], (N_ODD, GLA_DV), f32),
        'odd_w_out': nrm(ks[17], (N_ODD, GLA_VAL, D_MODEL), f32) * GLA_VAL ** -0.5,
    }

def second_block(x, even_norm_pre, even_norm_post, even_w_in, rg_conv_w, rg_conv_b, rg_gate_w,
              rg_gate_b, rg_lambda, sc_conv_w, even_w_out, odd_norm_pre, odd_norm_post,
              odd_w_in, gla_w_gate_lr, gla_b_gate, gla_norm_g, odd_w_out):
    for layer in range(DEPTH):
        j = layer // 2
        if layer % 2 == 0:
            x = even_layer(x, even_norm_pre[j], even_norm_post[j], even_w_in[j], rg_conv_w[j],
                           rg_conv_b[j], rg_gate_w[j], rg_gate_b[j], rg_lambda[j],
                           sc_conv_w[j], even_w_out[j])
        else:
            x = odd_layer(x, odd_norm_pre[j], odd_norm_post[j], odd_w_in[j], gla_w_gate_lr[j],
                          gla_b_gate[j], gla_norm_g[j], odd_w_out[j])
    return x


def setup_inputs(seed=0):
    out = dict(first_inputs(seed))
    for name, value in second_inputs(seed + 1).items():
        if name != "x":
            out[name + "_2"] = value
    return out


def reference(
    x, norm_mix_g, norm_mlp_g, final_g, mlp_w1, mlp_w2, dsa_w_in, dsa_idx_k_g, dsa_idx_k_b,
    dsa_w_out, conv_w_pw1, conv_b_pw1, conv_w_dw, conv_b_dw, conv_ln_g, conv_ln_b, conv_w_pw2,
    conv_b_pw2, mla_w_in, mla_q_norm_g, mla_w_uq, mla_kv_norm_g, mla_w_ukv, mla_w_out, gdn_w_in,
    gdn_conv_w, gdn_a_log, gdn_dt_bias, gdn_o_norm_g, gdn_w_out, even_norm_pre_2,
    even_norm_post_2, even_w_in_2, rg_conv_w_2, rg_conv_b_2, rg_gate_w_2, rg_gate_b_2,
    rg_lambda_2, sc_conv_w_2, even_w_out_2, odd_norm_pre_2, odd_norm_post_2, odd_w_in_2,
    gla_w_gate_lr_2, gla_b_gate_2, gla_norm_g_2, odd_w_out_2,
):
    x = first_block(
        x, norm_mix_g, norm_mlp_g, final_g, mlp_w1, mlp_w2, dsa_w_in, dsa_idx_k_g, dsa_idx_k_b,
        dsa_w_out, conv_w_pw1, conv_b_pw1, conv_w_dw, conv_b_dw, conv_ln_g, conv_ln_b,
        conv_w_pw2, conv_b_pw2, mla_w_in, mla_q_norm_g, mla_w_uq, mla_kv_norm_g, mla_w_ukv,
        mla_w_out, gdn_w_in, gdn_conv_w, gdn_a_log, gdn_dt_bias, gdn_o_norm_g, gdn_w_out,
    )
    return second_block(
        x, even_norm_pre_2, even_norm_post_2, even_w_in_2, rg_conv_w_2, rg_conv_b_2,
        rg_gate_w_2, rg_gate_b_2, rg_lambda_2, sc_conv_w_2, even_w_out_2, odd_norm_pre_2,
        odd_norm_post_2, odd_w_in_2, gla_w_gate_lr_2, gla_b_gate_2, gla_norm_g_2, odd_w_out_2,
    )


_drawn_inputs = setup_inputs


def setup_inputs(seed=0):
    import zlib

    import numpy as np

    out = dict(_drawn_inputs(seed))
    spreads = {}
    factors = {'even_norm_post_2': 2.693,
     'rg_conv_b_2': 8.0,
     'rg_gate_b_2': 8.0,
     'odd_norm_post_2': 3.616,
     'gla_norm_g_2': 3.165}
    for name, (base, spread) in spreads.items():
        noise = np.random.default_rng([zlib.crc32(name.encode()), seed]).standard_normal(out[name].shape)
        drawn = base * np.exp(spread * noise) if base else spread * noise
        out[name] = __import__('jax').numpy.asarray(drawn.astype(out[name].dtype))
    for name, factor in factors.items():
        out[name] = (out[name] * factor).astype(out[name].dtype)
    return out
```

```python
from contextlib import ExitStack

import numpy as np

import concourse.bass as bass
from concourse import mybir

F32 = mybir.dt.float32
F32R = mybir.dt.float32r
ALU = mybir.AluOpType
ACT = mybir.ActivationFunctionType
AX = mybir.AxisListType

P = 128
S = 512
T = S // P
D = 1024
KD = D // P
FF = 4 * D
EPS = 1e-6
BIG = 1e30
CAUSAL_FILL = -3.0e38
TAKEN = -3.4e38
HEADS = 8
IDX_DIM = 64
TOPK = min(256, S // 4)
CONV_W = 31
RG_W = 4
SC_W = 3
RG_C = 8.0
GLA_HEADS = 4
GLA_DK = 128
GLA_DV = 256
GLA_RANK = 16
CHUNK = 64
NCH = S // CHUNK
GLA_NORM = 16.0

VEC_SIZES = [
    ("mix_g0", KD), ("mlp_g0", KD), ("mix_g1", KD), ("mlp_g1", KD), ("pw1_b", 2 * KD),
    ("dw_w", KD * CONV_W), ("dw_b", KD), ("ln_g", KD), ("ln_b", KD), ("idx_g", 1), ("idx_b", 1),
    ("even_g", KD), ("rg_w", KD * RG_W), ("rg_b", KD), ("gate_b", 4 * KD), ("lam", 2 * KD),
    ("sc_w", KD * SC_W), ("odd_g", KD), ("gla_b", 2 * GLA_HEADS),
]
VEC = {}
_at = 0
for _name, _n in VEC_SIZES:
    VEC[_name] = (_at, _n)
    _at += _n
NVEC = _at

CON_SIZES = [("ident", P), ("mean", P), ("fwd_mask", P), ("bwd_mask", P), ("causal", P),
             ("fwd_keep", S), ("bwd_keep", S)]
CON = {}
_at = 0
for _name, _n in CON_SIZES:
    CON[_name] = (_at, _n)
    _at += _n
NCON = _at

RAW = 4
RING = 4
SLOT = 1024
AHEAD = 3


class Lane:

    def __init__(self, name, sem):
        self.name, self.sem, self.count = name, sem, 0
        self.queue, self.waited = [], {}

    def wait(self, *marks):
        for m in marks:
            if m is None:
                continue
            sem, value = m
            if self.waited.get(id(sem), 0) < value:
                self.waited[id(sem)] = value
                self.queue.append(lambda e, sem=sem, value=value: e.wait_ge(sem, value))

    def do(self, make, after=(), signal=True):
        self.wait(*after)
        if not signal:
            self.queue.append(make)
            return None
        self.count += 1
        self.queue.append(lambda e: make(e).then_inc(self.sem, 1))
        return (self.sem, self.count)

    def last(self):
        return (self.sem, self.count) if self.count else None

    def play(self, engine):
        for step in self.queue:
            step(engine)


class Landing:

    def __init__(self, sem):
        self.sem, self.count = sem, 0

    def start(self, lane, out, in_, after=()):
        lane.wait(*after)
        self.count += 16
        sem = self.sem
        lane.queue.append(lambda e: e.dma_start(out, in_).then_inc(sem, 16))
        return (self.sem, self.count)


def build(nc, a, out):
    ctx = ExitStack()
    with ctx:
        def sem(name):
            return ctx.enter_context(nc.semaphore(name))

        def sb(name, shape, dt=F32, scope=ctx):
            return scope.enter_context(nc.sbuf_tensor(name, shape, dt))

        pe, act = Lane("pe", sem("pe_done")), Lane("act", sem("act_done"))
        dve, pool = Lane("dve", sem("dve_done")), Lane("pool", sem("pool_done"))
        sp = Lane("sp", None)

        H = sb("residual", [P, T, D])
        XH = sb("x_hi", [P, KD, S], F32R)
        XL = sb("x_lo", [P, KD, S], F32R)
        raw = [sb(f"w_raw{i}", [P, SLOT]) for i in range(RAW)]
        WH = [sb(f"w_hi{i}", [P, SLOT], F32R) for i in range(RING)]
        WL = [sb(f"w_lo{i}", [P, SLOT], F32R) for i in range(RING)]
        vec = sb("vectors", [P, NVEC])
        con = sb("constants", [P, NCON])
        row = [sb(f"row{i}", [P, D]) for i in range(2)]
        stat = sb("stat", [P, 8, 16])
        epsc = sb("eps_col", [P, 1])
        bank = [ctx.enter_context(nc.psum_tensor(f"bank{i}", [P, 512], F32)) for i in range(8)]
        bank_free = [[] for _ in range(8)]

        def V(name, i=0, n=1):
            at = VEC[name][0] + i
            return vec[:, at:at + n]

        def C(name):
            at, n = CON[name]
            return con[:, at:at + n]

        ident, mean_ones = C("ident"), C("mean")

        load_vec = Landing(sem("vec_landed"))
        load_x = Landing(sem("x_landed"))
        load_row = [Landing(sem(f"row_landed{i}")) for i in range(2)]
        load_raw = [Landing(sem(f"raw_landed{i}")) for i in range(RAW)]

        vec_in = load_vec.start(sp, vec[:, :], a["vectors"])
        load_con = Landing(sem("con_landed"))
        con_in = load_con.start(sp, con[:, :], a["constants"])
        x_in = load_x.start(sp, H[:, :, :], a["x"].rearrange("b (t p) d -> p (b t) d", p=P))
        consts = [vec_in, con_in]
        eps_set = dve.do(lambda e: e.memset(epsc[:, :], EPS))

        def load_row_into(i, name, n, after):
            return load_row[i].start(sp, row[i][:, 0:n], a[name].partition_broadcast(P), after)

        def units_of(name, src, col0, ncols, krows, per=None):
            per = per or SLOT // ncols
            src = src.rearrange("(k p) n -> p k n", p=P)
            return [(name, src[:, k:k + per, col0:col0 + ncols], per, ncols)
                    for k in range(krows[0], krows[1], per)]

        dsa_in, dsa_out = a["dsa_w_in"][0], a["dsa_w_out"][0]
        stream = []
        stream += units_of("idx_narrow", dsa_in, 3 * D + HEADS * IDX_DIM, IDX_DIM + HEADS, (0, KD), KD)
        for name, c in (("qi", 3 * D), ("q0", 0), ("q1", 512), ("k0", D), ("k1", D + 512),
                        ("v0", 2 * D), ("v1", 2 * D + 512)):
            stream += units_of(name, dsa_in, c, 512, (0, KD))
        for n in range(2):
            stream += units_of(f"dsa_out{n}", dsa_out, n * 512, 512, (0, KD))

        def mlp_units(layer):
            got = []
            for half in range(2):
                for g in range(4):
                    got += units_of(f"up{layer}{half}{g}", a["mlp_w1"][layer],
                                    half * (FF // 2) + g * 512, 512, (0, KD))
                for n in range(2):
                    got += units_of(f"down{layer}{half}{n}", a["mlp_w2"][layer], n * 512, 512,
                                    (half * 16, half * 16 + 16))
            return got

        stream += mlp_units(0)
        for g in range(2):
            stream += units_of(f"pw1a{g}", a["conv_w_pw1"][0], g * 512, 512, (0, KD))
            stream += units_of(f"pw1b{g}", a["conv_w_pw1"][0], D + g * 512, 512, (0, KD))
        for n in range(2):
            stream += units_of(f"pw2{n}", a["conv_w_pw2"][0], n * 512, 512, (0, KD))
        stream += mlp_units(1)
        even_in, even_out = a["even_w_in_2"][0], a["even_w_out_2"][0]
        EVEN_ORDER = [("xa0", 0), ("gc0", 4 * D), ("xb0", 2 * D), ("gb0", 3 * D), ("zb0", 5 * D),
                      ("xa1", 512), ("gc1", 4 * D + 512), ("xb1", 2 * D + 512), ("gb1", 3 * D + 512),
                      ("zb1", 5 * D + 512), ("za0", D), ("za1", D + 512)]
        for name, c in EVEN_ORDER:
            stream += units_of(name, even_in, c, 512, (0, KD))
        for n in range(2):
            stream += units_of(f"eout{n}", even_out, n * 512, 512, (KD, 2 * KD))
        for n in range(2):
            stream += units_of(f"eouta{n}", even_out, n * 512, 512, (0, KD))
        odd_in, odd_out = a["odd_w_in_2"][0], a["odd_w_out_2"][0]
        stream += units_of("lr", odd_in, 3 * D, 2 * GLA_RANK, (0, KD), KD)
        for name, c in (("gq", 0), ("gk", 512), ("gv0", D), ("gv1", D + 512), ("gr0", 2 * D),
                        ("gr1", 2 * D + 512)):
            stream += units_of(name, odd_in, c, 512, (0, KD))
        for n in range(2):
            stream += units_of(f"oout{n}", odd_out, n * 512, 512, (0, KD))

        state = {"loaded": 0, "split": 0, "used": 0}
        raw_free = [[] for _ in range(RAW)]
        ring_free = [[] for _ in range(RING)]
        split_of = []

        def queue_loads(upto):
            while state["loaded"] < min(upto, len(stream)):
                u = state["loaded"]
                _, src, per, cols = stream[u]
                i = u % RAW
                dst = raw[i][:, 0:per * cols].rearrange("p (k n) -> p k n", k=per)
                stream[u] += (load_raw[i].start(sp, dst, src, raw_free[i]),)
                state["loaded"] += 1

        def queue_splits(upto):
            while state["split"] < min(upto, len(stream)):
                u = state["split"]
                queue_loads(u + 1)
                n = stream[u][2] * stream[u][3]
                landed = stream[u][4]
                r, i = raw[u % RAW], u % RING
                hi = act.do(lambda e, i=i, r=r, n=n: e.activation(WH[i][:, 0:n], r[:, 0:n], ACT.Copy),
                            [landed] + ring_free[i])
                lo = pool.do(lambda e, i=i, r=r, n=n: e.tensor_tensor(
                    WL[i][:, 0:n], r[:, 0:n], WH[i][:, 0:n].bitcast(F32), ALU.subtract),
                    [landed, hi] + ring_free[i])
                raw_free[u % RAW] = [hi, lo]
                split_of.append([hi, lo])
                state["split"] += 1
                queue_loads(u + 1 + RAW)

        def product(name, k0, banks, xh, xl, x_ready, feature_major, first, last, background=None):
            k = k0
            mark = None
            while state["used"] < len(stream) and stream[state["used"]][0] == name:
                u = state["used"]
                queue_splits(u + AHEAD)
                if background:
                    background()
                _, _, per, cols = stream[u][:4]
                i = u % RING
                pe.wait(*split_of[u])
                wh = WH[i][:, 0:per * cols].rearrange("p (k n) -> p k n", k=per)
                wl = WL[i][:, 0:per * cols].rearrange("p (k n) -> p k n", k=per)
                ends = u + 1 == len(stream) or stream[u + 1][0] != name
                for kk in range(per):
                    pe.wait(*x_ready[k])
                    for j, b in enumerate(banks):
                        begin = first and k == k0
                        if begin:
                            pe.wait(*bank_free[b])
                        end = last and ends and kk == per - 1
                        if feature_major:
                            m = min(P, cols - j * P)
                            wj, wlj = wh[:, kk, j * P:j * P + m], wl[:, kk, j * P:j * P + m]
                            o = bank[b][0:m, :]
                            trio = ((wj, xh[:, k, :]), (wj, xl[:, k, :]), (wlj, xh[:, k, :]))
                        else:
                            xt, xlt = xh[:, k, j * P:(j + 1) * P], xl[:, k, j * P:(j + 1) * P]
                            o = bank[b][:, 0:cols]
                            trio = ((xt, wh[:, kk, :]), (xt, wl[:, kk, :]), (xlt, wh[:, kk, :]))
                        for n, (l, r) in enumerate(trio):
                            done = kk == per - 1 and j == len(banks) - 1 and n == 2
                            mark = pe.do(lambda e, o=o, l=l, r=r, s=(begin and n == 0), t=(end and n == 2):
                                         e.matmul(o, l, r, start=s, stop=t), signal=done) or mark
                    k += 1
                ring_free[i] = [mark]
                state["used"] += 1
            assert mark is not None, name
            return mark

        side = [0]

        def four():
            side[0] ^= 1
            return [0, 1, 2, 3] if side[0] else [4, 5, 6, 7]

        def fence():
            marks = [lane.last() for lane in (pe, act, dve, pool)]
            for lane in (act, dve, pool, sp):
                lane.wait(*marks)

        stat_row = [0]

        def token_rstd(parts, width, after):
            root = act.do(lambda e: e.activation(parts, parts, ACT.Sqrt, bias=epsc[:, 0:1], scale=1.0 / width),
                          list(after) + [eps_set])
            return dve.do(lambda e: e.reciprocal(parts, parts), [root])

        def residual_rstd(scratch, ready):
            sums = []
            for t in range(T):
                o = stat[:, 0, t:t + 1]
                if t % 2 == 0:
                    sums.append(act.do(lambda e, t=t, o=o: e.activation(
                        scratch[:, 0, :], H[:, t, :], ACT.Square, accum_out=o), list(ready) + sums[-2:]))
                else:
                    sums.append(dve.do(lambda e, t=t, o=o: e.tensor_tensor_reduce(
                        out=scratch[:, 1, :], in0=H[:, t, :], in1=H[:, t, :], scale=1.0, scalar=0.0,
                        op0=ALU.mult, op1=ALU.add, accum_out=o), list(ready) + sums[-2:]))
            return token_rstd(stat[:, 0, 0:T], D, sums)

        def split_bank(b, src, hi, lo, scale, after):
            h = act.do(lambda e: e.activation(hi, src, ACT.Copy, scale=scale), after)
            l = dve.do(lambda e: e.scalar_tensor_tensor(
                out=lo, in0=src, scalar=scale, in1=hi.bitcast(F32), op0=ALU.mult, op1=ALU.subtract), [h])
            bank_free[b] = [h, l]
            return [h, l]

        def split_sbuf(src, hi, lo, after):
            h = act.do(lambda e: e.activation(hi, src, ACT.Copy), after)
            l = dve.do(lambda e: e.tensor_tensor(lo, src, hi.bitcast(F32), ALU.subtract), [h])
            return [h, l]

        def transpose_split(src, ready, gain, x_free):
            done = []
            for t in range(T):
                for k in range(KD):
                    if t == 0:
                        pe.wait(*bank_free[k])
                    m = pe.do(lambda e, t=t, k=k: e.transpose(
                        bank[k][:, t * P:(t + 1) * P], src[:, t, k * P:(k + 1) * P], ident),
                        list(ready[t]) + consts, signal=(t == T - 1))
                    if t == T - 1:
                        done.append(m)
            marks = []
            for k in range(KD):
                after = [done[k]] + consts + list(x_free)
                if gain is None:
                    h = act.do(lambda e, k=k: e.activation(XH[:, k, :], bank[k][:, :], ACT.Copy), after)
                    l = dve.do(lambda e, k=k: e.tensor_tensor(
                        XL[:, k, :], bank[k][:, :], XH[:, k, :].bitcast(F32), ALU.subtract), [h])
                    bank_free[k] = [h, l]
                    marks.append([h, l])
                else:
                    marks.append(split_bank(k, bank[k][:, :], XH[:, k, :], XL[:, k, :], gain(k), after))
            return marks

        def norm_to_x(scope, gain_name, ready, tag):
            xn = sb(f"normed_{tag}", [P, T, D], scope=scope)
            rstd = residual_rstd(xn, ready)
            scaled = []
            for t in range(T):
                scaled.append([dve.do(lambda e, t=t: e.tensor_scalar(
                    xn[:, t, :], H[:, t, :], stat[:, 0, t:t + 1], None, ALU.mult), [rstd])])
            free = [pe.last()]
            return transpose_split(xn, scaled, lambda k: V(gain_name, k), free)

        def add_to_residual(banks, n, mark, res):
            for t, b in enumerate(banks):
                m = dve.do(lambda e, t=t, b=b: e.tensor_tensor(
                    H[:, t, n * 512:(n + 1) * 512], bank[b][:, :], H[:, t, n * 512:(n + 1) * 512], ALU.add),
                    [mark])
                bank_free[b] = [m]
                res.append(m)

        def dsa_stage(ready):
            scope = ExitStack()
            with scope:
                ns = ExitStack()
                with ns:
                    x_ready = norm_to_x(ns, "mix_g0", ready, "dsa")
                fence()
                vT = sb("v_tok", [P, T, D], scope=scope)
                qT = sb("q_feat", [P, HEADS, S], scope=scope)
                kT = sb("k_feat", [P, HEADS, S], scope=scope)
                qiT = sb("qi_feat", [P, HEADS // 2, S], scope=scope)
                ki = sb("ki_tok", [P, T, P], scope=scope)
                kiT = sb("ki_feat", [P, S], scope=scope)
                wi = sb("wi_tok", [P, T, HEADS], scope=scope)
                bn = sb("ki_stats", [P, T, 6], scope=scope)
                mv = sb("ki_meanvar", [P, T, 2], scope=scope)
                score = sb("score", [P, T, S], scope=scope)
                relu = [sb(f"relu{i}", [P, S], scope=scope) for i in range(2)]
                top8 = sb("top8", [P, T, 8], scope=scope)
                bias = sb("mask_bias", [P, T, S], scope=scope)

                banks = four()
                m = product("idx_narrow", 0, banks, XH, XL, x_ready, False, True, True)
                norm_marks = []
                for t, b in enumerate(banks):
                    kraw = bank[b][:, 0:IDX_DIM]
                    w = act.do(lambda e, t=t, b=b: e.activation(
                        wi[:, t, :], bank[b][:, IDX_DIM:IDX_DIM + HEADS], ACT.Copy,
                        scale=HEADS ** -0.5 * IDX_DIM ** -0.5), [m])
                    s1 = dve.do(lambda e, t=t, kraw=kraw: e.bn_stats(bn[:, t, :], kraw), [w])
                    s2 = dve.do(lambda e, t=t: e.bn_aggr(mv[:, t, :], bn[:, t, :]), [s1])
                    root = act.do(lambda e, t=t: e.activation(
                        stat[:, 1, t:t + 1], mv[:, t, 1:2], ACT.Sqrt, bias=epsc[:, 0:1]), [s2, eps_set])
                    rs = dve.do(lambda e, t=t: e.reciprocal(stat[:, 1, t:t + 1], stat[:, 1, t:t + 1]), [root])
                    for c in range(2):
                        kn = dve.do(lambda e, t=t, c=c, kraw=kraw: e.tensor_scalar(
                            ki[:, t, c * IDX_DIM:(c + 1) * IDX_DIM], kraw, mv[:, t, 0:1],
                            stat[:, 1, t:t + 1], ALU.subtract, ALU.mult), [rs])
                    bank_free[b] = [w, kn]
                    norm_marks.append(kn)
                b = banks[0]
                for t in range(T):
                    m = pe.do(lambda e, t=t, b=b: e.transpose(bank[b][:, t * P:(t + 1) * P], ki[:, t, :], ident),
                              [norm_marks[t]] + bank_free[b] + consts)
                ki_ready = dve.do(lambda e, b=b: e.tensor_scalar(
                    kiT[:, :], bank[b][:, :], V("idx_g"), V("idx_b"), ALU.mult, ALU.add), [m])
                bank_free[b] = [ki_ready]

                def evac_feature(name, dst, t0, kind="act"):
                    banks = four()
                    m = product(name, 0, banks, XH, XL, x_ready, True, True, True, background.step)
                    marks = []
                    for j, b in enumerate(banks):
                        o = dst[:, t0 + j, :]
                        d = act.do(lambda e, o=o, b=b: e.activation(o, bank[b][:, :], ACT.Copy), [m])
                        bank_free[b] = [d]
                        marks.append(d)
                    return marks

                class Background:
                    queue = []

                    def step(self, n=4):
                        for _ in range(n):
                            if self.queue:
                                self.queue.pop(0)()

                background = Background()
                qi_ready = evac_feature("qi", qiT, 0)

                assert TOPK == P
                score_ready = [None] * T
                uses = 0
                relu_free = [[], []]
                for t in range(1, T):
                    n = (t + 1) * P
                    acc = None
                    for h in range(HEADS):
                        b = (uses % 4) + (0 if side[0] == 0 else 4)
                        p0 = IDX_DIM * (h % 2)
                        m = pe.do(lambda e, b=b, h=h, t=t, n=n, p0=p0: e.matmul(
                            bank[b][:, 0:n], qiT[p0:p0 + IDX_DIM, h // 2, t * P:(t + 1) * P],
                            kiT[p0:p0 + IDX_DIM, 0:n], start=True, stop=True),
                            [qi_ready[h // 2], ki_ready] + bank_free[b])
                        i = uses % 2
                        r = act.do(lambda e, b=b, i=i, n=n: e.activation(relu[i][:, 0:n], bank[b][:, 0:n], ACT.Relu),
                                   [m] + relu_free[i])
                        bank_free[b] = [r]
                        w = wi[:, t, h:h + 1]
                        if h == 0:
                            acc = dve.do(lambda e, i=i, n=n, t=t, w=w: e.tensor_scalar(
                                score[:, t, 0:n], relu[i][:, 0:n], w, None, ALU.mult), [r])
                        else:
                            acc = dve.do(lambda e, i=i, n=n, t=t, w=w: e.scalar_tensor_tensor(
                                out=score[:, t, 0:n], in0=relu[i][:, 0:n], scalar=w, in1=score[:, t, 0:n],
                                op0=ALU.mult, op1=ALU.add), [r, acc])
                        relu_free[i] = [acc]
                        uses += 1
                    c = score[:, t, t * P:n]
                    score_ready[t] = pool.do(lambda e, c=c: e.affine_select(
                        out=c, in_=c, compare_op=ALU.is_ge, fill=CAUSAL_FILL, base=0,
                        pattern=[[-1, P]], channel_multiplier=1), [acc])

                bias_ready = [None] * T
                bias_ready[0] = dve.do(lambda e: e.tensor_copy(bias[:, 0, 0:P], C("causal")), consts)

                def top_round(t, r):
                    n = (t + 1) * P
                    after = [score_ready[t]]
                    m8 = dve.do(lambda e: e.max(top8[:, t, :], score[:, t, 0:n]), after)
                    score_ready[t] = dve.do(lambda e: e.match_replace(
                        out=score[:, t, 0:n], in_to_replace=top8[:, t, :], in_values=score[:, t, 0:n],
                        imm_value=TAKEN), [m8])
                    if r == TOPK // 8 - 1:
                        bias_ready[t] = dve.do(lambda e: e.tensor_scalar(
                            bias[:, t, 0:n], score[:, t, 0:n], TAKEN, -BIG, ALU.not_equal, ALU.mult),
                            [score_ready[t]])

                for r in range(TOPK // 8):
                    for t in range(1, T):
                        background.queue.append(lambda t=t, r=r: top_round(t, r))

                q_ready = evac_feature("q0", qT, 0) + evac_feature("q1", qT, 4)
                k_ready = evac_feature("k0", kT, 0) + evac_feature("k1", kT, 4)
                v_ready = []
                for n in range(2):
                    banks = four()
                    m = product(f"v{n}", 0, banks, XH, XL, x_ready, False, True, True, background.step)
                    for t, b in enumerate(banks):
                        d = act.do(lambda e, t=t, n=n, b=b: e.activation(
                            vT[:, t, n * 512:(n + 1) * 512], bank[b][:, :], ACT.Copy), [m])
                        bank_free[b] = [d]
                        v_ready.append(d)
                background.step(1000)
                x_free = [pe.last()]

                logit = [sb(f"logit{i}", [P, (i + 1) * P], scope=scope) for i in range(T)]
                prob = [score]
                probT = [sb(f"probT{i}", [P, T, S], scope=scope) for i in range(1)]
                place = [(5, 0), (5, P), (6, 0), (7, 0)]
                scale = P ** -0.5
                logits_mark, prob_marks = {}, {}
                o_ready = []
                prob_free, probT_free = [], []
                logit_free = [[] for _ in range(4)]

                def logits(h):
                    for t in range(T):
                        b, c = place[t]
                        n = (t + 1) * P
                        logits_mark[h, t] = pe.do(lambda e, b=b, c=c, n=n, t=t: e.matmul(
                            bank[b][:, c:c + n], qT[:, h, t * P:(t + 1) * P], kT[:, h, 0:n],
                            start=True, stop=True), [q_ready[h], k_ready[h]] + bank_free[b])

                def softmax(h):
                    read = {5: [], 6: [], 7: []}
                    for t in range(T):
                        b, c = place[t]
                        n = (t + 1) * P
                        mx, sm = stat[:, 2, t:t + 1], stat[:, 3, t:t + 1]
                        lg = logit[t]
                        m1 = dve.do(lambda e, b=b, c=c, n=n, t=t, mx=mx, lg=lg: e.tensor_tensor_reduce(
                            out=lg[:, 0:n], in0=bank[b][:, c:c + n], in1=bias[:, t, 0:n], scale=1.0,
                            scalar=-3e38, op0=ALU.add, op1=ALU.max, accum_out=mx),
                            [logits_mark[h, 1 if t == 0 else t], bias_ready[t]] + logit_free[t])
                        m2 = dve.do(lambda e, mx=mx: e.tensor_scalar(mx, mx, -scale, None, ALU.mult), [m1])
                        ex = act.do(lambda e, n=n, t=t, mx=mx, sm=sm, lg=lg: e.activation(
                            prob[0][:, t, 0:n], lg[:, 0:n], ACT.Exp, bias=mx, scale=scale, accum_out=sm),
                            [m2] + prob_free)
                        logit_free[t] = [ex]
                        rc = dve.do(lambda e, sm=sm: e.reciprocal(sm, sm), [ex])
                        prob_marks[h, t] = dve.do(lambda e, n=n, t=t, sm=sm: e.tensor_scalar(
                            prob[0][:, t, 0:n], prob[0][:, t, 0:n], sm, None, ALU.mult), [rc])
                        read[b].append(m1)
                    for b in read:
                        bank_free[b] = read[b]

                def values(h):
                    nonlocal prob_free, probT_free
                    turned = [None] * T
                    for t in range(T):
                        for s in range(t + 1):
                            turned[s] = pe.do(lambda e, t=t, s=s: e.transpose(
                                bank[s][:, t * P:(t + 1) * P], prob[0][:, t, s * P:(s + 1) * P], ident),
                                [prob_marks[h, t]] + bank_free[s], signal=True)
                    prob_free = [turned[T - 1]]
                    copied = []
                    for s in range(T):
                        src, dst = bank[s][:, s * P:S], probT[0][:, s, s * P:S]
                        if s % 2 == 0:
                            c = act.do(lambda e, src=src, dst=dst: e.activation(dst, src, ACT.Copy),
                                       [turned[s]] + probT_free)
                        else:
                            c = dve.do(lambda e, src=src, dst=dst: e.tensor_copy(dst, src),
                                       [turned[s]] + probT_free)
                        bank_free[s] = [c]
                        copied.append(c)
                    for t in range(T):
                        for s in range(t + 1):
                            m = pe.do(lambda e, s=s, t=t: e.matmul(
                                bank[4][:, t * P:(t + 1) * P], vT[:, s, h * P:(h + 1) * P],
                                probT[0][:, s, t * P:(t + 1) * P], start=(s == 0), stop=(s == t)),
                                [copied[s]] + v_ready + bank_free[4])
                    probT_free = [m]
                    hi = act.do(lambda e: e.activation(XH[:, h, :], bank[4][:, :], ACT.Copy), [m] + x_free)
                    lo = dve.do(lambda e: e.tensor_tensor(
                        XL[:, h, :], bank[4][:, :], XH[:, h, :].bitcast(F32), ALU.subtract), [hi])
                    bank_free[4] = [hi, lo]
                    o_ready.append([hi, lo])

                logits(0)
                softmax(0)
                for h in range(HEADS):
                    if h + 1 < HEADS:
                        logits(h + 1)
                    values(h)
                    if h + 1 < HEADS:
                        softmax(h + 1)

                res = []
                side[0] = 0
                for n in range(2):
                    banks = four()
                    m = product(f"dsa_out{n}", 0, banks, XH, XL, o_ready, False, True, True)
                    add_to_residual(banks, n, m, res)
            fence()
            return res

        def mlp_stage(layer, ready):
            scope = ExitStack()
            with scope:
                ns = ExitStack()
                with ns:
                    x_ready = norm_to_x(ns, f"mlp_g{layer}", ready, f"mlp{layer}")
                fence()
                FH = sb(f"f_hi{layer}", [P, 16, S], F32R, scope=scope)
                FL = sb(f"f_lo{layer}", [P, 16, S], F32R, scope=scope)
                relu = [sb(f"f_relu{layer}_{i}", [P, S], scope=scope) for i in range(4)]
                square = [sb(f"f_square{layer}_{i}", [P, S], scope=scope) for i in range(4)]
                relu_free, square_free = [[] for _ in range(4)], [[] for _ in range(4)]
                f_free = []
                res = []
                for half in range(2):
                    f_ready = []
                    for g in range(4):
                        banks = four()
                        m = product(f"up{layer}{half}{g}", 0, banks, XH, XL, x_ready, True, True, True)
                        for j, b in enumerate(banks):
                            r = act.do(lambda e, j=j, b=b: e.activation(relu[j][:, :], bank[b][:, :], ACT.Relu),
                                       [m] + relu_free[j])
                            bank_free[b] = [r]
                            s = dve.do(lambda e, j=j: e.tensor_tensor(square[j][:, :], relu[j][:, :], relu[j][:, :],
                                                                      ALU.mult), [r] + square_free[j])
                            relu_free[j] = [s]
                            k = g * 4 + j
                            f = split_sbuf(square[j][:, :], FH[:, k, :], FL[:, k, :], [s] + f_free)
                            square_free[j] = f
                            f_ready.append(f)
                    for n in range(2):
                        banks = four()
                        m = product(f"down{layer}{half}{n}", 0, banks, FH, FL, f_ready, False, True, True)
                        add_to_residual(banks, n, m, res)
                    f_free = [m]
            fence()
            return res

        def conv_stage(ready):
            scope = ExitStack()
            with scope:
                b2 = load_row_into(0, "b_pw2", D, [])
                ns = ExitStack()
                with ns:
                    x_ready = norm_to_x(ns, "mix_g1", ready, "conv")
                fence()
                PAD = CONV_W - 1
                u = sb("conv_u", [P, KD, PAD + S], scope=scope)
                c = sb("conv_c", [P, KD, S], scope=scope)
                gate = sb("conv_gate", [P, 4, S], scope=scope)
                lin = sb("conv_lin", [P, 4, S], scope=scope)
                sq = [sb(f"conv_sq{i}", [P, S], scope=scope) for i in range(2)]
                rstd = sb("conv_rstd", [P, S], scope=scope)
                padded = dve.do(lambda e: e.memset(u[:, :, 0:PAD], 0.0))
                conv_done = [None] * KD
                lin_free = []
                for g in range(2):
                    banks = four()
                    m = product(f"pw1a{g}", 0, banks, XH, XL, x_ready, True, True, True)
                    lins = []
                    for j, b in enumerate(banks):
                        k = g * 4 + j
                        d = dve.do(lambda e, b=b, j=j, k=k: e.tensor_scalar(
                            lin[:, j, :], bank[b][:, :], V("pw1_b", k), None, ALU.add), [m] + lin_free)
                        bank_free[b] = [d]
                        lins.append(d)
                    banks = four()
                    m = product(f"pw1b{g}", 0, banks, XH, XL, x_ready, True, True, True)
                    us = []
                    for j, b in enumerate(banks):
                        k = g * 4 + j
                        s = act.do(lambda e, b=b, j=j, k=k: e.activation(
                            gate[:, j, :], bank[b][:, :], ACT.Sigmoid, bias=V("pw1_b", KD + k)), [m] + lin_free)
                        bank_free[b] = [s]
                        us.append(dve.do(lambda e, j=j, k=k: e.tensor_tensor(
                            u[:, k, PAD:PAD + S], lin[:, j, :], gate[:, j, :], ALU.mult), [s, lins[j]]))
                    lin_free = us
                    for i in range(CONV_W):
                        for j in range(4):
                            k = g * 4 + j
                            w = V("dw_w", k * CONV_W + i)
                            src, dst = u[:, k, i:i + S], c[:, k, :]
                            if i == 0:
                                conv_done[k] = dve.do(lambda e, src=src, dst=dst, w=w, k=k: e.tensor_scalar(
                                    dst, src, w, V("dw_b", k), ALU.mult, ALU.add), [us[j], padded])
                            else:
                                conv_done[k] = dve.do(lambda e, src=src, dst=dst, w=w: e.scalar_tensor_tensor(
                                    out=dst, in0=src, scalar=w, in1=dst, op0=ALU.mult, op1=ALU.add),
                                    [conv_done[k]])
                x_free = [pe.last()]
                bm, bv = four()[:2]
                for k in range(KD):
                    m = pe.do(lambda e, k=k: e.matmul(bank[bm][:, :], mean_ones, c[:, k, :], start=(k == 0),
                                                      stop=(k == KD - 1)), [conv_done[k]] + bank_free[bm])
                cent = []
                for k in range(KD):
                    cent.append(dve.do(lambda e, k=k: e.tensor_tensor(
                        c[:, k, :], c[:, k, :], bank[bm][:, :], ALU.subtract), [m]))
                bank_free[bm] = [cent[-1]]
                sq_free = [[], []]
                for k in range(KD):
                    i = k % 2
                    s = act.do(lambda e, k=k, i=i: e.activation(sq[i][:, :], c[:, k, :], ACT.Square),
                               [cent[k]] + sq_free[i])
                    m = pe.do(lambda e, k=k, i=i: e.matmul(bank[bv][:, :], mean_ones, sq[i][:, :], start=(k == 0),
                                                           stop=(k == KD - 1)), [s] + bank_free[bv])
                    sq_free[i] = [m]
                root = act.do(lambda e: e.activation(rstd[:, :], bank[bv][:, :], ACT.Sqrt, bias=epsc[:, 0:1]), [m])
                bank_free[bv] = [root]
                rs = dve.do(lambda e: e.reciprocal(rstd[:, :], rstd[:, :]), [root])
                y_ready = []
                for k in range(KD):
                    n = dve.do(lambda e, k=k: e.tensor_tensor(c[:, k, :], c[:, k, :], rstd[:, :], ALU.mult), [rs])
                    s = act.do(lambda e, k=k: e.activation(c[:, k, :], c[:, k, :], ACT.Silu,
                                                           bias=V("ln_b", k), scale=V("ln_g", k)), [n])
                    y_ready.append(split_sbuf(c[:, k, :], XH[:, k, :], XL[:, k, :], [s] + x_free))
                res = []
                for n in range(2):
                    banks = four()
                    m = product(f"pw2{n}", 0, banks, XH, XL, y_ready, False, True, True)
                    for t, b in enumerate(banks):
                        hh = H[:, t, n * 512:(n + 1) * 512]
                        d = dve.do(lambda e, b=b, hh=hh: e.tensor_tensor(hh, bank[b][:, :], hh, ALU.add), [m])
                        bank_free[b] = [d]
                        res.append(dve.do(lambda e, hh=hh, n=n: e.tensor_tensor(
                            hh, hh, row[0][:, n * 512:(n + 1) * 512], ALU.add), [d, b2]))
            fence()
            return res

        def final_norm(ready):
            g = load_row_into(1, "final_g", D, [])
            scope = ExitStack()
            with scope:
                scratch = sb("final_scratch", [P, 2, D], scope=scope)
                rstd = residual_rstd(scratch, ready)
                res = [dve.do(lambda e, t=t: e.scalar_tensor_tensor(
                    out=H[:, t, :], in0=H[:, t, :], scalar=stat[:, 0, t:t + 1], in1=row[1][:, :],
                    op0=ALU.mult, op1=ALU.mult), [rstd, g]) for t in range(T)]
            fence()
            return res

        def add_normed(scope, banks_of, marks, gain_row, gain_in, tag, sink=None):
            sums, junk = [], sb(f"post_junk_{tag}", [P, 2, 512], scope=scope)
            tmp = [sb(f"post_tmp_{tag}{i}", [P, 512], scope=scope) for i in range(4)]
            for n in range(2):
                for t in range(T):
                    b = banks_of[n][t]
                    sums.append(act.do(lambda e, n=n, t=t, b=b: e.activation(
                        junk[:, n, :], bank[b][:, :], ACT.Square, accum_out=stat[:, 4 + n, t:t + 1]),
                        [marks[n]] + sums[-1:]))
            both = dve.do(lambda e: e.tensor_tensor(stat[:, 4, 0:T], stat[:, 4, 0:T], stat[:, 5, 0:T], ALU.add), sums)
            rstd = token_rstd(stat[:, 4, 0:T], D, [both])
            res, tmp_free = [], [[] for _ in range(4)]
            for t in range(T):
                for n in range(2):
                    b, i = banks_of[n][t], (2 * t + n) % 4
                    hh = H[:, t, n * 512:(n + 1) * 512]
                    m = dve.do(lambda e, b=b, t=t, n=n, i=i: e.scalar_tensor_tensor(
                        out=tmp[i][:, :], in0=bank[b][:, :], scalar=stat[:, 4, t:t + 1],
                        in1=gain_row[:, n * 512:(n + 1) * 512], op0=ALU.mult, op1=ALU.mult),
                        [rstd, gain_in] + tmp_free[i])
                    bank_free[b] = [m]
                    s = dve.do(lambda e, i=i, hh=hh: e.tensor_tensor(hh, hh, tmp[i][:, :], ALU.add), [m])
                    tmp_free[i] = [s]
                    res.append(s)
                if sink:
                    sink(t, res[-2:])
            return res

        def even_stage(ready):
            scope = ExitStack()
            with scope:
                post_in = load_row_into(0, "even_post", D, [])
                ns = ExitStack()
                with ns:
                    x_ready = norm_to_x(ns, "even_g", ready, "even")
                fence()
                YBH = sb("yb_hi", [P, KD, S], F32R, scope=scope)
                YBL = sb("yb_lo", [P, KD, S], F32R, scope=scope)
                work = ExitStack()
                with work:
                    ua = sb("rg_u", [P, 4, S], scope=work)
                    ya = sb("rg_y", [P, KD, S], scope=work)
                    R = sb("rg_r", [P, 4, S], scope=work)
                    I = sb("rg_i", [P, 4, S], scope=work)
                    Q = sb("rg_t", [P, 4, S], scope=work)
                    xpad = sb("conv_in", [P, 4, S + 3], scope=work)
                    sc = sb("sc_acc", [P, 4, S], scope=work)
                    gw = [sb(f"gate_w{i}", [P, 8, P], scope=work) for i in range(1)]
                    coef = sb("rg_coef", [P, 2 * KD], scope=work)
                    sp1 = sb("sp_z", [P, 2 * KD], scope=work)
                    sp2 = sb("sp_w", [P, 2 * KD], scope=work)
                    sp3 = sb("sp_s", [P, 2 * KD], scope=work)
                    load_gw = Landing(sem("gate_w_landed"))

                    lam = V("lam", 0, 2 * KD)
                    m = act.do(lambda e: e.activation(sp1[:, :], lam, ACT.Abs), consts)
                    m = act.do(lambda e: e.activation(sp1[:, :], sp1[:, :], ACT.Exp, scale=-1.0), [m])
                    m = dve.do(lambda e: e.tensor_scalar(sp2[:, :], sp1[:, :], 2.0, None, ALU.add), [m])
                    m = dve.do(lambda e: e.reciprocal(sp2[:, :], sp2[:, :]), [m])
                    m = dve.do(lambda e: e.tensor_tensor(sp1[:, :], sp1[:, :], sp2[:, :], ALU.mult), [m])
                    m = dve.do(lambda e: e.tensor_tensor(sp2[:, :], sp1[:, :], sp1[:, :], ALU.mult), [m])
                    m = dve.do(lambda e: e.memset(sp3[:, :], 1.0 / 19), [m])
                    for d in range(17, 0, -2):
                        m = dve.do(lambda e: e.tensor_tensor(sp3[:, :], sp3[:, :], sp2[:, :], ALU.mult), [m])
                        m = dve.do(lambda e, d=d: e.tensor_scalar(sp3[:, :], sp3[:, :], 1.0 / d, None, ALU.add), [m])
                    m = dve.do(lambda e: e.scalar_tensor_tensor(
                        out=sp3[:, :], in0=sp3[:, :], scalar=2.0, in1=sp1[:, :], op0=ALU.mult, op1=ALU.mult), [m])
                    m = dve.do(lambda e: e.tensor_scalar(sp2[:, :], lam, -1.0, 0.0, ALU.mult, ALU.max), [m])
                    m = dve.do(lambda e: e.tensor_tensor(sp3[:, :], sp3[:, :], sp2[:, :], ALU.add), [m])
                    coef_ready = dve.do(lambda e: e.tensor_scalar(coef[:, :], sp3[:, :], -RG_C, None, ALU.mult), [m])

                    ua_ready = [None] * KD
                    pad_free, ua_free = [], []

                    def bank_copy(banks, m, dst, width0, after, engine=None):
                        marks = []
                        for j, b in enumerate(banks):
                            d = act.do(lambda e, j=j, b=b: e.activation(
                                dst[:, j, width0:width0 + S], bank[b][:, :], ACT.Copy), [m] + after)
                            bank_free[b] = [d]
                            marks.append(d)
                        return marks

                    def long_conv(g):
                        nonlocal pad_free, ua_free
                        edges = [dve.do(lambda e: e.memset(xpad[:, :, 0:2], 0.0), pad_free)]
                        edges.append(dve.do(lambda e: e.memset(xpad[:, :, S + 2:S + 3], 0.0), pad_free))
                        banks = four()
                        m = product(f"xa{g}", 0, banks, XH, XL, x_ready, True, True, True)
                        xs = bank_copy(banks, m, xpad, 2, pad_free)
                        pad_free = []
                        for j in range(4):
                            k = g * 4 + j
                            d = dve.do(lambda e, j=j, k=k: e.tensor_scalar(
                                ua[:, j, :], xpad[:, j, 0:S], V("rg_w", k * RG_W), V("rg_b", k), ALU.mult, ALU.add),
                                [xs[j]] + edges + ua_free)
                            for i in range(1, RG_W):
                                d = dve.do(lambda e, j=j, k=k, i=i: e.scalar_tensor_tensor(
                                    out=ua[:, j, :], in0=xpad[:, j, i:i + S], scalar=V("rg_w", k * RG_W + i),
                                    in1=ua[:, j, :], op0=ALU.mult, op1=ALU.add), [d])
                            ua_ready[k] = d
                            pad_free.append(d)

                    ya_ready = [None] * KD
                    rg_free = []
                    gw_free = []

                    def lru(direction, g):
                        nonlocal rg_free, gw_free, ua_free
                        for which in range(2):
                            landed = load_gw.start(sp, gw[0][:, 4 * which:4 * which + 4, :],
                                                   a["rg_gate_w_2"][0, direction, which, 4 * g:4 * g + 4]
                                                   .rearrange("h i j -> i h j"), gw_free)
                        gates = []
                        for which, dst in ((0, R), (1, I)):
                            banks = four()
                            for j, b in enumerate(banks):
                                k = 4 * g + j
                                m = pe.do(lambda e, b=b, j=j, k=k, which=which: e.matmul(
                                    bank[b][:, :], gw[0][:, 4 * which + j, :], ua[:, j, :], start=True, stop=True),
                                    [landed, ua_ready[k]] + bank_free[b])
                                s = act.do(lambda e, b=b, j=j, k=k, which=which, dst=dst: e.activation(
                                    dst[:, j, :], bank[b][:, :], ACT.Sigmoid,
                                    bias=V("gate_b", (2 * direction + which) * KD + k)), [m] + rg_free)
                                bank_free[b] = [s]
                                gates.append(s)
                        gw_free = [m]
                        th, ex, iu = [], [], []
                        for j in range(4):
                            k = 4 * g + j
                            cf = coef[:, direction * KD + k:direction * KD + k + 1]
                            th.append(act.do(lambda e, j=j, cf=cf: e.activation(Q[:, j, :], R[:, j, :], ACT.Tanh, scale=cf),
                                             [gates[j], coef_ready] + rg_free))
                        for j in range(4):
                            k = 4 * g + j
                            cf = coef[:, direction * KD + k:direction * KD + k + 1]
                            ex.append(act.do(lambda e, j=j, cf=cf: e.activation(R[:, j, :], R[:, j, :], ACT.Exp, scale=cf),
                                             [th[j]]))
                            iu.append(dve.do(lambda e, j=j, k=k: e.tensor_tensor(
                                I[:, j, :], I[:, j, :], ua[:, j, :], ALU.mult), [gates[4 + j]]))
                        ua_free = [m] + iu
                        rt = []
                        for j in range(4):
                            d = dve.do(lambda e, j=j: e.tensor_tensor(
                                sqr[j % 2][:, :], R[:, j, :], R[:, j, :], ALU.mult), [ex[j]] + sqr_free[j % 2])
                            d = dve.do(lambda e, j=j: e.scalar_tensor_tensor(
                                out=Q[:, j, :], in0=sqr[j % 2][:, :], scalar=1.0, in1=Q[:, j, :], op0=ALU.add,
                                op1=ALU.mult), [d])
                            sqr_free[j % 2] = [d]
                            rt.append(act.do(lambda e, j=j: e.activation(Q[:, j, :], Q[:, j, :], ACT.Sqrt, scale=-1.0), [d]))
                        rg_free = []
                        for j in range(4):
                            k = 4 * g + j
                            d = dve.do(lambda e, j=j: e.tensor_tensor(I[:, j, :], I[:, j, :], Q[:, j, :], ALU.mult),
                                       [rt[j], iu[j]])
                            if direction == 0:
                                d = dve.do(lambda e, j=j, k=k: e.tensor_tensor_scan(
                                    ya[:, k, :], R[:, j, :], I[:, j, :], 0.0, ALU.mult, ALU.add), [d])
                                ya_ready[k] = d
                            else:
                                s = dve.do(lambda e, j=j: e.tensor_tensor_scan(
                                    Q[:, j, ::-1], R[:, j, ::-1], I[:, j, ::-1], 0.0, ALU.mult, ALU.add), [d])
                                d = dve.do(lambda e, j=j, k=k: e.tensor_tensor(
                                    ya[:, k, :], ya[:, k, :], Q[:, j, :], ALU.add), [s, ya_ready[k]])
                                ya_ready[k] = d
                            rg_free.append(d)

                    sqr = [sb(f"rg_sq{i}", [P, S], scope=work) for i in range(2)]
                    sqr_free = [[], []]
                    yb_ready = [None] * KD
                    sc_free = []

                    def short_conv(g):
                        nonlocal pad_free, sc_free
                        edges = [dve.do(lambda e: e.memset(xpad[:, :, 0:1], 0.0), pad_free)]
                        edges.append(dve.do(lambda e: e.memset(xpad[:, :, S + 1:S + 2], 0.0), pad_free))
                        banks = four()
                        m = product(f"gc{g}", 0, banks, XH, XL, x_ready, True, True, True)
                        cs = bank_copy(banks, m, xpad, 1, pad_free)
                        banks = four()
                        m = product(f"xb{g}", 0, banks, XH, XL, x_ready, True, True, True)
                        acc = []
                        pad_free = []
                        for j, b in enumerate(banks):
                            k = 4 * g + j
                            d = dve.do(lambda e, j=j, b=b: e.tensor_tensor(
                                xpad[:, j, 1:1 + S], bank[b][:, :], xpad[:, j, 1:1 + S], ALU.mult), [m, cs[j]])
                            bank_free[b] = [d]
                            d = dve.do(lambda e, j=j, k=k: e.tensor_scalar(
                                sc[:, j, :], xpad[:, j, 0:S], V("sc_w", k * SC_W), None, ALU.mult), [d] + edges + sc_free)
                            for i in range(1, SC_W):
                                d = dve.do(lambda e, j=j, k=k, i=i: e.scalar_tensor_tensor(
                                    out=sc[:, j, :], in0=xpad[:, j, i:i + S], scalar=V("sc_w", k * SC_W + i),
                                    in1=sc[:, j, :], op0=ALU.mult, op1=ALU.add), [d])
                            pad_free.append(d)
                            acc.append(d)
                        banks = four()
                        m = product(f"gb{g}", 0, banks, XH, XL, x_ready, True, True, True)
                        for j, b in enumerate(banks):
                            acc[j] = dve.do(lambda e, j=j, b=b: e.tensor_tensor(
                                sc[:, j, :], bank[b][:, :], sc[:, j, :], ALU.mult), [m, acc[j]])
                            bank_free[b] = [acc[j]]
                        banks = four()
                        m = product(f"zb{g}", 0, banks, XH, XL, x_ready, True, True, True)
                        sc_free = []
                        for j, b in enumerate(banks):
                            k = 4 * g + j
                            s = act.do(lambda e, j=j, b=b: e.activation(silu[j % 2][:, :], bank[b][:, :], ACT.Silu),
                                       [m] + silu_free[j % 2])
                            bank_free[b] = [s]
                            d = dve.do(lambda e, j=j: e.tensor_tensor(sc[:, j, :], sc[:, j, :], silu[j % 2][:, :], ALU.mult),
                                       [s, acc[j]])
                            silu_free[j % 2] = [d]
                            yb_ready[k] = split_sbuf(sc[:, j, :], YBH[:, k, :], YBL[:, k, :], [d])
                            sc_free += yb_ready[k]

                    silu = [sb(f"even_silu{i}", [P, S], scope=work) for i in range(2)]
                    silu_free = [[], []]
                    for g in range(2):
                        long_conv(g)
                        lru(0, g)
                        lru(1, g)
                        short_conv(g)

                    za_marks = []
                    for g in range(2):
                        banks = four()
                        m = product(f"za{g}", 0, banks, XH, XL, x_ready, True, True, True)
                        for j, b in enumerate(banks):
                            k = 4 * g + j
                            s = act.do(lambda e, j=j, b=b: e.activation(silu[j % 2][:, :], bank[b][:, :], ACT.Silu),
                                       [m] + silu_free[j % 2])
                            bank_free[b] = [s]
                            d = dve.do(lambda e, j=j, k=k: e.tensor_tensor(
                                ya[:, k, :], ya[:, k, :], silu[j % 2][:, :], ALU.mult), [s, ya_ready[k]])
                            za_marks.append(d)
                            silu_free[j % 2] = [d]
                    x_free = [pe.last()]
                    yax = [split_sbuf(ya[:, k, :], XH[:, k, :], XL[:, k, :], [za_marks[k]] + x_free)
                           for k in range(KD)]
                both = [four(), four()]
                for n in range(2):
                    product(f"eout{n}", 0, both[n], YBH, YBL, yb_ready, False, True, False)
                marks = [product(f"eouta{n}", 0, both[n], XH, XL, yax, False, False, True) for n in range(2)]
                fence()
                post = ExitStack()
                with post:
                    res = add_normed(post, both, marks, row[0], post_in, "even")
            fence()
            return res

        def odd_stage(ready):
            scope = ExitStack()
            with scope:
                post_in = load_row_into(0, "odd_post", D, [dve.last()])
                head_in = load_row_into(1, "gla_norm_g", GLA_DV, [dve.last()])
                ns = ExitStack()
                with ns:
                    x_ready = norm_to_x(ns, "odd_g", ready, "odd")
                fence()
                qT = sb("gla_q", [P, GLA_HEADS, S], scope=scope)
                kT = sb("gla_k", [P, GLA_HEADS, S], scope=scope)
                v = sb("gla_v", [P, T, D], scope=scope)
                r = sb("gla_r", [P, T, D], scope=scope)
                main = ExitStack()
                with main:
                    G = sb("gla_g", [P, 2, GLA_HEADS, S], scope=main)
                    gates = ExitStack()
                    lrT = sb("gla_lr", [2 * GLA_RANK, S], scope=gates)
                    wg = sb("gla_wg", [2 * GLA_RANK, 2, 512], scope=gates)
                    tmp = [sb(f"gla_tmp{i}", [P, S], scope=gates) for i in range(2)]
                    load_wg = Landing(sem("wg_landed"))
                    zeroed = dve.do(lambda e: e.memset(wg[:, :, :], 0.0))
                    for d in range(2):
                        wg_in = load_wg.start(sp, wg[d * GLA_RANK:(d + 1) * GLA_RANK, d, :],
                                              a["gla_w_gate_lr_2"][0, d], [zeroed])
                    sp.wait(wg_in)

                    b = four()[0]
                    m = product("lr", 0, [b], XH, XL, x_ready, True, True, True)
                    lr_ready = act.do(lambda e, b=b: e.activation(lrT[:, :], bank[b][0:2 * GLA_RANK, :], ACT.Copy), [m])
                    bank_free[b] = [lr_ready]
                    act.queue.append(lambda e: e.preload_act_table_set("natural_log_exp_and_others"))
                    g_ready = {}
                    z_done = [[], []]
                    for d in range(2):
                        for h in range(GLA_HEADS):
                            b = four()[0]
                            i = (d * GLA_HEADS + h) % 2
                            z = G[:, d, h, :]
                            m = pe.do(lambda e, b=b, d=d, h=h: e.matmul(
                                bank[b][:, :], wg[:, d, h * P:(h + 1) * P], lrT[:, :], start=True, stop=True),
                                [wg_in, lr_ready] + bank_free[b])
                            m1 = dve.do(lambda e, b=b, d=d, h=h, z=z: e.tensor_scalar(
                                z, bank[b][:, :], V("gla_b", d * GLA_HEADS + h), None, ALU.add), [m])
                            bank_free[b] = [m1]
                            m2 = act.do(lambda e, i=i, z=z: e.activation(tmp[i][:, :], z, ACT.Abs), [m1] + z_done[i])
                            m2 = act.do(lambda e, i=i: e.activation(tmp[i][:, :], tmp[i][:, :], ACT.Exp, scale=-1.0), [m2])
                            m2 = act.do(lambda e, i=i: e.activation(tmp[i][:, :], tmp[i][:, :], ACT.Ln, bias=1.0), [m2])
                            m3 = dve.do(lambda e, i=i, z=z: e.scalar_tensor_tensor(
                                out=z, in0=z, scalar=0.0, in1=tmp[i][:, :], op0=ALU.min, op1=ALU.subtract), [m2])
                            z_done[i] = [m3]
                            g_ready[d, h] = dve.do(lambda e, z=z: e.tensor_scalar(
                                z, z, 1.0 / GLA_NORM, None, ALU.mult), [m3])

                    def feature(name, dst):
                        banks = four()
                        m = product(name, 0, banks, XH, XL, x_ready, True, True, True)
                        marks = []
                        for j, b in enumerate(banks):
                            d = act.do(lambda e, j=j, b=b: e.activation(dst[:, j, :], bank[b][:, :], ACT.Copy), [m])
                            bank_free[b] = [d]
                            marks.append(d)
                        return marks

                    q_ready = feature("gq", qT)
                    k_ready = feature("gk", kT)
                    v_ready, r_ready = [], []
                    for name, dst, func, marks in (("gv", v, ACT.Copy, v_ready), ("gr", r, ACT.Silu, r_ready)):
                        for n in range(2):
                            banks = four()
                            m = product(f"{name}{n}", 0, banks, XH, XL, x_ready, False, True, True)
                            for t, b in enumerate(banks):
                                d = act.do(lambda e, t=t, n=n, b=b, dst=dst, func=func: e.activation(
                                    dst[:, t, n * 512:(n + 1) * 512], bank[b][:, :], func), [m])
                                bank_free[b] = [d]
                                marks.append(d)
                    act.queue.append(lambda e: e.preload_act_table_set("natural_log_exp_and_others"))

                    gates.close()
                    fence()
                    cum = [sb(f"gla_cum{d}", [P, S], scope=main) for d in range(2)]
                    e1 = [sb(f"gla_e1{d}", [P, S], scope=main) for d in range(2)]
                    e2 = [sb(f"gla_e2{d}", [P, S], scope=main) for d in range(2)]
                    e3 = [sb(f"gla_e3{d}", [P, S], scope=main) for d in range(2)]
                    kst = [sb(f"gla_kst{d}", [P, T, P], scope=main) for d in range(2)]
                    stm = [sb(f"gla_stm{d}", [P, T, P], scope=main) for d in range(2)]
                    stt = sb("gla_state", [P, 2, NCH, GLA_DV], scope=main)
                    ssq = sb("gla_ssq", [P, GLA_HEADS, T], scope=main)
                    oj = sb("gla_junk", [P, GLA_DV], scope=main)
                    masks = [C("fwd_mask"), C("bwd_mask")]
                    keeps = [C("fwd_keep"), C("bwd_keep")]
                    dk_scale = GLA_DK ** -0.5
                    prev = {}

                    def chunks(ap):
                        return ap.rearrange("p (c n) -> p c n", n=CHUNK)

                    y_marks = [[] for _ in range(T)]
                    for h in range(GLA_HEADS):
                        ready_q, ready_k, ready_s, dec = {}, {}, {}, {}
                        for d in range(2):
                            free = prev.get(d, [])
                            sl = (lambda x: x) if d == 0 else (lambda x: x[:, ::-1])
                            m = dve.do(lambda e, d=d, h=h, sl=sl: e.tensor_tensor_scan(
                                sl(cum[d][:, :]), sl(keeps[d]), sl(G[:, d, h, :]), 0.0, ALU.mult, ALU.add),
                                [g_ready[d, h]] + free)
                            x1 = act.do(lambda e, d=d: e.activation(e1[d][:, :], cum[d][:, :], ACT.Exp), [m] + free)
                            x2 = act.do(lambda e, d=d: e.activation(e2[d][:, :], cum[d][:, :], ACT.Exp, scale=-1.0), [m] + free)
                            at = CHUNK - 1 if d == 0 else 0
                            df = dve.do(lambda e, d=d, at=at: e.tensor_tensor(
                                chunks(e3[d][:, :]), chunks(cum[d][:, :])[:, :, at:at + 1].broadcast_to([P, NCH, CHUNK]),
                                chunks(cum[d][:, :]), ALU.subtract), [m] + free)
                            x3 = act.do(lambda e, d=d: e.activation(e3[d][:, :], e3[d][:, :], ACT.Exp), [df])
                            dec[d] = dve.do(lambda e, d=d, at=at: e.tensor_copy(
                                stat[:, 6 + d, 0:NCH], chunks(e1[d][:, :])[:, :, at]), [x1] + free)
                            ready_q[d] = dve.do(lambda e, d=d, h=h: e.scalar_tensor_tensor(
                                out=e1[d][:, :], in0=qT[:, h, :], scalar=dk_scale, in1=e1[d][:, :], op0=ALU.mult,
                                op1=ALU.mult), [dec[d], q_ready[h]])
                            ready_k[d] = dve.do(lambda e, d=d, h=h: e.tensor_tensor(
                                e2[d][:, :], kT[:, h, :], e2[d][:, :], ALU.mult), [x2, k_ready[h]])
                            ready_s[d] = dve.do(lambda e, d=d, h=h: e.tensor_tensor(
                                e3[d][:, :], kT[:, h, :], e3[d][:, :], ALU.mult), [x3])
                        last_score = {}
                        kst_ready, stm_ready = {}, {}
                        for d in range(2):
                            for t in range(T):
                                m = pe.do(lambda e, d=d, t=t: e.matmul(
                                    bank[d][:, t * P:(t + 1) * P], e2[d][:, t * P:(t + 1) * P],
                                    e1[d][:, t * P:(t + 1) * P], start=True, stop=True),
                                    [ready_q[d], ready_k[d]] + bank_free[d])
                            stm_ready[d] = dve.do(lambda e, d=d: e.tensor_tensor(
                                stm[d][:, :, :], bank[d][:, :].rearrange("p (t n) -> p t n", n=P),
                                masks[d].unsqueeze(1).broadcast_to([P, T, P]), ALU.mult), [m] + prev.get("stm", []))
                            bank_free[d] = [stm_ready[d]]
                            for t in range(T):
                                m = pe.do(lambda e, d=d, t=t: e.transpose(
                                    bank[2 + d][:, t * P:(t + 1) * P], e3[d][:, t * P:(t + 1) * P], ident),
                                    [ready_s[d]] + bank_free[2 + d])
                            kst_ready[d] = act.do(lambda e, d=d: e.activation(
                                kst[d][:, :, :].rearrange("p t n -> p (t n)"), bank[2 + d][:, :], ACT.Copy),
                                [m] + prev.get("kst", []))
                            bank_free[2 + d] = [kst_ready[d]]
                        st_ready = {}
                        for d in range(2):
                            order = list(range(NCH)) if d == 0 else list(range(NCH - 1, -1, -1))
                            homes = {}
                            for n, c in enumerate(order):
                                b = (0, 1)[n % 2] if (n // 4) % 2 == 0 else (2, 3)[n % 2]
                                homes[c] = (b, (n // 2) % 2 * GLA_DV)
                            for quad in range(2):
                                marks = {}
                                for n in range(4 * quad, 4 * quad + 4):
                                    c = order[n]
                                    b, col = homes[c]
                                    p0 = (c % 2) * CHUNK
                                    marks[c] = pe.do(lambda e, b=b, col=col, c=c, d=d, h=h, p0=p0: e.matmul(
                                        bank[b][:, col:col + GLA_DV], kst[d][p0:p0 + CHUNK, c // 2, :],
                                        v[p0:p0 + CHUNK, c // 2, h * GLA_DV:(h + 1) * GLA_DV], start=True, stop=True),
                                        [kst_ready[d]] + v_ready + bank_free[b])
                                reads = []
                                for n in range(4 * quad, 4 * quad + 4):
                                    c = order[n]
                                    b, col = homes[c]
                                    if n == NCH - 1:
                                        continue
                                    src, dst = bank[b][:, col:col + GLA_DV], stt[:, d, order[n + 1], :]
                                    after = [marks[order[4 * quad + 3]]] + prev.get("stt", [])
                                    if n == 0:
                                        s = dve.do(lambda e, src=src, dst=dst: e.tensor_copy(dst, src), after)
                                    else:
                                        s = dve.do(lambda e, src=src, dst=dst, d=d, c=c: e.scalar_tensor_tensor(
                                            out=dst, in0=stt[:, d, c, :], scalar=stat[:, 6 + d, c:c + 1], in1=src,
                                            op0=ALU.mult, op1=ALU.add), after + [st_ready[d, c], dec[d]])
                                    st_ready[d, order[n + 1]] = s
                                    reads.append(s)
                                for b in ((0, 1), (2, 3))[quad]:
                                    bank_free[b] = list(reads)
                        out_marks = []
                        for t in range(T):
                            b, col = 4 + t % 4, 0
                            o = bank[b][:, 0:GLA_DV]
                            vv = v[:, t, h * GLA_DV:(h + 1) * GLA_DV]
                            pe.do(lambda e, o=o, t=t, vv=vv: e.matmul(o, stm[0][:, t, :], vv, start=True, stop=False),
                                  [stm_ready[0]] + v_ready + bank_free[b])
                            inter = [(d, c) for d in range(2) for c in (2 * t, 2 * t + 1)
                                     if c != (0 if d == 0 else NCH - 1)]
                            for d, c in inter:
                                p0 = (c % 2) * CHUNK
                                pe.do(lambda e, b=b, d=d, c=c, p0=p0: e.matmul(
                                    bank[b][p0:p0 + CHUNK, 0:GLA_DV], e1[d][:, c * CHUNK:(c + 1) * CHUNK],
                                    stt[:, d, c, :], start=False, stop=False), [st_ready[d, c]])
                            m = pe.do(lambda e, o=o, t=t, vv=vv: e.matmul(o, stm[1][:, t, :], vv, start=False, stop=True),
                                      [stm_ready[1]])
                            out_marks.append(m)
                        prev[0] = prev[1] = prev["stm"] = prev["kst"] = prev["stt"] = [m]
                        ss = []
                        for t in range(T):
                            b = 4 + t
                            ss.append(act.do(lambda e, t=t, b=b, h=h: e.activation(
                                oj[:, :], bank[b][:, 0:GLA_DV], ACT.Square, accum_out=ssq[:, h, t:t + 1]),
                                [out_marks[t]] + ss[-1:]))
                        rstd = token_rstd(ssq[:, h, :], GLA_DV, ss)
                        for t in range(T):
                            b = 4 + t
                            rr = r[:, t, h * GLA_DV:(h + 1) * GLA_DV]
                            m = dve.do(lambda e, rr=rr: e.tensor_tensor(rr, rr, row[1][:, 0:GLA_DV], ALU.mult),
                                       [head_in] + r_ready)
                            m = dve.do(lambda e, b=b, t=t, h=h, rr=rr: e.scalar_tensor_tensor(
                                out=rr, in0=bank[b][:, 0:GLA_DV], scalar=ssq[:, h, t:t + 1], in1=rr,
                                op0=ALU.mult, op1=ALU.mult), [m, rstd])
                            bank_free[b] = [m]
                            y_marks[t].append(m)
                x_free = [pe.last()]
                y_ready = transpose_split(r, y_marks, None, x_free)
                both = [four(), four()]
                marks = [product(f"oout{n}", 0, both[n], XH, XL, y_ready, False, True, True) for n in range(2)]
                fence()
                post = ExitStack()
                with post:
                    out_landed = Landing(sem("out_landed"))

                    def sink(t, after):
                        return out_landed.start(sp, out[0, t * P:(t + 1) * P, :], H[:, t, :], after)

                    add_normed(post, both, marks, row[0], post_in, "odd", sink)
                    sp.wait((out_landed.sem, out_landed.count))

        queue_loads(RAW)
        ready = dsa_stage([x_in])
        ready = mlp_stage(0, ready)
        ready = conv_stage(ready)
        ready = mlp_stage(1, ready)
        ready = final_norm(ready)
        ready = even_stage(ready)
        odd_stage(ready)
        assert state["used"] == len(stream)

        block = ctx.enter_context(nc.Block())

        @block.sync
        def _(e):
            sp.play(e)

        @block.scalar
        def _(e):
            act.play(e)

        @block.gpsimd
        def _(e):
            pool.play(e)

        @block.vector
        def _(e):
            dve.play(e)

        @block.tensor
        def _(e):
            pe.play(e)


def constants():
    i = np.arange(P)
    same = (i[:, None] // CHUNK) == (i[None, :] // CHUNK)
    parts = {
        "ident": np.eye(P),
        "mean": np.full((P, P), 1.0 / D),
        "fwd_mask": same & (i[None, :] >= i[:, None]),
        "bwd_mask": same & (i[None, :] <= i[:, None]),
        "causal": np.where(i[None, :] <= i[:, None], 0.0, -BIG),
        "fwd_keep": np.tile((np.arange(S) % CHUNK != 0)[None], (P, 1)),
        "bwd_keep": np.tile((np.arange(S) % CHUNK != CHUNK - 1)[None], (P, 1)),
    }
    return np.concatenate([parts[n].astype(np.float32) for n, _ in CON_SIZES], axis=1)


def columns(x):
    return np.ascontiguousarray(np.asarray(x).reshape(-1, P).T)


def taps(w):
    w = np.asarray(w)
    return np.ascontiguousarray(w.reshape(w.shape[0], -1, P).transpose(2, 1, 0)).reshape(P, -1)


def kernel(**inputs):
    import concourse.bacc as bacc
    from concourse.bass_utils import run_bass_kernel_spmd

    x = {k: np.asarray(v) for k, v in inputs.items()}
    vectors = {
        "mix_g0": columns(x["norm_mix_g"][0]), "mix_g1": columns(x["norm_mix_g"][1]),
        "mlp_g0": columns(x["norm_mlp_g"][0]), "mlp_g1": columns(x["norm_mlp_g"][1]),
        "pw1_b": columns(x["conv_b_pw1"][0]), "dw_w": taps(x["conv_w_dw"][0]),
        "dw_b": columns(x["conv_b_dw"][0]), "ln_g": columns(x["conv_ln_g"][0]),
        "ln_b": columns(x["conv_ln_b"][0]),
        "idx_g": columns(np.concatenate([x["dsa_idx_k_g"][0]] * 2)),
        "idx_b": columns(np.concatenate([x["dsa_idx_k_b"][0]] * 2)),
        "even_g": columns(x["even_norm_pre_2"][0]), "rg_w": taps(x["rg_conv_w_2"][0]),
        "rg_b": columns(x["rg_conv_b_2"][0]), "gate_b": columns(x["rg_gate_b_2"][0]),
        "lam": columns(x["rg_lambda_2"][0]), "sc_w": taps(x["sc_conv_w_2"][0]),
        "odd_g": columns(x["odd_norm_pre_2"][0]), "gla_b": columns(x["gla_b_gate_2"][0]),
    }
    arrays = {
        "x": x["x"],
        "vectors": np.concatenate([vectors[n] for n, _ in VEC_SIZES], axis=1),
        "constants": constants(),
        "b_pw2": x["conv_b_pw2"][0], "final_g": x["final_g"], "even_post": x["even_norm_post_2"][0],
        "odd_post": x["odd_norm_post_2"][0], "gla_norm_g": x["gla_norm_g_2"][0],
    }
    for name in ("dsa_w_in", "dsa_w_out", "mlp_w1", "mlp_w2", "conv_w_pw1", "conv_w_pw2", "even_w_in_2",
                 "even_w_out_2", "rg_gate_w_2", "odd_w_in_2", "odd_w_out_2", "gla_w_gate_lr_2"):
        arrays[name] = x[name]
    arrays = {k: np.ascontiguousarray(v) for k, v in arrays.items()}

    nc = bacc.Bacc("TRN2", target_bir_lowering=False, num_devices=1,
                   dynamic_dma_scratch_size=1024)
    a = {k: nc.dram_tensor(f"in_{k}", v.shape, mybir.dt.from_np(v.dtype), kind="ExternalInput").ap()
         for k, v in arrays.items()}
    out = nc.dram_tensor("out", (1, S, D), F32, kind="ExternalOutput").ap()
    build(nc, a, out)
    result = run_bass_kernel_spmd(nc, [{f"in_{k}": v for k, v in arrays.items()}], core_ids=[0])
    return result.results[0]["out"]
```

```python
from contextlib import ExitStack

import numpy as np

import concourse.bass as bass
from concourse import mybir

F32 = mybir.dt.float32
F32R = mybir.dt.float32r
ALU = mybir.AluOpType
ACT = mybir.ActivationFunctionType
AX = mybir.AxisListType

P = 128
S = 512
T = S // P
D = 1024
KD = D // P
FF = 4 * D
EPS = 1e-6
BIG = 1e30
CAUSAL_FILL = -3.0e38
TAKEN = -3.4e38
HEADS = 8
IDX_DIM = 64
TOPK = min(256, S // 4)
CONV_W = 31
RG_W = 4
SC_W = 3
RG_C = 8.0
GLA_HEADS = 4
GLA_DK = 128
GLA_DV = 256
GLA_RANK = 16
CHUNK = 64
NCH = S // CHUNK
GLA_NORM = 16.0

VEC_SIZES = [
    ("mix_g0", KD), ("mlp_g0", KD), ("mix_g1", KD), ("mlp_g1", KD), ("pw1_b", 2 * KD),
    ("dw_w", KD * CONV_W), ("dw_b", KD), ("ln_g", KD), ("ln_b", KD), ("idx_g", 1), ("idx_b", 1),
    ("even_g", KD), ("rg_w", KD * RG_W), ("rg_b", KD), ("gate_b", 4 * KD), ("lam", 2 * KD),
    ("sc_w", KD * SC_W), ("odd_g", KD), ("final_g", KD), ("gla_b", 2 * GLA_HEADS),
]
VEC = {}
_at = 0
for _name, _n in VEC_SIZES:
    VEC[_name] = (_at, _n)
    _at += _n
NVEC = _at

CON_SIZES = [("ident", P), ("mean", P), ("fwd_mask", P), ("bwd_mask", P), ("causal", P),
             ("fwd_keep", S), ("bwd_keep", S)]
CON = {}
_at = 0
for _name, _n in CON_SIZES:
    CON[_name] = (_at, _n)
    _at += _n
NCON = _at

RAW = 4
RING = 4
SLOT = 1024
AHEAD = 3


class Lane:

    def __init__(self, name, sem):
        self.name, self.sem, self.count = name, sem, 0
        self.queue, self.waited = [], {}

    def wait(self, *marks):
        for m in marks:
            if m is None:
                continue
            sem, value = m
            if self.waited.get(id(sem), 0) < value:
                self.waited[id(sem)] = value
                self.queue.append(lambda e, sem=sem, value=value: e.wait_ge(sem, value))

    def do(self, make, after=(), signal=True):
        self.wait(*after)
        if not signal:
            self.queue.append(make)
            return None
        self.count += 1
        self.queue.append(lambda e: make(e).then_inc(self.sem, 1))
        return (self.sem, self.count)

    def last(self):
        return (self.sem, self.count) if self.count else None

    def play(self, engine):
        for step in self.queue:
            step(engine)


class Landing:

    def __init__(self, sem):
        self.sem, self.count = sem, 0

    def start(self, lane, out, in_, after=()):
        lane.wait(*after)
        self.count += 16
        sem = self.sem
        lane.queue.append(lambda e: e.dma_start(out, in_).then_inc(sem, 16))
        return (self.sem, self.count)


def build(nc, a, out):
    ctx = ExitStack()
    with ctx:
        def sem(name):
            return ctx.enter_context(nc.semaphore(name))

        def sb(name, shape, dt=F32, scope=ctx):
            return scope.enter_context(nc.sbuf_tensor(name, shape, dt))

        pe, act = Lane("pe", sem("pe_done")), Lane("act", sem("act_done"))
        dve, pool = Lane("dve", sem("dve_done")), Lane("pool", sem("pool_done"))
        sp = Lane("sp", None)

        H = sb("residual", [P, T, D])
        XH = sb("x_hi", [P, KD, S], F32R)
        XL = sb("x_lo", [P, KD, S], F32R)
        raw = [sb(f"w_raw{i}", [P, SLOT]) for i in range(RAW)]
        WH = [sb(f"w_hi{i}", [P, SLOT], F32R) for i in range(RING)]
        WL = [sb(f"w_lo{i}", [P, SLOT], F32R) for i in range(RING)]
        vec = sb("vectors", [P, NVEC])
        con = sb("constants", [P, NCON])
        gain_row = sb("gain_row", [P, D])
        norm_stat = sb("norm_stats", [P, 8, 8, T])
        rrow = sb("rstd_row", [P, S])
        rrow2 = sb("rstd_row_squared", [P, S])
        spare = sb("spare", [P, T, P])
        epsc = sb("eps_col", [P, 1])
        bank = [ctx.enter_context(nc.psum_tensor(f"bank{i}", [P, 512], F32)) for i in range(8)]
        bank_free = [[] for _ in range(8)]

        def V(name, i=0, n=1):
            at = VEC[name][0] + i
            return vec[:, at:at + n]

        def C(name):
            at, n = CON[name]
            return con[:, at:at + n]

        ident, mean_ones = C("ident"), C("mean")

        load_vec = Landing(sem("vec_landed"))
        load_x = [Landing(sem(f"x_landed{t}")) for t in range(T)]
        load_row = Landing(sem("gain_row_landed"))
        load_raw = [Landing(sem(f"raw_landed{i}")) for i in range(RAW)]

        load_con, load_con2 = Landing(sem("con_landed")), Landing(sem("con2_landed"))
        con_in = load_con.start(sp, con[:, 0:2 * P], a["constants"][:, 0:2 * P])
        x_in = [load_x[t].start(sp, H[:, t, :], a["x"][0, t * P:(t + 1) * P, :]) for t in range(T)]
        vec_in = load_vec.start(sp, vec[:, :], a["vectors"])
        eps_set = dve.do(lambda e: e.memset(epsc[:, :], EPS))

        def load_gain_row(name, after):
            return load_row.start(sp, gain_row[:, :], a[name].partition_broadcast(P), after)

        def units_of(name, src, cols, krows, per=None):
            ncols = sum(n for _, n in cols)
            per = per or SLOT // ncols
            src = src.rearrange("(k p) n -> p k n", p=P)
            return [{"name": name, "per": per, "cols": ncols,
                     "src": [src[:, k:k + per, c:c + n] for c, n in cols]}
                    for k in range(krows[0], krows[1], per)]

        dsa_in, dsa_out = a["dsa_w_in"][0], a["dsa_w_out"][0]
        stream = []
        stream += units_of("idx_narrow", dsa_in, [(3 * D + HEADS * IDX_DIM, IDX_DIM + HEADS)], (0, KD), KD)
        for name, c in (("qi", 3 * D), ("v0", 2 * D), ("v1", 2 * D + 512), ("q0", 0), ("k0", D), ("q1", 512),
                        ("k1", D + 512)):
            stream += units_of(name, dsa_in, [(c, 512)], (0, KD))
        for n in range(2):
            stream += units_of(f"dsa_out{n}", dsa_out, [(n * 512, 512)], (0, KD))

        def mlp_units(layer):
            got = []
            for half in range(2):
                for g in range(4):
                    got += units_of(f"up{layer}{half}{g}", a["mlp_w1"][layer],
                                    [(half * (FF // 2) + g * 512, 512)], (0, KD))
                for n in range(2):
                    got += units_of(f"down{layer}{half}{n}", a["mlp_w2"][layer], [(n * 512, 512)],
                                    (half * 16, half * 16 + 16))
            return got

        stream += mlp_units(0)
        for g in range(4):
            stream += units_of(f"pw1{g}", a["conv_w_pw1"][0], [(g * 256, 256), (D + g * 256, 256)], (0, KD))
        for n in range(2):
            stream += units_of(f"pw2{n}", a["conv_w_pw2"][0], [(n * 512, 512)], (0, KD))
        stream += mlp_units(1)
        even_in, even_out = a["even_w_in_2"][0], a["even_w_out_2"][0]
        EVEN_ORDER = [("xa0", 0), ("gc0", 4 * D), ("xb0", 2 * D), ("gb0", 3 * D), ("zb0", 5 * D),
                      ("xa1", 512), ("gc1", 4 * D + 512), ("xb1", 2 * D + 512), ("gb1", 3 * D + 512),
                      ("zb1", 5 * D + 512), ("za0", D), ("za1", D + 512)]
        for name, c in EVEN_ORDER:
            stream += units_of(name, even_in, [(c, 512)], (0, KD))
        for name, n, k in (("eout_b0", 0, KD), ("eout_a0", 0, 0), ("eout_a1", 1, 0), ("eout_b1", 1, KD)):
            stream += units_of(name, even_out, [(n * 512, 512)], (k, k + KD))
        odd_in, odd_out = a["odd_w_in_2"][0], a["odd_w_out_2"][0]
        stream += units_of("gq", odd_in, [(0, 512)], (0, KD))
        stream += units_of("lr", odd_in, [(3 * D, 2 * GLA_RANK)], (0, KD), KD)
        for name, c in (("gk", 512), ("gr0", 2 * D), ("gv0", D), ("gv1", D + 512), ("gr1", 2 * D + 512)):
            stream += units_of(name, odd_in, [(c, 512)], (0, KD))
        for n in range(2):
            stream += units_of(f"oout{n}", odd_out, [(n * 512, 512)], (0, KD))

        state = {"loaded": 0, "split": 0, "used": 0}
        raw_free = [[] for _ in range(RAW)]
        ring_free = [[] for _ in range(RING)]
        split_of = []

        def queue_loads(upto):
            while state["loaded"] < min(upto, len(stream)):
                unit, i = stream[state["loaded"]], state["loaded"] % RAW
                dst = raw[i][:, 0:unit["per"] * unit["cols"]].rearrange("p (k n) -> p k n", k=unit["per"])
                at = 0
                for src in unit["src"]:
                    n = src.shape[2]
                    unit["landed"] = load_raw[i].start(sp, dst[:, :, at:at + n], src, raw_free[i])
                    at += n
                state["loaded"] += 1

        def queue_splits(upto):
            while state["split"] < min(upto, len(stream)):
                u = state["split"]
                queue_loads(u + 1)
                unit, i = stream[u], u % RING
                n = unit["per"] * unit["cols"]
                src, hi, lo = raw[u % RAW][:, 0:n], WH[i][:, 0:n], WL[i][:, 0:n]
                h = act.do(lambda e, src=src, hi=hi: e.activation(hi, src, ACT.Copy), [unit["landed"]] + ring_free[i])
                l = pool.do(lambda e, src=src, hi=hi, lo=lo: e.tensor_tensor(
                    lo, src, hi.bitcast(F32), ALU.subtract), [unit["landed"], h] + ring_free[i])
                raw_free[u % RAW] = [h, l]
                unit["split"] = [h, l]
                state["split"] += 1
                queue_loads(u + 1 + RAW)

        slots = []

        def slot():
            if slots:
                task = slots.pop(0)
                if task:
                    task()

        def all_slots():
            while slots:
                slot()

        def product(name, k0, banks, x, x_ready, feature_major, first=True, last=True):
            xh, xl = x
            k, mark = k0, None
            while state["used"] < len(stream) and stream[state["used"]]["name"] == name:
                u = state["used"]
                queue_splits(u + AHEAD)
                unit, i = stream[u], u % RING
                per, cols = unit["per"], unit["cols"]
                pe.wait(*unit["split"])
                wh = WH[i][:, 0:per * cols].rearrange("p (k n) -> p k n", k=per)
                wl = WL[i][:, 0:per * cols].rearrange("p (k n) -> p k n", k=per)
                ends = u + 1 == len(stream) or stream[u + 1]["name"] != name
                for kk in range(per):
                    while k >= len(x_ready):
                        slot()
                    pe.wait(*x_ready[k])
                    for j, b in enumerate(banks):
                        begin = first and k == k0
                        if begin:
                            pe.wait(*bank_free[b])
                        end = last and ends and kk == per - 1
                        if feature_major:
                            m = min(P, cols - j * P)
                            wj, wlj = wh[:, kk, j * P:j * P + m], wl[:, kk, j * P:j * P + m]
                            o = bank[b][0:m, :]
                            trio = ((wj, xh[:, k, :]), (wj, xl[:, k, :]), (wlj, xh[:, k, :]))
                        else:
                            xt, xlt = xh[:, k, j * P:(j + 1) * P], xl[:, k, j * P:(j + 1) * P]
                            o = bank[b][:, 0:cols]
                            trio = ((xt, wh[:, kk, :]), (xt, wl[:, kk, :]), (xlt, wh[:, kk, :]))
                        for n, (l, r) in enumerate(trio):
                            done = kk == per - 1 and j == len(banks) - 1 and n == 2
                            mark = mm(o, l, r, begin and n == 0, end and n == 2, signal=done) or mark
                    k += 1
                    if kk == per - 1:
                        ring_free[i] = [mark]
                        state["used"] += 1
                    if not (ends and kk == per - 1):
                        slot()
            assert mark is not None, name
            return mark

        turn_bank = {"ring": list(range(8)), "at": 0, "now": [0, 1, 2, 3]}

        def four():
            ring, at = turn_bank["ring"], turn_bank["at"]
            turn_bank["now"] = [ring[(at + i) % len(ring)] for i in range(4)]
            turn_bank["at"] = (at + 4) % len(ring)
            return turn_bank["now"]

        def others():
            return [b for b in range(8) if b not in turn_bank["now"]]

        def product_banks(ring, at=0):
            turn_bank["ring"], turn_bank["at"] = ring, at

        def mm(o, l, r, start, stop, after=(), signal=True):
            return pe.do(lambda e: e.matmul(o, l, r, start=start, stop=stop), after, signal)

        def turn(o, i, after=(), signal=True):
            return pe.do(lambda e: e.transpose(o, i, ident), list(after) + [con_in], signal)

        def gone():
            return [lane.last() for lane in (pe, act, dve, pool)]

        def settle(marks, *lanes):
            for lane in lanes:
                lane.wait(*marks)

        final_even = sb("final_even_gain", [P, KD])
        gains_in = dve.do(lambda e: e.tensor_tensor(final_even[:, :], V("final_g", 0, KD), V("even_g", 0, KD),
                                                    ALU.mult), [vec_in])
        spare_free = [[]]

        def split_bank(b, src, hi, lo, scale, after):
            if scale is None:
                h = act.do(lambda e: e.activation(hi, src, ACT.Copy), after)
                l = dve.do(lambda e: e.tensor_tensor(lo, src, hi.bitcast(F32), ALU.subtract), [h])
            else:
                h = act.do(lambda e: e.activation(hi, src, ACT.Copy, scale=scale), after)
                l = dve.do(lambda e: e.scalar_tensor_tensor(
                    out=lo, in0=src, scalar=scale, in1=hi.bitcast(F32), op0=ALU.mult, op1=ALU.subtract), [h])
            bank_free[b] = [h, l]
            return [h, l]

        def split_sbuf(src, hi, lo, after):
            h = act.do(lambda e: e.activation(hi, src, ACT.Copy), after)
            l = dve.do(lambda e: e.tensor_tensor(lo, src, hi.bitcast(F32), ALU.subtract), [h])
            return [h, l]

        def turn_and_split(src, k, marks, gain, x_free, x_ready):
            b = others()[turned_count[0] % 4]
            turned_count[0] += 1
            for t in range(T):
                m = turn(bank[b][:, t * P:(t + 1) * P], src[:, t, k * P:(k + 1) * P],
                         list(marks[t]) + bank_free[b], signal=(t == T - 1))
            assert len(x_ready) == k
            x_ready.append(split_bank(b, bank[b][:, :], XH[:, k, :], XL[:, k, :], gain, [m, gains_in] + x_free))

        turned_count = [0]

        def squares(src, out, after):
            junk = spare[:, 0:src.shape[-1] // P, :].rearrange("p t n -> p (t n)")
            m = act.do(lambda e: e.activation(junk, src, ACT.Square, accum_out=out), list(after) + spare_free[0])
            spare_free[0] = [m]
            return m

        def inverse_root(out, total, width, after):
            root = act.do(lambda e: e.activation(out, total, ACT.Sqrt, bias=epsc[:, 0:1], scale=1.0 / width),
                          list(after) + [eps_set])
            return dve.do(lambda e: e.reciprocal(out, out), [root])

        def broadcast(column, out, after, b=None):
            marks = [dve.do(lambda e, t=t: e.tensor_scalar(
                spare[:, t, :], ident, column[:, t:t + 1], None, ALU.mult), list(after) + [con_in] + spare_free[0])
                for t in range(T)]
            b = others()[turned_count[0] % 4] if b is None else b
            turned_count[0] += 1
            m = mm(bank[b][:, :], mean_ones, spare[:, :, :].rearrange("p t n -> p (t n)"), True, True,
                   marks + bank_free[b])
            spare_free[0] = [m]
            r = act.do(lambda e: e.activation(out, bank[b][:, :], ACT.Copy, scale=float(D)), [m, dve.last()])
            bank_free[b] = [r]
            return r

        class Norm:
            count = 0

            def __init__(self, gain, x_free):
                self.at, self.gain, self.x_free = Norm.count, gain, x_free
                Norm.count += 1
                self.x_ready, self.sums = [], []

            def col(self, c):
                return norm_stat[:, self.at, c, :]

            def r(self, t):
                return norm_stat[:, self.at, 2, t:t + 1]

            def rr(self, t):
                return norm_stat[:, self.at, 3, t:t + 1]

            def turn(self, k):
                turn_and_split(H, k, self.marks[k // 4], self.gain(k), self.x_free, self.x_ready)

            def add_squares(self, half):
                for t in range(T):
                    self.sums.append(squares(H[:, t, half * 512:(half + 1) * 512],
                                             norm_stat[:, self.at, half, t:t + 1], self.marks[half][t]))

            def roots(self):
                both = dve.do(lambda e: e.tensor_tensor(self.col(2), self.col(0), self.col(1), ALU.add), self.sums)
                self.r_ready = inverse_root(self.col(2), self.col(2), D, [both])
                self.rr_ready = dve.do(lambda e: e.tensor_tensor(self.col(3), self.col(2), self.col(2), ALU.mult),
                                       [self.r_ready])

            def row(self):
                self.row_ready = broadcast(self.col(2), rrow[:, :], [self.r_ready])

            marks = None

            def half(self, n, marks):
                self.marks = (self.marks or []) + [marks]
                if n == 0:
                    for k in range(4):
                        slots.append(lambda k=k: self.turn(k))
                    slots.append(lambda: self.add_squares(0))
                else:
                    slots.append(lambda: [self.turn(4), self.turn(5)])
                    slots.append(lambda: [self.turn(6), self.turn(7)])
                    slots.append(lambda: self.add_squares(1))
                    slots.append(self.roots)

        def start_norm():
            norm = Norm(lambda k: V("mix_g0", k), [])
            norm.marks = [[[x_in[t]] for t in range(T)]] * 2
            for t in range(T):
                for k in range(KD):
                    m = turn(bank[k][:, t * P:(t + 1) * P], H[:, t, k * P:(k + 1) * P], [x_in[t]])
            for k in range(KD):
                norm.x_ready.append(split_bank(k, bank[k][:, :], XH[:, k, :], XL[:, k, :], norm.gain(k),
                                               [m, gains_in]))
            norm.add_squares(0)
            norm.add_squares(1)
            norm.roots()
            return norm

        def close(names, x, x_ready, evacuate, norm):
            for n in range(2):
                banks = four()
                m = product(names[n], 0, banks, x, x_ready, False)
                all_slots()
                norm.half(n, evacuate(n, banks, m))
            return norm

        def add_to_residual(n, banks, m, scale=None, after=()):
            marks = []
            for t, b in enumerate(banks):
                hh = H[:, t, n * 512:(n + 1) * 512]
                if scale is None:
                    d = dve.do(lambda e, b=b, hh=hh: e.tensor_tensor(hh, bank[b][:, :], hh, ALU.add), [m] + list(after))
                else:
                    d = dve.do(lambda e, b=b, hh=hh, t=t: e.scalar_tensor_tensor(
                        out=hh, in0=bank[b][:, :], scalar=scale(t), in1=hh, op0=ALU.mult, op1=ALU.add),
                        [m] + list(after))
                bank_free[b] = [d]
                marks.append([d])
            return marks

        def times_row(b, m, dst, row, after=()):
            d = dve.do(lambda e: e.tensor_tensor(dst, bank[b][:, :], row, ALU.mult), [m] + list(after))
            bank_free[b] = [d]
            return d

        X = (XH, XL)

        def dsa_stage(norm):
            scope = ExitStack()
            with scope:
                YH = sb("att_hi", [P, HEADS, S], F32R, scope=scope)
                YL = sb("att_lo", [P, HEADS, S], F32R, scope=scope)
                vT = sb("v_tok", [P, T, D], scope=scope)
                qT = sb("q_feat", [P, HEADS, S], scope=scope)
                kT = sb("k_feat", [P, HEADS, S], scope=scope)
                bias = sb("score_then_bias", [P, T, S], scope=scope)
                att = sb("att_stats", [P, 4, 2], scope=scope)
                index = ExitStack()
                qiT = sb("qi_feat", [P, HEADS // 2, S], scope=index)
                ki = sb("ki_tok", [P, T, P], scope=index)
                kiT = sb("ki_feat", [P, S], scope=index)
                wi = sb("wi_tok", [P, T, HEADS], scope=index)
                bn = sb("ki_stats", [P, T, 6], scope=index)
                mv = sb("ki_meanvar", [P, T, 2], scope=index)
                relu = [sb(f"relu{i}", [P, S], scope=index) for i in range(2)]
                top8 = sb("top8", [P, T, 8], scope=index)
                x_ready = norm.x_ready

                banks = four()
                m = product("idx_narrow", 0, banks, X, x_ready, False)
                sc = dve.do(lambda e: e.tensor_scalar(norm.col(4), norm.col(2), P ** -0.5, None, ALU.mult),
                            [norm.r_ready])
                nsc_ready = dve.do(lambda e: e.tensor_scalar(norm.col(5), norm.col(4), -1.0, None, ALU.mult), [sc])
                wi_ready, ln = [], []
                for t, b in enumerate(banks):
                    w = dve.do(lambda e, t=t, b=b: e.tensor_scalar(
                        wi[:, t, :], bank[b][:, IDX_DIM:IDX_DIM + HEADS], norm.rr(t),
                        HEADS ** -0.5 * IDX_DIM ** -0.5, ALU.mult, ALU.mult), [m, norm.rr_ready])
                    c = dve.do(lambda e, t=t, b=b: e.tensor_scalar(
                        ki[:, t, 0:IDX_DIM], bank[b][:, 0:IDX_DIM], norm.r(t), None, ALU.mult), [m, norm.r_ready])
                    bank_free[b] = [w, c]
                    wi_ready.append(w)
                    s = dve.do(lambda e, t=t: e.bn_stats(bn[:, t, :], ki[:, t, 0:IDX_DIM]), [c])
                    ln.append(dve.do(lambda e, t=t: e.bn_aggr(mv[:, t, :], bn[:, t, :]), [s]))
                root = act.do(lambda e: e.activation(norm.col(6), mv[:, :, 1], ACT.Sqrt, bias=epsc[:, 0:1]),
                              ln + [eps_set])
                rs = dve.do(lambda e: e.reciprocal(norm.col(6), norm.col(6)), [root])
                kn = []
                for t in range(T):
                    for c in (1, 0):
                        d = dve.do(lambda e, t=t, c=c: e.tensor_scalar(
                            ki[:, t, c * IDX_DIM:(c + 1) * IDX_DIM], ki[:, t, 0:IDX_DIM], mv[:, t, 0:1],
                            norm_stat[:, norm.at, 6, t:t + 1], ALU.subtract, ALU.mult), [rs] + kn[-1:])
                        kn.append(d)
                ki_ready = []

                def turn_ki():
                    b = others()[0]
                    for t in range(T):
                        m = turn(bank[b][:, t * P:(t + 1) * P], ki[:, t, :], [kn[-1]] + bank_free[b])
                    ki_ready.append(dve.do(lambda e: e.tensor_scalar(
                        kiT[:, :], bank[b][:, :], V("idx_g"), V("idx_b"), ALU.mult, ALU.add), [m]))
                    bank_free[b] = [ki_ready[0]]

                def feature(name, dst, t0, row=None):
                    banks = four()
                    m = product(name, 0, banks, X, x_ready, True)
                    marks = []
                    for j, b in enumerate(banks):
                        if row is None:
                            d = act.do(lambda e, j=j, b=b: e.activation(dst[:, t0 + j, :], bank[b][:, :], ACT.Copy), [m])
                            bank_free[b] = [d]
                        else:
                            d = times_row(b, m, dst[:, t0 + j, :], row, [norm.row_ready])
                        marks.append(d)
                    return marks

                slots.extend([turn_ki, norm.row])
                qi_ready = feature("qi", qiT, 0)

                assert TOPK == P
                score_ready, bias_ready = [None] * T, [None] * T
                relu_free = [[], []]
                uses = [0]
                bias_ready[0] = dve.do(lambda e: e.tensor_copy(bias[:, 0, 0:P], C("causal")), [con2_in])

                def score_task(t, h):
                    n = (t + 1) * P
                    b, i, p0 = others()[uses[0] % 4], uses[0] % 2, IDX_DIM * (h % 2)
                    uses[0] += 1
                    m = mm(bank[b][:, 0:n], qiT[p0:p0 + IDX_DIM, h // 2, t * P:(t + 1) * P],
                           kiT[p0:p0 + IDX_DIM, 0:n], True, True, [qi_ready[h // 2], ki_ready[0]] + bank_free[b])
                    r = act.do(lambda e: e.activation(relu[i][:, 0:n], bank[b][:, 0:n], ACT.Relu), [m] + relu_free[i])
                    bank_free[b] = [r]
                    w = wi[:, t, h:h + 1]
                    if h == 0:
                        acc = dve.do(lambda e: e.tensor_scalar(
                            bias[:, t, 0:n], relu[i][:, 0:n], w, None, ALU.mult), [r, wi_ready[t]])
                    else:
                        acc = dve.do(lambda e: e.scalar_tensor_tensor(
                            out=bias[:, t, 0:n], in0=relu[i][:, 0:n], scalar=w, in1=bias[:, t, 0:n],
                            op0=ALU.mult, op1=ALU.add), [r, score_ready[t]])
                    relu_free[i] = [acc]
                    score_ready[t] = acc
                    if h == HEADS - 1:
                        c = bias[:, t, t * P:n]
                        score_ready[t] = pool.do(lambda e: e.affine_select(
                            out=c, in_=c, compare_op=ALU.is_ge, fill=CAUSAL_FILL, base=0,
                            pattern=[[-1, P]], channel_multiplier=1), [acc])

                def top_round(t, r):
                    n = (t + 1) * P
                    m8 = dve.do(lambda e: e.max(top8[:, t, :], bias[:, t, 0:n]), [score_ready[t]])
                    score_ready[t] = dve.do(lambda e: e.match_replace(
                        out=bias[:, t, 0:n], in_to_replace=top8[:, t, :], in_values=bias[:, t, 0:n],
                        imm_value=TAKEN), [m8])
                    if r == TOPK // 8 - 1:
                        bias_ready[t] = dve.do(lambda e: e.tensor_scalar(
                            bias[:, t, 0:n], bias[:, t, 0:n], TAKEN, -BIG, ALU.not_equal, ALU.mult),
                            [score_ready[t]])

                scoring = [(score_task, t, h) for t in range(1, T) for h in range(HEADS)]
                rounds = [(top_round, t, r) for r in range(TOPK // 8) for t in range(1, T)]
                all_slots()
                in_slots(scoring, 4)
                in_slots(rounds, 3)

                v_ready = []
                for n in range(2):
                    banks = four()
                    m = product(f"v{n}", 0, banks, X, x_ready, False)
                    for t, b in enumerate(banks):
                        d = act.do(lambda e, t=t, n=n, b=b: e.activation(
                            vT[:, t, n * 512:(n + 1) * 512], bank[b][:, :], ACT.Copy, scale=norm.r(t)), [m])
                        bank_free[b] = [d]
                        v_ready.append(d)
                q_ready = feature("q0", qT, 0)
                k_ready = feature("k0", kT, 0, rrow[:, :])
                all_slots()
                index.close()
                left = gone()
                settle(left, act, dve)
                lg = [sb(f"prob{i}", [P, S], scope=scope) for i in range(4)]
                PT = [sb(f"prob_turned{i}", [P, S], scope=scope) for i in range(3)]

                product_banks([0, 1, 2, 3])
                items = [(h, t) for h in range(HEADS) for t in range(T)]
                logit_mark, prob_mark = {}, {}
                turned_mark, copied = {}, {}
                value_mark, exp_mark = {}, {}
                o_ready = []

                def logits(i):
                    h, t = items[i]
                    n, b = (t + 1) * P, 4 + i % 2
                    logit_mark[i] = mm(bank[b][:, 0:n], qT[:, h, t * P:(t + 1) * P], kT[:, h, 0:n], True, True,
                                       [q_ready[h], k_ready[h]] + bank_free[b])

                def softmax(i):
                    h, t = items[i]
                    n, b, p = (t + 1) * P, 4 + i % 2, lg[i % 4]
                    mx, sm = att[:, i % 4, 0:1], att[:, i % 4, 1:2]
                    m1 = dve.do(lambda e: e.tensor_tensor_reduce(
                        out=p[:, 0:n], in0=bank[b][:, 0:n], in1=bias[:, t, 0:n], scale=1.0,
                        scalar=-3e38, op0=ALU.add, op1=ALU.max, accum_out=mx),
                        [logit_mark[i], bias_ready[t], turned_mark.get(i - 4), prob_mark.get(i - 4)])
                    bank_free[b] = [m1]
                    m2 = dve.do(lambda e: e.tensor_scalar(
                        mx, mx, norm_stat[:, norm.at, 5, t:t + 1], None, ALU.mult), [m1, nsc_ready])
                    ex = act.do(lambda e: e.activation(
                        p[:, 0:n], p[:, 0:n], ACT.Exp, bias=mx, scale=norm_stat[:, norm.at, 4, t:t + 1],
                        accum_out=sm), [m2])
                    rc = dve.do(lambda e: e.reciprocal(sm, sm), [ex])
                    prob_mark[i] = dve.do(lambda e: e.tensor_scalar(p[:, 0:n], p[:, 0:n], sm, None, ALU.mult), [rc])

                def turn_probs(i):
                    h, t = items[i]
                    n, p, o = (t + 1) * P, lg[i % 4], PT[i % 3]
                    for s in range(t + 1):
                        m = turn(bank[6][:, s * P:(s + 1) * P], p[:, s * P:(s + 1) * P],
                                 [prob_mark[i]] + bank_free[6])
                    turned_mark[i] = m
                    after = [m, value_mark.get(i - 3)]
                    if i % 2:
                        c = act.do(lambda e: e.activation(o[:, 0:n], bank[6][:, 0:n], ACT.Copy), after)
                    else:
                        c = dve.do(lambda e: e.tensor_copy(o[:, 0:n], bank[6][:, 0:n]), after)
                    bank_free[6] = [c]
                    copied[i] = c

                def values(i):
                    h, t = items[i]
                    p = PT[i % 3]
                    for s in range(t + 1):
                        m = mm(bank[7][:, t * P:(t + 1) * P], vT[:, s, h * P:(h + 1) * P],
                               p[:, s * P:(s + 1) * P], s == 0, s == t, [copied[i]] + v_ready + bank_free[7])
                    value_mark[i] = m
                    if t == T - 1:
                        o_ready.append(split_bank(7, bank[7][:, :], YH[:, h, :], YL[:, h, :], None, [m]))

                def step(i):
                    if i < len(items):
                        logits(i)
                    if 0 <= i - 2 < len(items):
                        turn_probs(i - 2)
                    if 0 <= i - 3 < len(items):
                        values(i - 3)
                    if i < len(items):
                        softmax(i)

                steps = [(step, i) for i in range(len(items) + 3)]
                in_slots(steps[:14], 1)
                q_ready += feature("q1", qT, 4)
                k_ready += feature("k1", kT, 4, rrow[:, :])
                x_free = [pe.last()]
                all_slots()
                in_slots(steps[14:], 2)

                nxt = Norm(lambda k: V("mlp_g0", k), x_free)
                banks = four()
                m = product("dsa_out0", 0, banks, (YH, YL), o_ready, False)
                all_slots()
                product_banks(list(range(8)), 4)
                nxt.half(0, add_to_residual(0, banks, m))
                banks = four()
                m = product("dsa_out1", 0, banks, (YH, YL), o_ready, False)
                all_slots()
                nxt.half(1, add_to_residual(1, banks, m))
            nxt.left = gone()
            return nxt

        def mlp_stage(layer, norm, next_gain):
            scope = ExitStack()
            with scope:
                FH = sb(f"f_hi{layer}", [P, 16, S], F32R, scope=scope)
                FL = sb(f"f_lo{layer}", [P, 16, S], F32R, scope=scope)
                relu = [sb(f"f_relu{layer}_{i}", [P, S], scope=scope) for i in range(4)]
                square = [sb(f"f_square{layer}_{i}", [P, S], scope=scope) for i in range(4)]
                relu_free, square_free = [[] for _ in range(4)], [[] for _ in range(4)]
                f_free = []
                for half in range(2):
                    f_ready = []
                    for g in range(4):
                        banks = four()
                        m = product(f"up{layer}{half}{g}", 0, banks, X, norm.x_ready, True)
                        all_slots()
                        if half == 0 and g == 0:
                            settle(norm.left, act, dve)
                        for j, b in enumerate(banks):
                            r = act.do(lambda e, j=j, b=b: e.activation(relu[j][:, :], bank[b][:, :], ACT.Relu),
                                       [m] + relu_free[j])
                            bank_free[b] = [r]
                            s = dve.do(lambda e, j=j: e.tensor_tensor(square[j][:, :], relu[j][:, :], relu[j][:, :],
                                                                      ALU.mult), [r] + square_free[j])
                            relu_free[j] = [s]
                            k = g * 4 + j
                            f = split_sbuf(square[j][:, :], FH[:, k, :], FL[:, k, :], [s] + f_free)
                            square_free[j] = f
                            f_ready.append(f)
                    def evacuate(n, banks, m):
                        return add_to_residual(n, banks, m, norm.rr, [norm.rr_ready])

                    if half == 0:
                        for n in range(2):
                            banks = four()
                            m = product(f"down{layer}{half}{n}", 0, banks, (FH, FL), f_ready, False)
                            evacuate(n, banks, m)
                        f_free = [m]
                    else:
                        nxt = close([f"down{layer}10", f"down{layer}11"], (FH, FL), f_ready, evacuate,
                                    Norm(next_gain, [m]))
            nxt.left = gone()
            return nxt

        def conv_stage(norm):
            scope = ExitStack()
            with scope:
                PAD = CONV_W - 1
                every = list(range(CONV_W))
                PE_TAPS = {7: every, 6: every[11:]}
                POOL_TAPS = {1: every, 3: every[:25]}
                DVE_TAPS = {0: every, 2: every, 3: every[25:], 4: every, 5: every, 6: every[:11]}
                u = sb("conv_u", [P, KD, PAD + S], scope=scope)
                c = sb("conv_c", [P, KD, S], scope=scope)
                odd = [sb(f"conv_sum{i}", [P, S], scope=scope) for i in range(2)]
                mean = sb("conv_mean", [P, S], scope=scope)
                var = sb("conv_var", [P, T], scope=scope)
                taps = ExitStack()
                diag = sb("conv_diag", [P, sum(len(v) for v in PE_TAPS.values()), P], scope=taps)
                lin = [sb(f"conv_lin{i}", [P, S], scope=taps) for i in range(2)]
                gate = [sb(f"conv_gate{i}", [P, S], scope=taps) for i in range(2)]
                part = [sb(f"conv_product{i}", [P, S], scope=taps) for i in range(3)]
                u_ready = [None] * KD
                parts_done = {k: [] for k in range(KD)}
                odd_free, part_free = [[], []], [[], [], []]

                def window(k, i):
                    return u[:, k, i:i + S], V("dw_w", k * CONV_W + i)

                def dve_tap(k, i):
                    n = DVE_TAPS[k].index(i)
                    (src, w), side = window(k, i), n % 2
                    dst = c[:, k, :] if side == 0 and k not in POOL_TAPS else odd[side][:, :]
                    if n == 0 and k not in POOL_TAPS:
                        m = dve.do(lambda e: e.tensor_scalar(dst, src, w, V("dw_b", k), ALU.mult, ALU.add), [u_ready[k]])
                    elif n < 2:
                        m = dve.do(lambda e: e.tensor_scalar(dst, src, w, None, ALU.mult), [u_ready[k]] + odd_free[side])
                    else:
                        m = dve.do(lambda e: e.scalar_tensor_tensor(
                            out=dst, in0=src, scalar=w, in1=dst, op0=ALU.mult, op1=ALU.add), [dve_mark[side]])
                    dve_mark[side] = m
                    if n == len(DVE_TAPS[k]) - 1:
                        for side in ((0, 1) if k in POOL_TAPS else (1,)):
                            d = dve.do(lambda e, side=side: e.tensor_tensor(
                                c[:, k, :], c[:, k, :], odd[side][:, :], ALU.add), dve_mark + parts_done[k])
                            parts_done[k] = [d]
                            odd_free[side] = [d]

                def pool_tap(k, i):
                    (src, w), p = window(k, i), pool_count[0] % 3
                    if i == POOL_TAPS[k][0]:
                        m = act.do(lambda e: e.activation(c[:, k, :], src, ACT.Identity, scale=w, bias=V("dw_b", k)),
                                   [u_ready[k]])
                    else:
                        m = act.do(lambda e: e.activation(part[p][:, :], src, ACT.Copy, scale=w),
                                   [u_ready[k]] + part_free[p])
                        m = pool.do(lambda e: e.tensor_tensor(c[:, k, :], c[:, k, :], part[p][:, :], ALU.add),
                                    [m, pool_mark[0]])
                        part_free[p] = [m]
                        pool_count[0] += 1
                    pool_mark[0] = m
                    if i == POOL_TAPS[k][-1]:
                        parts_done[k] = [m]

                pool_count, pool_mark, dve_mark = [0], [None], [None, None]
                diag_at, diag_marks = {}, {}
                for k in PE_TAPS:
                    for i in PE_TAPS[k]:
                        diag_at[k, i] = len(diag_at)

                def make_diag(k, i):
                    diag_marks[k, i] = act.do(lambda e: e.activation(
                        diag[:, diag_at[k, i], :], ident, ACT.Copy, scale=V("dw_w", k * CONV_W + i)), [con_in])

                slots.append(norm.row)
                dve_due, pool_due, diag_due = [], [], list(diag_at)

                def some(n_dve, n_pool, n_diag=0):
                    for n, due, take in ((n_dve, dve_due, dve_tap), (n_pool, pool_due, pool_tap),
                                         (n_diag, diag_due, make_diag)):
                        for _ in range(min(n, len(due))):
                            take(*due.pop(0))

                lin_free, gate_free = [[], []], [[], []]
                x_ready = norm.x_ready
                for g in range(4):
                    banks = four()
                    m = product(f"pw1{g}", 0, banks, X, x_ready, True)
                    all_slots()
                    if g == 0:
                        settle(norm.left, act, dve, pool)
                        row_in = load_gain_row("b_pw2", [])
                        padded = dve.do(lambda e: e.memset(u[:, :, 0:PAD], 0.0))
                    for j in range(2):
                        k = 2 * g + j
                        g2 = times_row(banks[2 + j], m, gate[j][:, :], rrow[:, :], [norm.row_ready] + gate_free[j])
                        g1 = times_row(banks[j], m, lin[j][:, :], rrow[:, :], lin_free[j])
                        s = act.do(lambda e, j=j, k=k: e.activation(
                            gate[j][:, :], gate[j][:, :], ACT.Sigmoid, bias=V("pw1_b", KD + k)), [g2])
                        u_ready[k] = dve.do(lambda e, j=j, k=k: e.scalar_tensor_tensor(
                            out=u[:, k, PAD:PAD + S], in0=lin[j][:, :], scalar=V("pw1_b", k), in1=gate[j][:, :],
                            op0=ALU.add, op1=ALU.mult), [s, g1, padded])
                        lin_free[j] = gate_free[j] = [u_ready[k]]
                    for k in (2 * g, 2 * g + 1):
                        pool_due += [(k, i) for i in POOL_TAPS.get(k, [])]
                        if k != 3:
                            dve_due += [(k, i) for i in DVE_TAPS.get(k, [])]
                    if g < 3:
                        in_slots([(some, 3, 1, 3)] * 7, 1)
                x_free = [pe.last()]
                while pool_due:
                    some(2, 1)
                dve_due += [(3, i) for i in DVE_TAPS[3]]
                some(len(dve_due), 0)

                bm, bc, bv = four()[:3]
                order = [0, 1, 2, 7, 4, 5, 6, 3]
                for k in order:
                    if k in PE_TAPS:
                        for i in PE_TAPS[k]:
                            m = mm(bank[bc][:, :], diag[:, diag_at[k, i], :], u[:, k, i:i + S], i == PE_TAPS[k][0],
                                   i == PE_TAPS[k][-1], [diag_marks[k, i], u_ready[k], padded] + bank_free[bc])
                        if k in DVE_TAPS:
                            d = dve.do(lambda e, k=k: e.tensor_tensor(c[:, k, :], bank[bc][:, :], c[:, k, :], ALU.add),
                                       [m] + parts_done[k])
                        else:
                            d = act.do(lambda e, k=k: e.activation(
                                c[:, k, :], bank[bc][:, :], ACT.Identity, bias=V("dw_b", k)), [m])
                        bank_free[bc] = parts_done[k] = [d]
                    if k == 7:
                        continue
                    m = mm(bank[bm][:, :], mean_ones, c[:, k, :], k == order[0], False,
                           parts_done[k] + bank_free[bm])
                m = mm(bank[bm][:, :], mean_ones, c[:, 7, :], False, True, parts_done[7])
                taps.close()
                after_taps = gone()
                YH = sb("conv_hi", [P, KD, S], F32R, scope=scope)
                YL = sb("conv_lo", [P, KD, S], F32R, scope=scope)
                mean_ready = act.do(lambda e: e.activation(mean[:, :], bank[bm][:, :], ACT.Copy), [m])
                bank_free[bm] = [mean_ready]
                sq_free = [[], []]
                sq = odd
                sq_marks = []
                for n, k in enumerate(order):
                    i = n % 2
                    lane = pool if n in (2, 5) else dve
                    cent = lane.do(lambda e, k=k: e.tensor_tensor(
                        c[:, k, :], c[:, k, :], mean[:, :], ALU.subtract), [mean_ready])
                    s = act.do(lambda e, k=k, i=i: e.activation(sq[i][:, :], c[:, k, :], ACT.Square),
                               [cent] + odd_free[i] + sq_free[i])
                    for t in range(T):
                        m = mm(bank[bv][:, t:t + 1], sq[i][:, t * P:(t + 1) * P], mean_ones[:, 0:1],
                               n == 0 and t == 0, n == KD - 1 and t == T - 1, [s] + bank_free[bv])
                    sq_free[i] = [m]
                root = act.do(lambda e: e.activation(var[:, :], bank[bv][:, 0:T], ACT.Sqrt, bias=epsc[:, 0:1]), [m])
                bank_free[bv] = [root]
                rs = dve.do(lambda e: e.reciprocal(var[:, :], var[:, :]), [root])
                rs = broadcast(var[:, :], rrow[:, :], [rs], bc)
                y_ready = []
                settle(after_taps, act, dve)
                for k in range(KD):
                    n = dve.do(lambda e, k=k: e.tensor_tensor(c[:, k, :], c[:, k, :], rrow[:, :], ALU.mult), [rs])
                    s = act.do(lambda e, k=k: e.activation(c[:, k, :], c[:, k, :], ACT.Silu,
                                                           bias=V("ln_b", k), scale=V("ln_g", k)), [n])
                    y_ready.append(split_sbuf(c[:, k, :], YH[:, k, :], YL[:, k, :], [s]))
                biased = [[None] * T for _ in range(2)]

                def add_bias(n):
                    for t in range(T):
                        hh = H[:, t, n * 512:(n + 1) * 512]
                        biased[n][t] = pool.do(lambda e, hh=hh: e.tensor_tensor(
                            hh, hh, gain_row[:, n * 512:(n + 1) * 512], ALU.add), [row_in])

                slots.extend([lambda: add_bias(0), None, None, lambda: add_bias(1)])

                def evacuate(n, banks, m):
                    return add_to_residual(n, banks, m, None, biased[n])

                nxt = close(["pw20", "pw21"], (YH, YL), y_ready, evacuate, Norm(lambda k: V("mlp_g1", k), x_free))
            nxt.left = gone()
            return nxt

        def in_slots(tasks, per):
            for i in range(0, len(tasks), per):
                slots.append(lambda group=tasks[i:i + per]: [f(*args) for f, *args in group])

        def even_stage(norm):
            scope = ExitStack()
            with scope:
                YBH = sb("yb_hi", [P, KD, S], F32R, scope=scope)
                YBL = sb("yb_lo", [P, KD, S], F32R, scope=scope)
                ya = sb("rg_y", [P, KD, S], scope=scope)
                ua = sb("rg_u", [P, 4, S], scope=scope)
                R = sb("rg_r", [P, 4, S], scope=scope)
                I = sb("rg_i", [P, 4, S], scope=scope)
                Q = sb("rg_t", [P, 4, S], scope=scope)
                xpad = sb("conv_in", [P, 4, S + 3], scope=scope)
                sc = sb("sc_acc", [P, 4, S], scope=scope)
                silu = [sb(f"even_silu{i}", [P, S], scope=scope) for i in range(2)]
                sqr = [sb(f"rg_sq{i}", [P, S], scope=scope) for i in range(1)]
                gw = sb("gate_w", [P, 8, P], scope=scope)
                coef = sb("rg_coef", [P, 2 * KD], scope=scope)
                sp1 = sb("sp_z", [P, 2 * KD], scope=scope)
                sp2 = sb("sp_w", [P, 2 * KD], scope=scope)
                sp3 = sb("sp_s", [P, 2 * KD], scope=scope)
                load_gw = Landing(sem("gate_w_landed"))
                x_ready = norm.x_ready
                got = {}

                def finish_norm():
                    h1 = []
                    for t in range(T):
                        m = dve.do(lambda e, t=t: e.scalar_tensor_tensor(
                            out=H[:, t, :], in0=H[:, t, :], scalar=norm.r(t), in1=gain_row[:, :],
                            op0=ALU.mult, op1=ALU.mult), [norm.r_ready, got["final_g"], got["turned"]])
                        for n in range(2):
                            h1.append(squares(H[:, t, n * 512:(n + 1) * 512],
                                              norm_stat[:, norm.at, 4 + n, t:t + 1], [m]))
                    got["h1"] = h1

                def second_root():
                    c4, c5, c6 = norm.col(4), norm.col(5), norm.col(6)
                    both = dve.do(lambda e: e.tensor_tensor(c6, c4, c5, ALU.add), got["h1"])
                    r2 = inverse_root(c6, c6, D, [both])
                    both = dve.do(lambda e: e.tensor_tensor(c4, c6, norm.col(2), ALU.mult), [r2])
                    sq = dve.do(lambda e: e.tensor_tensor(c5, c4, c4, ALU.mult), [both])
                    norm.row_ready = broadcast(c4, rrow[:, :], [both])
                    norm.row2_ready = broadcast(c5, rrow2[:, :], [sq])
                    got["row"] = load_gain_row("even_post", got["h1"])

                def load_gates(direction, g, after):
                    for which in range(2):
                        landed = load_gw.start(sp, gw[:, 4 * which:4 * which + 4, :],
                                               a["rg_gate_w_2"][0, direction, which, 4 * g:4 * g + 4]
                                               .rearrange("h i j -> i h j"), after)
                    got["gates"] = landed

                got["final_g"] = load_gain_row("final_g", [dve.last(), pool.last()])
                slots.insert(2, lambda: got.update(turned=pe.last()))
                slots.extend([finish_norm, second_root])

                def make_coef():
                    lam = V("lam", 0, 2 * KD)
                    m = act.do(lambda e: e.activation(sp1[:, :], lam, ACT.Abs), [vec_in])
                    m = act.do(lambda e: e.activation(sp1[:, :], sp1[:, :], ACT.Exp, scale=-1.0), [m])
                    m = dve.do(lambda e: e.tensor_scalar(sp2[:, :], sp1[:, :], 2.0, None, ALU.add), [m])
                    m = dve.do(lambda e: e.reciprocal(sp2[:, :], sp2[:, :]), [m])
                    m = dve.do(lambda e: e.tensor_tensor(sp1[:, :], sp1[:, :], sp2[:, :], ALU.mult), [m])
                    m = dve.do(lambda e: e.tensor_tensor(sp2[:, :], sp1[:, :], sp1[:, :], ALU.mult), [m])
                    m = dve.do(lambda e: e.memset(sp3[:, :], 1.0 / 19), [m])
                    for d in range(17, 0, -2):
                        m = dve.do(lambda e: e.tensor_tensor(sp3[:, :], sp3[:, :], sp2[:, :], ALU.mult), [m])
                        m = dve.do(lambda e, d=d: e.tensor_scalar(sp3[:, :], sp3[:, :], 1.0 / d, None, ALU.add), [m])
                    m = dve.do(lambda e: e.scalar_tensor_tensor(
                        out=sp3[:, :], in0=sp3[:, :], scalar=2.0, in1=sp1[:, :], op0=ALU.mult, op1=ALU.mult), [m])
                    m = dve.do(lambda e: e.tensor_scalar(sp2[:, :], lam, -1.0, 0.0, ALU.mult, ALU.max), [m])
                    m = dve.do(lambda e: e.tensor_tensor(sp3[:, :], sp3[:, :], sp2[:, :], ALU.add), [m])
                    got["coef"] = dve.do(lambda e: e.tensor_scalar(coef[:, :], sp3[:, :], -RG_C, None, ALU.mult), [m])

                ua_ready, ya_ready, yb_ready = [None] * KD, [None] * KD, [None] * KD
                state = {"pad_free": [], "ua_free": [], "rg_free": [], "gw_free": [], "sqr_free": []}

                def long_conv(g, banks, m):
                    edges = [dve.do(lambda e: e.memset(xpad[:, :, 0:2], 0.0), state["pad_free"]),
                             dve.do(lambda e: e.memset(xpad[:, :, S + 2:S + 3], 0.0), state["pad_free"])]
                    xs = [times_row(b, m, xpad[:, j, 2:2 + S], rrow[:, :], [norm.row_ready] + state["pad_free"])
                          for j, b in enumerate(banks)]
                    pad_free = []
                    for j in range(4):
                        k = g * 4 + j
                        d = dve.do(lambda e, j=j, k=k: e.tensor_scalar(
                            ua[:, j, :], xpad[:, j, 0:S], V("rg_w", k * RG_W), V("rg_b", k), ALU.mult, ALU.add),
                            [xs[j]] + edges + state["ua_free"])
                        for i in range(1, RG_W):
                            d = dve.do(lambda e, j=j, k=k, i=i: e.scalar_tensor_tensor(
                                out=ua[:, j, :], in0=xpad[:, j, i:i + S], scalar=V("rg_w", k * RG_W + i),
                                in1=ua[:, j, :], op0=ALU.mult, op1=ALU.add), [d])
                        ua_ready[k] = d
                        pad_free.append(d)
                    state["pad_free"] = pad_free

                gates, root = {}, {}

                def gate_task(direction, g, which, j):
                    dst, k, b = (R, I)[which], 4 * g + j, others()[j]
                    m = mm(bank[b][:, :], gw[:, 4 * which + j, :], ua[:, j, :], True, True,
                           [got["gates"], ua_ready[k]] + bank_free[b])
                    gates[which, j] = act.do(lambda e: e.activation(
                        dst[:, j, :], bank[b][:, :], ACT.Sigmoid,
                        bias=V("gate_b", (2 * direction + which) * KD + k)), [m] + state["rg_free"])
                    bank_free[b] = [gates[which, j]]
                    state["gw_free"] = [m]

                def decay_task(direction, g):
                    cf = [coef[:, direction * KD + 4 * g + j:direction * KD + 4 * g + j + 1] for j in range(4)]
                    th = [act.do(lambda e, j=j: e.activation(Q[:, j, :], R[:, j, :], ACT.Tanh, scale=cf[j]),
                                 [gates[0, j], got["coef"]] + state["rg_free"]) for j in range(4)]
                    state["ex"] = [act.do(lambda e, j=j: e.activation(R[:, j, :], R[:, j, :], ACT.Exp, scale=cf[j]),
                                          [th[j]]) for j in range(4)]
                    state["iu"] = [dve.do(lambda e, j=j: e.tensor_tensor(I[:, j, :], I[:, j, :], ua[:, j, :], ALU.mult),
                                          [gates[1, j]]) for j in range(4)]
                    state["ua_free"] = state["gw_free"] + state["iu"]

                def root_task(j):
                    s = sqr[0]
                    d = dve.do(lambda e: e.tensor_tensor(s[:, :], R[:, j, :], R[:, j, :], ALU.mult),
                               [state["ex"][j]] + state["sqr_free"])
                    d = dve.do(lambda e: e.scalar_tensor_tensor(
                        out=Q[:, j, :], in0=s[:, :], scalar=1.0, in1=Q[:, j, :], op0=ALU.add, op1=ALU.mult), [d])
                    state["sqr_free"] = [d]
                    root[j] = act.do(lambda e: e.activation(Q[:, j, :], Q[:, j, :], ACT.Sqrt, scale=-1.0), [d])

                def scan_task(direction, g, j):
                    k = 4 * g + j
                    if j == 0:
                        state["rg_free"] = []
                    d = dve.do(lambda e: e.tensor_tensor(I[:, j, :], I[:, j, :], Q[:, j, :], ALU.mult),
                               [root[j], state["iu"][j]])
                    if direction == 0:
                        d = dve.do(lambda e: e.tensor_tensor_scan(
                            ya[:, k, :], R[:, j, :], I[:, j, :], 0.0, ALU.mult, ALU.add), [d])
                    else:
                        s = dve.do(lambda e: e.tensor_tensor_scan(
                            Q[:, j, ::-1], R[:, j, ::-1], I[:, j, ::-1], 0.0, ALU.mult, ALU.add), [d])
                        d = dve.do(lambda e: e.tensor_tensor(ya[:, k, :], ya[:, k, :], Q[:, j, :], ALU.add),
                                   [s, ya_ready[k]])
                    ya_ready[k] = d
                    state["rg_free"].append(d)

                def lru(direction, g):
                    in_slots([(gate_task, direction, g, w, j) for w in range(2) for j in range(4)], 2)
                    in_slots([(decay_task, direction, g)], 1)
                    in_slots([(root_task, j) for j in range(4)], 2)
                    in_slots([(scan_task, direction, g, j) for j in range(4)], 1)
                    slots.append(lambda: load_gates(*following[direction, g], state["gw_free"])
                                 if (direction, g) in following else None)

                following = {(0, 0): (1, 0), (1, 0): (0, 1), (0, 1): (1, 1)}
                silu_free = [[], []]

                def silu_of(banks, m, j):
                    s, i = silu[j % 2], j % 2
                    z = times_row(banks[j], m, s[:, :], rrow[:, :], silu_free[i])
                    return act.do(lambda e: e.activation(s[:, :], s[:, :], ACT.Silu), [z])

                sc_free = []
                for g in range(2):
                    banks = four()
                    m = product(f"xa{g}", 0, banks, X, x_ready, True)
                    all_slots()
                    if g == 0:
                        settle(norm.left, act, dve, sp)
                        load_gates(0, 0, [])
                    long_conv(g, banks, m)

                    slots.append(make_coef if g == 0 else None)
                    slots.extend([None] * 3)
                    lru(0, g)
                    lru(1, g)
                    banks = four()
                    m = product(f"gc{g}", 0, banks, X, x_ready, True)
                    edges = [dve.do(lambda e: e.memset(xpad[:, :, 0:1], 0.0), state["pad_free"]),
                             dve.do(lambda e: e.memset(xpad[:, :, S + 1:S + 2], 0.0), state["pad_free"])]
                    cs = [times_row(b, m, xpad[:, j, 1:1 + S], rrow2[:, :], [norm.row2_ready] + state["pad_free"])
                          for j, b in enumerate(banks)]
                    banks = four()
                    m = product(f"xb{g}", 0, banks, X, x_ready, True)
                    acc, pad_free = [], []
                    for j, b in enumerate(banks):
                        k = 4 * g + j
                        d = dve.do(lambda e, j=j, b=b: e.tensor_tensor(
                            xpad[:, j, 1:1 + S], bank[b][:, :], xpad[:, j, 1:1 + S], ALU.mult), [m, cs[j]])
                        bank_free[b] = [d]
                        acc.append(d)
                    for j in range(4):
                        k = 4 * g + j
                        d = dve.do(lambda e, j=j, k=k: e.tensor_scalar(
                            sc[:, j, :], xpad[:, j, 0:S], V("sc_w", k * SC_W), None, ALU.mult),
                            [acc[j]] + edges + sc_free)
                        for i in range(1, SC_W):
                            d = dve.do(lambda e, j=j, k=k, i=i: e.scalar_tensor_tensor(
                                out=sc[:, j, :], in0=xpad[:, j, i:i + S], scalar=V("sc_w", k * SC_W + i),
                                in1=sc[:, j, :], op0=ALU.mult, op1=ALU.add), [d])
                        pad_free.append(d)
                        acc[j] = d
                    state["pad_free"] = pad_free
                    banks = four()
                    m = product(f"gb{g}", 0, banks, X, x_ready, True)
                    for j, b in enumerate(banks):
                        d = dve.do(lambda e, j=j, b=b: e.tensor_tensor(
                            sc[:, j, :], bank[b][:, :], sc[:, j, :], ALU.mult), [m, acc[j]])
                        bank_free[b] = [d]
                        acc[j] = pool.do(lambda e, j=j: e.tensor_tensor(
                            sc[:, j, :], sc[:, j, :], rrow[:, :], ALU.mult), [d])
                    banks = four()
                    m = product(f"zb{g}", 0, banks, X, x_ready, True)
                    sc_free = []
                    for j in range(4):
                        k = 4 * g + j
                        s = silu_of(banks, m, j)
                        d = dve.do(lambda e, j=j: e.tensor_tensor(sc[:, j, :], sc[:, j, :], silu[j % 2][:, :], ALU.mult),
                                   [s, acc[j]])
                        silu_free[j % 2] = [d]
                        yb_ready[k] = split_sbuf(sc[:, j, :], YBH[:, k, :], YBL[:, k, :], [d])
                        sc_free += yb_ready[k]
                    if g == 0:
                        all_slots()

                za_marks = []
                for g in range(2):
                    banks = four()
                    m = product(f"za{g}", 0, banks, X, x_ready, True)
                    all_slots()
                    for j in range(4):
                        k = 4 * g + j
                        s = silu_of(banks, m, j)
                        d = dve.do(lambda e, j=j, k=k: e.tensor_tensor(
                            ya[:, k, :], ya[:, k, :], silu[j % 2][:, :], ALU.mult), [s, ya_ready[k]])
                        silu_free[j % 2] = [d]
                        za_marks.append(d)
                yax = [split_sbuf(ya[:, k, :], XH[:, k, :], XL[:, k, :], [za_marks[k], m]) for k in range(KD)]
                post = Post([R, I], norm.at, got["row"], state["rg_free"])
                b0 = four()
                product("eout_b0", 0, b0, (YBH, YBL), yb_ready, False, True, False)
                m0 = product("eout_a0", 0, b0, X, yax, False, False, True)
                slots.extend([lambda t=t: post.take(0, t, b0, m0) for t in range(T)])
                b1 = four()
                m1 = product("eout_a1", 0, b1, X, yax, False, True, False)
                nxt = Norm(lambda k: V("odd_g", k), [m1])
                m1 = product("eout_b1", 0, b1, (YBH, YBL), yb_ready, False, False, True)
                all_slots()
                for t in range(T):
                    post.take(1, t, b1, m1)
                post.root()
                for n in range(2):
                    marks = [[post.add(t, n)] for t in range(T)]
                    nxt.half(n, marks)
                    if n == 0:
                        all_slots()
            nxt.left = gone()
            return nxt

        class Post:

            def __init__(self, buffers, at, gain_in, free):
                self.buf, self.at, self.gain_in, self.free = buffers, at, gain_in, free
                self.sums, self.taken = [], {}

            def take(self, n, t, banks, m):
                b = banks[t]
                s = squares(bank[b][:, :], norm_stat[:, self.at, 4 + n, t:t + 1], [m])
                d = dve.do(lambda e: e.tensor_tensor(self.buf[n][:, t, :], bank[b][:, :],
                                                     gain_row[:, n * 512:(n + 1) * 512], ALU.mult),
                           [s, self.gain_in] + self.free)
                bank_free[b] = [d]
                self.sums.append(s)
                self.taken[n, t] = d

            def root(self):
                c4, c5, c6 = (norm_stat[:, self.at, c, :] for c in (4, 5, 6))
                both = dve.do(lambda e: e.tensor_tensor(c6, c4, c5, ALU.add), self.sums)
                self.ready = inverse_root(c6, c6, D, [both])

            def add(self, t, n):
                hh = H[:, t, n * 512:(n + 1) * 512]
                z, r = self.buf[n][:, t, :], norm_stat[:, self.at, 6, t:t + 1]
                if t == T - 1:
                    m = act.do(lambda e: e.activation(z, z, ACT.Copy, scale=r), [self.ready, self.taken[n, t]])
                    return pool.do(lambda e: e.tensor_tensor(hh, hh, z, ALU.add), [m])
                return dve.do(lambda e: e.scalar_tensor_tensor(
                    out=hh, in0=z, scalar=r, in1=hh,
                    op0=ALU.mult, op1=ALU.add), [self.ready, self.taken[n, t]])

        def odd_stage(norm):
            scope = ExitStack()
            with scope:
                qT = sb("gla_q", [P, GLA_HEADS, S], scope=scope)
                kT = sb("gla_k", [P, GLA_HEADS, S], scope=scope)
                v = sb("gla_v", [P, T, D], scope=scope)
                r = sb("gla_r", [P, T, D], scope=scope)
                G = sb("gla_g", [P, 2, GLA_HEADS, S], scope=scope)
                e1 = [[sb(f"gla_e1{d}{i}", [P, S], scope=scope) for d in range(2)] for i in range(2)]
                e2 = [[sb(f"gla_e2{d}{i}", [P, S], scope=scope) for d in range(2)] for i in range(2)]
                kst = [sb(f"gla_kst{d}", [P, T, P], scope=scope) for d in range(2)]
                stm = [sb(f"gla_stm{d}", [P, T, P], scope=scope) for d in range(2)]
                stt = sb("gla_state", [P, 2, NCH, GLA_DV], scope=scope)
                dec = sb("gla_decay", [P, 2, 2, NCH], scope=scope)
                ssq = sb("gla_ssq", [P, GLA_HEADS, T], scope=scope)
                head_g = sb("gla_head_gain", [P, GLA_DV], scope=scope)
                lrT = kst[0][0:2 * GLA_RANK, :, :].rearrange("p t n -> p (t n)")
                wg = stt[0:2 * GLA_RANK, :, 0:2, :]
                load_wg, load_head = Landing(sem("wg_landed")), Landing(sem("head_gain_landed"))
                masks = [C("fwd_mask"), C("bwd_mask")]
                keeps = [C("fwd_keep"), C("bwd_keep")]
                x_ready = norm.x_ready
                got, g_ready, q_ready, k_ready, v_ready, r_ready = {}, {}, [], [], [], []
                slots.append(norm.row)

                def feature(name, dst):
                    banks = four()
                    m = product(name, 0, banks, X, x_ready, True)
                    return banks, m, lambda: [times_row(b, m, dst[:, j, :], rrow[:, :], [norm.row_ready])
                                              for j, b in enumerate(banks)]

                _, _, take = feature("gq", qT)
                all_slots()
                settle(norm.left, act, dve, pool, sp)
                q_ready += take()
                head_in = load_head.start(sp, head_g[:, :], a["gla_norm_g"].partition_broadcast(P))
                row_in = load_gain_row("odd_post", [dve.last()])
                zeroed = dve.do(lambda e: e.memset(wg, 0.0))
                for d in range(2):
                    wg_in = load_wg.start(sp, stt[d * GLA_RANK:(d + 1) * GLA_RANK, d, 0:2, :],
                                          a["gla_w_gate_lr_2"][0, d].rearrange("r (c n) -> r c n", n=GLA_DV), [zeroed])

                banks = four()
                m = product("lr", 0, banks[:1], X, x_ready, True)
                b = banks[0]
                lr_ready = dve.do(lambda e: e.tensor_tensor(
                    lrT, bank[b][0:2 * GLA_RANK, :], rrow[0:2 * GLA_RANK, :], ALU.mult), [m, norm.row_ready])
                bank_free[b] = [lr_ready]
                act.queue.append(lambda e: e.preload_act_table_set("natural_log_exp_and_others"))
                z_done = [[], []]
                tmp = [e1[0][0], e1[0][1]]

                def z_task(h, d):
                    b, i, z = others()[(2 * h + d) % 4], d, G[:, d, h, :]
                    wz = stt[0:2 * GLA_RANK, d, h // 2, (h % 2) * P:(h % 2 + 1) * P]
                    m = mm(bank[b][:, :], wz, lrT, True, True, [wg_in, lr_ready] + bank_free[b])
                    m1 = dve.do(lambda e: e.tensor_scalar(
                        z, bank[b][:, :], V("gla_b", d * GLA_HEADS + h), None, ALU.add), [m])
                    bank_free[b] = [m1]
                    m2 = act.do(lambda e: e.activation(tmp[i][:, :], z, ACT.Abs), [m1] + z_done[i])
                    m2 = act.do(lambda e: e.activation(tmp[i][:, :], tmp[i][:, :], ACT.Exp, scale=-1.0), [m2])
                    m2 = act.do(lambda e: e.activation(tmp[i][:, :], tmp[i][:, :], ACT.Ln, bias=1.0), [m2])
                    m3 = dve.do(lambda e: e.scalar_tensor_tensor(
                        out=z, in0=z, scalar=0.0, in1=tmp[i][:, :], op0=ALU.min, op1=ALU.subtract), [m2])
                    z_done[i] = [m3]
                    g_ready[d, h] = dve.do(lambda e: e.tensor_scalar(z, z, 1.0 / GLA_NORM, None, ALU.mult), [m3])
                    got["z"] = [m, m3]

                def chunks(ap):
                    return ap.rearrange("p (c n) -> p c n", n=CHUNK)

                dk_scale = GLA_DK ** -0.5
                free = {}
                ready = {}
                y_marks = [[] for _ in range(T)]

                def decays(h, d):
                    i, g = h % 2, G[:, d, h, :]
                    a1, a2 = e1[i][d], e2[i][d]
                    before = free.get(("e", i, d), got["z"])
                    sl = (lambda x: x) if d == 0 else (lambda x: x[:, ::-1])
                    at = CHUNK - 1 if d == 0 else 0
                    m = dve.do(lambda e: e.tensor_tensor_scan(sl(g), sl(keeps[d]), sl(g), 0.0, ALU.mult, ALU.add),
                               [g_ready[d, h], con2_in])
                    x1 = act.do(lambda e: e.activation(a1[:, :], g, ACT.Exp), [m] + before)
                    x2 = act.do(lambda e: e.activation(a2[:, :], g, ACT.Exp, scale=-1.0), [m] + before)
                    ready["dec", h, d] = dve.do(lambda e: e.tensor_copy(dec[:, i, d, :], chunks(a1[:, :])[:, :, at]),
                                                [x1] + before)
                    total = dve.do(lambda e: e.tensor_copy(tot[:, d, :], chunks(g)[:, :, at]), [m] + free.get(("tot", d), []))
                    df = dve.do(lambda e: e.tensor_tensor(
                        chunks(g), tot[:, d, :].unsqueeze(2).broadcast_to([P, NCH, CHUNK]), chunks(g), ALU.subtract),
                        [total, x1, x2])
                    free["tot", d] = [df]
                    x3 = act.do(lambda e: e.activation(g, g, ACT.Exp), [df])
                    ready["q", h, d] = dve.do(lambda e: e.scalar_tensor_tensor(
                        out=a1[:, :], in0=qT[:, h, :], scalar=dk_scale, in1=a1[:, :], op0=ALU.mult, op1=ALU.mult),
                        [ready["dec", h, d], q_ready[h]])
                    ready["k", h, d] = dve.do(lambda e: e.tensor_tensor(a2[:, :], kT[:, h, :], a2[:, :], ALU.mult),
                                              [x2, k_ready[h]])
                    ready["s", h, d] = dve.do(lambda e: e.tensor_tensor(g, kT[:, h, :], g, ALU.mult), [x3])

                tot = sb("gla_total", [P, 2, NCH], scope=scope)

                def intra(h, d):
                    i, b, b2 = h % 2, 4 + d, 6 + d
                    for t in range(T):
                        m = mm(bank[b][:, t * P:(t + 1) * P], e2[i][d][:, t * P:(t + 1) * P],
                               e1[i][d][:, t * P:(t + 1) * P], True, True,
                               [ready["q", h, d], ready["k", h, d]] + bank_free[b])
                    for t in range(T):
                        m2 = turn(bank[b2][:, t * P:(t + 1) * P], G[:, d, h, t * P:(t + 1) * P],
                                  [ready["s", h, d]] + bank_free[b2])
                    ready["stm", d] = dve.do(lambda e: e.tensor_tensor(
                        stm[d][:, :, :], bank[b][:, :].rearrange("p (t n) -> p t n", n=P),
                        masks[d].unsqueeze(1).broadcast_to([P, T, P]), ALU.mult), [m, con2_in] + free.get("out", []))
                    bank_free[b] = [ready["stm", d]]
                    ready["kst", d] = act.do(lambda e: e.activation(
                        kst[d][:, :, :].rearrange("p t n -> p (t n)"), bank[b2][:, :], ACT.Copy),
                        [m2] + free.get("out", got["z"]))
                    bank_free[b2] = [ready["kst", d]]

                def states(h, d, quad):
                    i = h % 2
                    order = list(range(NCH)) if d == 0 else list(range(NCH - 1, -1, -1))
                    four_n = [n for n in range(4 * quad, 4 * quad + 4) if n < NCH - 1]
                    pair, place = (4, 5) if (quad + d) % 2 == 0 else (6, 7), {}
                    for n in four_n:
                        c = order[n]
                        b, col, p0 = pair[n % 2], (n // 2) % 2 * GLA_DV, (c % 2) * CHUNK
                        place[n] = bank[b][:, col:col + GLA_DV]
                        m = mm(place[n], kst[d][p0:p0 + CHUNK, c // 2, :],
                               v[p0:p0 + CHUNK, c // 2, h * GLA_DV:(h + 1) * GLA_DV], True, True,
                               [ready["kst", d]] + v_ready[(h // 2) * T:(h // 2 + 1) * T] + bank_free[b])
                    reads = []
                    for n in four_n:
                        dst, c = stt[:, d, order[n + 1], :], order[n]
                        after = [m] + free.get("out", got["z"])
                        if n == 0:
                            s = dve.do(lambda e, src=place[n], dst=dst: e.tensor_copy(dst, src), after)
                        else:
                            s = dve.do(lambda e, src=place[n], dst=dst, c=c: e.scalar_tensor_tensor(
                                out=dst, in0=stt[:, d, c, :], scalar=dec[:, i, d, c:c + 1], in1=src,
                                op0=ALU.mult, op1=ALU.add), after + [ready["st", d, c], ready["dec", h, d]])
                        ready["st", d, order[n + 1]] = s
                        reads.append(s)
                    for b in pair:
                        bank_free[b] = list(reads)

                def outputs(h, t):
                    i, b = h % 2, 4 + t
                    o, vv = bank[b][:, 0:GLA_DV], v[:, t, h * GLA_DV:(h + 1) * GLA_DV]
                    mm(o, stm[0][:, t, :], vv, True, False, [ready["stm", 0]] + bank_free[b])
                    for d in range(2):
                        for c in (2 * t, 2 * t + 1):
                            if c != (0 if d == 0 else NCH - 1):
                                p0 = (c % 2) * CHUNK
                                mm(bank[b][p0:p0 + CHUNK, 0:GLA_DV], e1[i][d][:, c * CHUNK:(c + 1) * CHUNK],
                                   stt[:, d, c, :], False, False, [ready["st", d, c]])
                    m = mm(o, stm[1][:, t, :], vv, False, True, [ready["stm", 1]])
                    ready["out", t] = m
                    if t == T - 1:
                        free["out"] = free["e", i, 0] = free["e", i, 1] = [m]

                def head_norm(h):
                    ss = [squares(bank[4 + t][:, 0:GLA_DV], ssq[:, h, t:t + 1], [ready["out", t]]) for t in range(T)]
                    ready["rstd"] = inverse_root(ssq[:, h, :], ssq[:, h, :], GLA_DV, ss)

                def head_out(h):
                    for t in range(T):
                        b, rr = 4 + t, r[:, t, h * GLA_DV:(h + 1) * GLA_DV]
                        m = dve.do(lambda e, rr=rr: e.tensor_tensor(rr, rr, head_g[:, :], ALU.mult),
                                   [head_in, r_ready[(h // 2) * T + t]])
                        m = dve.do(lambda e, b=b, t=t, rr=rr: e.scalar_tensor_tensor(
                            out=rr, in0=bank[b][:, 0:GLA_DV], scalar=ssq[:, h, t:t + 1], in1=rr,
                            op0=ALU.mult, op1=ALU.mult), [m, ready["rstd"]])
                        bank_free[b] = [m]
                        y_marks[t].append(m)

                def tokens(name, n, dst, func, marks):
                    banks = four()
                    m = product(name, 0, banks, X, x_ready, False)
                    for t, b in enumerate(banks):
                        d = act.do(lambda e, t=t, b=b: e.activation(
                            dst[:, t, n * 512:(n + 1) * 512], bank[b][:, :], func, scale=norm.r(t)), [m])
                        bank_free[b] = [d]
                        marks.append(d)
                    return m

                zs = [(z_task, h, d) for h in range(GLA_HEADS) for d in range(2)]
                slots.append(None)
                in_slots(zs, 1)
                _, _, take = feature("gk", kT)
                k_ready += take()
                tokens("gr0", 0, r, ACT.Silu, r_ready)
                all_slots()
                act.queue.append(lambda e: e.preload_act_table_set("natural_log_exp_and_others"))

                product_banks([0, 1, 2, 3])
                core = {h: ([(intra, h, 0), (intra, h, 1)]
                            + [(states, h, d, quad) for quad in range(2) for d in range(2)]
                            + [(outputs, h, t) for t in range(T)]) for h in range(GLA_HEADS)}
                pre = {h: [(decays, h, d) for d in range(2)] for h in range(GLA_HEADS)}
                end = {h: [(head_norm, h), (head_out, h)] for h in range(GLA_HEADS)}
                slots.extend([None, None])
                in_slots(pre[0] + core[0][:2], 1)
                tokens("gv0", 0, v, ACT.Copy, v_ready)
                all_slots()
                in_slots(core[0][2:6] + pre[1] + core[0][6:] + end[0] + core[1][:2], 2)
                tokens("gv1", 1, v, ACT.Copy, v_ready)
                all_slots()
                in_slots(core[1][2:6] + pre[2] + core[1][6:] + end[1] + core[2][:6], 3)
                x_free = [tokens("gr1", 1, r, ACT.Silu, r_ready)]
                all_slots()
                y_ready = []

                def turn_y(k):
                    turn_and_split(r, k, [[y_marks[t][k // 2]] for t in range(T)], None, x_free, y_ready)

                for k in range(4):
                    turn_y(k)
                in_slots(pre[3] + core[2][6:] + end[2] + [(turn_y, 4), (turn_y, 5)], 2)
                in_slots(core[3] + end[3] + [(turn_y, 6), (turn_y, 7)], 2)
                b0 = four()
                m0 = product("oout0", 0, b0, X, y_ready, False)
                all_slots()
                product_banks(list(range(8)), 4)
                post = Post([qT, kT], norm.at, row_in, [dve.last()])
                slots.extend([lambda t=t: post.take(0, t, b0, m0) for t in range(T)])
                b1 = four()
                m1 = product("oout1", 0, b1, X, y_ready, False)
                all_slots()
                for t in range(T):
                    post.take(1, t, b1, m1)
                post.root()
                out_landed = Landing(sem("out_landed"))
                for t in (3, 0, 1, 2):
                    marks = [post.add(t, n) for n in range(2)]
                    out_landed.start(sp, out[0, t * P:(t + 1) * P, :], H[:, t, :], marks)
                sp.wait((out_landed.sem, out_landed.count))

        queue_loads(RAW)
        con2_in = load_con2.start(sp, con[:, 2 * P:], a["constants"][:, 2 * P:])
        norm = start_norm()
        norm = dsa_stage(norm)
        norm = mlp_stage(0, norm, lambda k: V("mix_g1", k))
        norm = conv_stage(norm)
        norm = mlp_stage(1, norm, lambda k: final_even[:, k:k + 1])
        norm = even_stage(norm)
        odd_stage(norm)
        assert state["used"] == len(stream)

        block = ctx.enter_context(nc.Block())

        @block.sync
        def _(e):
            sp.play(e)

        @block.scalar
        def _(e):
            act.play(e)

        @block.gpsimd
        def _(e):
            pool.play(e)

        @block.vector
        def _(e):
            dve.play(e)

        @block.tensor
        def _(e):
            pe.play(e)


def constants():
    i = np.arange(P)
    same = (i[:, None] // CHUNK) == (i[None, :] // CHUNK)
    parts = {
        "ident": np.eye(P),
        "mean": np.full((P, P), 1.0 / D),
        "fwd_mask": same & (i[None, :] >= i[:, None]),
        "bwd_mask": same & (i[None, :] <= i[:, None]),
        "causal": np.where(i[None, :] <= i[:, None], 0.0, -BIG),
        "fwd_keep": np.tile((np.arange(S) % CHUNK != 0)[None], (P, 1)),
        "bwd_keep": np.tile((np.arange(S) % CHUNK != CHUNK - 1)[None], (P, 1)),
    }
    return np.concatenate([parts[n].astype(np.float32) for n, _ in CON_SIZES], axis=1)


def columns(x):
    return np.ascontiguousarray(np.asarray(x).reshape(-1, P).T)


def taps(w):
    w = np.asarray(w)
    return np.ascontiguousarray(w.reshape(w.shape[0], -1, P).transpose(2, 1, 0)).reshape(P, -1)


def kernel(**inputs):
    import concourse.bacc as bacc
    from concourse.bass_utils import run_bass_kernel_spmd

    x = {k: np.asarray(v) for k, v in inputs.items()}
    vectors = {
        "mix_g0": columns(x["norm_mix_g"][0]), "mix_g1": columns(x["norm_mix_g"][1]),
        "mlp_g0": columns(x["norm_mlp_g"][0]), "mlp_g1": columns(x["norm_mlp_g"][1]),
        "pw1_b": columns(x["conv_b_pw1"][0]), "dw_w": taps(x["conv_w_dw"][0]),
        "dw_b": columns(x["conv_b_dw"][0]), "ln_g": columns(x["conv_ln_g"][0]),
        "ln_b": columns(x["conv_ln_b"][0]),
        "idx_g": columns(np.concatenate([x["dsa_idx_k_g"][0]] * 2)),
        "idx_b": columns(np.concatenate([x["dsa_idx_k_b"][0]] * 2)),
        "even_g": columns(x["even_norm_pre_2"][0]), "rg_w": taps(x["rg_conv_w_2"][0]),
        "rg_b": columns(x["rg_conv_b_2"][0]), "gate_b": columns(x["rg_gate_b_2"][0]),
        "lam": columns(x["rg_lambda_2"][0]), "sc_w": taps(x["sc_conv_w_2"][0]),
        "final_g": columns(x["final_g"]),
        "odd_g": columns(x["odd_norm_pre_2"][0]), "gla_b": columns(x["gla_b_gate_2"][0]),
    }
    arrays = {
        "x": x["x"],
        "vectors": np.concatenate([vectors[n] for n, _ in VEC_SIZES], axis=1),
        "constants": constants(),
        "b_pw2": x["conv_b_pw2"][0], "final_g": x["final_g"], "even_post": x["even_norm_post_2"][0],
        "odd_post": x["odd_norm_post_2"][0], "gla_norm_g": x["gla_norm_g_2"][0],
    }
    for name in ("dsa_w_in", "dsa_w_out", "mlp_w1", "mlp_w2", "conv_w_pw1", "conv_w_pw2", "even_w_in_2",
                 "even_w_out_2", "rg_gate_w_2", "odd_w_in_2", "odd_w_out_2", "gla_w_gate_lr_2"):
        arrays[name] = x[name]
    arrays = {k: np.ascontiguousarray(v) for k, v in arrays.items()}

    nc = bacc.Bacc("TRN2", target_bir_lowering=False, num_devices=1,
                   dynamic_dma_scratch_size=1024)
    a = {k: nc.dram_tensor(f"in_{k}", v.shape, mybir.dt.from_np(v.dtype), kind="ExternalInput").ap()
         for k, v in arrays.items()}
    out = nc.dram_tensor("out", (1, S, D), F32, kind="ExternalOutput").ap()
    build(nc, a, out)
    result = run_bass_kernel_spmd(nc, [{f"in_{k}": v for k, v in arrays.items()}], core_ids=[0])
    return result.results[0]["out"]
```

```python
from contextlib import ExitStack

import numpy as np

import concourse.bass as bass
from concourse import mybir

F32 = mybir.dt.float32
F32R = mybir.dt.float32r
ALU = mybir.AluOpType
ACT = mybir.ActivationFunctionType

P = 128
S = 512
T = S // P
D = 1024
KD = D // P
FF = 4 * D
EPS = 1e-6
BIG = 1e30
CAUSAL_FILL = -3.0e38
TAKEN = -3.4e38
HEADS = 8
IDX_DIM = 64
TOPK = min(256, S // 4)
CONV_W = 31
RG_W = 4
SC_W = 3
RG_C = 8.0
GLA_HEADS = 4
GLA_DK = 128
GLA_DV = 256
GLA_RANK = 16
CHUNK = 64
NCH = S // CHUNK
GLA_NORM = 16.0

VEC_SIZES = [
    ("mix_g0", KD), ("mlp_g0", KD), ("mix_g1", KD), ("mlp_g1", KD), ("pw1_b", 2 * KD),
    ("dw_w", KD * CONV_W), ("dw_b", KD), ("ln_g", KD), ("ln_b", KD), ("idx_g", 1), ("idx_b", 1),
    ("even_g", KD), ("rg_w", KD * RG_W), ("rg_b", KD), ("gate_b", 4 * KD), ("lam", 2 * KD),
    ("sc_w", KD * SC_W), ("odd_g", KD), ("final_g", KD), ("gla_b", 2 * GLA_HEADS),
]
VEC = {}
_at = 0
for _name, _n in VEC_SIZES:
    VEC[_name] = (_at, _n)
    _at += _n
NVEC = _at

CON_SIZES = [("ident", P), ("mean", P), ("fwd_mask", P), ("bwd_mask", P), ("causal", P),
             ("fwd_keep", S), ("bwd_keep", S)]
CON = {}
_at = 0
for _name, _n in CON_SIZES:
    CON[_name] = (_at, _n)
    _at += _n
NCON = _at

RAW = 4
RING = 4
SLOT = 1024
AHEAD = 4


class Lane:

    def __init__(self, name, sem):
        self.name, self.sem, self.count = name, sem, 0
        self.queue, self.waited = [], {}

    def wait(self, *marks):
        for m in marks:
            if m is None:
                continue
            sem, value = m
            if self.waited.get(id(sem), 0) < value:
                self.waited[id(sem)] = value
                self.queue.append(lambda e, sem=sem, value=value: e.wait_ge(sem, value))

    def do(self, make, after=(), signal=True):
        self.wait(*after)
        if not signal:
            self.queue.append(make)
            return None
        self.count += 1
        self.queue.append(lambda e: make(e).then_inc(self.sem, 1))
        return (self.sem, self.count)

    def last(self):
        return (self.sem, self.count) if self.count else None

    def play(self, engine):
        for step in self.queue:
            step(engine)


class Landing:

    def __init__(self, sem):
        self.sem, self.count = sem, 0

    def start(self, lane, out, in_, after=()):
        lane.wait(*after)
        self.count += 16
        sem = self.sem
        lane.queue.append(lambda e: e.dma_start(out, in_).then_inc(sem, 16))
        return (self.sem, self.count)


def build(nc, a, out):
    ctx = ExitStack()
    with ctx:
        def sem(name):
            return ctx.enter_context(nc.semaphore(name))

        def sb(name, shape, dt=F32, scope=ctx):
            return scope.enter_context(nc.sbuf_tensor(name, shape, dt))

        pe, act = Lane("pe", sem("pe_done")), Lane("act", sem("act_done"))
        dve, pool = Lane("dve", sem("dve_done")), Lane("pool", sem("pool_done"))
        sp = Lane("sp", None)

        H = sb("residual", [P, T, D])
        XH = sb("x_hi", [P, KD, S], F32R)
        XL = sb("x_lo", [P, KD, S], F32R)
        raw = [sb(f"w_raw{i}", [P, SLOT]) for i in range(RAW)]
        WH = [sb(f"w_hi{i}", [P, SLOT], F32R) for i in range(RING)]
        WL = [sb(f"w_lo{i}", [P, SLOT], F32R) for i in range(RING)]
        vec = sb("vectors", [P, NVEC])
        con = sb("constants", [P, NCON])
        gain_row = sb("gain_row", [P, D])
        norm_stat = sb("norm_stats", [P, 8, 8, T])
        rrow = sb("rstd_row", [P, S])
        rrow2 = sb("rstd_row_squared", [P, S])
        spare = sb("spare", [P, T, P])
        epsc = sb("eps_col", [P, 1])
        bank = [ctx.enter_context(nc.psum_tensor(f"bank{i}", [P, 512], F32)) for i in range(8)]
        bank_free = [[] for _ in range(8)]

        def V(name, i=0, n=1):
            at = VEC[name][0] + i
            return vec[:, at:at + n]

        def C(name):
            at, n = CON[name]
            return con[:, at:at + n]

        ident, mean_ones = C("ident"), C("mean")

        load_vec = Landing(sem("vec_landed"))
        load_x = [Landing(sem(f"x_landed{q}")) for q in range(4)]
        load_row = Landing(sem("gain_row_landed"))
        load_raw = [Landing(sem(f"raw_landed{i}")) for i in range(RAW)]

        load_con, load_con2 = Landing(sem("con_landed")), Landing(sem("con2_landed"))
        con_in = load_con.start(sp, con[:, 0:2 * P], a["constants"][:, 0:2 * P])
        x_src = a["x"].rearrange("b (t p) d -> p (b t) d", p=P)
        x_in = []

        def load_x_quarter():
            q = len(x_in)
            at = slice(q * D // 4, (q + 1) * D // 4)
            x_in.append(load_x[q].start(sp, H[:, :, at], x_src[:, :, at]))

        load_x_quarter()
        vec_in = load_vec.start(sp, vec[:, :], a["vectors"])
        eps_set = dve.do(lambda e: e.memset(epsc[:, :], EPS))

        def load_gain_row(name, after):
            return load_row.start(sp, gain_row[:, :], a[name].partition_broadcast(P), after)

        def units_of(name, src, cols, krows, per=None):
            ncols = sum(n for _, n in cols)
            per = per or SLOT // ncols
            src = src.rearrange("(k p) n -> p k n", p=P)
            return [{"name": name, "per": per, "cols": ncols,
                     "src": [src[:, k:k + per, c:c + n] for c, n in cols]}
                    for k in range(krows[0], krows[1], per)]

        dsa_in, dsa_out = a["dsa_w_in"][0], a["dsa_w_out"][0]
        stream = []
        stream += units_of("idx_narrow", dsa_in, [(3 * D + HEADS * IDX_DIM, IDX_DIM + HEADS)], (0, KD), KD)
        for name, c in (("qi", 3 * D), ("v0", 2 * D), ("v1", 2 * D + 512), ("q0", 0), ("k0", D), ("q1", 512),
                        ("k1", D + 512)):
            stream += units_of(name, dsa_in, [(c, 512)], (0, KD))
        for n in range(2):
            stream += units_of(f"dsa_out{n}", dsa_out, [(n * 512, 512)], (0, KD))

        def mlp_units(layer):
            got = []
            for half in range(2):
                for g in range(4):
                    got += units_of(f"up{layer}{half}{g}", a["mlp_w1"][layer],
                                    [(half * (FF // 2) + g * 512, 512)], (0, KD))
                for n in range(2):
                    got += units_of(f"down{layer}{half}{n}", a["mlp_w2"][layer], [(n * 512, 512)],
                                    (half * 16, half * 16 + 16))
            return got

        stream += mlp_units(0)
        for g in range(KD):
            stream += units_of(f"pw1{g}", a["conv_w_pw1"][0], [(g * P, P), (D + g * P, P)], (0, KD))
        for n in range(2):
            stream += units_of(f"pw2{n}", a["conv_w_pw2"][0], [(n * 512, 512)], (0, KD))
        stream += mlp_units(1)
        even_in, even_out = a["even_w_in_2"][0], a["even_w_out_2"][0]
        EVEN_ORDER = [("xa0", 0), ("gc0", 4 * D), ("xb0", 2 * D), ("gb0", 3 * D), ("zb0", 5 * D),
                      ("xa1", 512), ("gc1", 4 * D + 512), ("xb1", 2 * D + 512), ("gb1", 3 * D + 512),
                      ("zb1", 5 * D + 512), ("za0", D), ("za1", D + 512)]
        for name, c in EVEN_ORDER:
            stream += units_of(name, even_in, [(c, 512)], (0, KD))
        for name, n, k in (("eout_b0", 0, KD), ("eout_a0", 0, 0), ("eout_a1", 1, 0), ("eout_b1", 1, KD)):
            stream += units_of(name, even_out, [(n * 512, 512)], (k, k + KD))
        odd_in, odd_out = a["odd_w_in_2"][0], a["odd_w_out_2"][0]
        stream += units_of("gq", odd_in, [(0, 512)], (0, KD))
        stream += units_of("lr", odd_in, [(3 * D, 2 * GLA_RANK)], (0, KD), KD)
        for name, c in (("gk", 512), ("gr0", 2 * D), ("gv0", D), ("gv1", D + 512), ("gr1", 2 * D + 512)):
            stream += units_of(name, odd_in, [(c, 512)], (0, KD))
        for n in range(2):
            stream += units_of(f"oout{n}", odd_out, [(n * 512, 512)], (0, KD))

        state = {"loaded": 0, "split": 0, "used": 0}
        raw_free = [[] for _ in range(RAW)]
        ring_free = [[] for _ in range(RING)]

        def queue_loads(upto):
            while state["loaded"] < min(upto, len(stream)):
                unit, i = stream[state["loaded"]], state["loaded"] % RAW
                dst = raw[i][:, 0:unit["per"] * unit["cols"]].rearrange("p (k n) -> p k n", k=unit["per"])
                at = 0
                for src in unit["src"]:
                    n = src.shape[2]
                    unit["landed"] = load_raw[i].start(sp, dst[:, :, at:at + n], src, raw_free[i])
                    at += n
                state["loaded"] += 1

        def queue_splits(upto):
            while state["split"] < min(upto, len(stream)):
                u = state["split"]
                queue_loads(u + 1)
                unit, i = stream[u], u % RING
                n = unit["per"] * unit["cols"]
                src, hi, lo = raw[u % RAW][:, 0:n], WH[i][:, 0:n], WL[i][:, 0:n]
                h = act.do(lambda e, src=src, hi=hi: e.activation(hi, src, ACT.Copy), [unit["landed"]] + ring_free[i])
                l = pool.do(lambda e, src=src, hi=hi, lo=lo: e.tensor_tensor(
                    lo, src, hi.bitcast(F32), ALU.subtract), [unit["landed"], h] + ring_free[i])
                raw_free[u % RAW] = [h, l]
                unit["split"] = [h, l]
                state["split"] += 1
                queue_loads(u + 1 + RAW)

        def split_ahead(n=RING):
            queue_splits(state["used"] + n)

        slots = []

        def slot():
            if slots:
                task = slots.pop(0)
                if task:
                    task()

        def all_slots():
            while slots:
                slot()

        def product(name, k0, banks, x, x_ready, feature_major, first=True, last=True):
            xh, xl = x
            k, mark = k0, None
            while state["used"] < len(stream) and stream[state["used"]]["name"] == name:
                u = state["used"]
                queue_splits(u + AHEAD)
                unit, i = stream[u], u % RING
                per, cols = unit["per"], unit["cols"]
                pe.wait(*unit["split"])
                wh = WH[i][:, 0:per * cols].rearrange("p (k n) -> p k n", k=per)
                wl = WL[i][:, 0:per * cols].rearrange("p (k n) -> p k n", k=per)
                ends = u + 1 == len(stream) or stream[u + 1]["name"] != name
                for kk in range(per):
                    while k >= len(x_ready):
                        slot()
                    for j, b in enumerate(banks):
                        pe.wait(*(x_ready[k][j // 2] if isinstance(x_ready[k], tuple) else x_ready[k]))
                        begin = first and k == k0
                        if begin:
                            pe.wait(*bank_free[b])
                        end = last and ends and kk == per - 1
                        if feature_major:
                            m = min(P, cols - j * P)
                            wj, wlj = wh[:, kk, j * P:j * P + m], wl[:, kk, j * P:j * P + m]
                            o = bank[b][0:m, :]
                            trio = ((wj, xh[:, k, :]), (wj, xl[:, k, :]), (wlj, xh[:, k, :]))
                        else:
                            xt, xlt = xh[:, k, j * P:(j + 1) * P], xl[:, k, j * P:(j + 1) * P]
                            o = bank[b][:, 0:cols]
                            trio = ((xt, wh[:, kk, :]), (xt, wl[:, kk, :]), (xlt, wh[:, kk, :]))
                        for n, (l, r) in enumerate(trio):
                            done = kk == per - 1 and j == len(banks) - 1 and n == 2
                            mark = mm(o, l, r, begin and n == 0, end and n == 2, signal=done) or mark
                    k += 1
                    if kk == per - 1:
                        ring_free[i] = [mark]
                        state["used"] += 1
                    if not (ends and kk == per - 1):
                        slot()
            assert mark is not None, name
            return mark

        def product_by_tokens(name, banks, x, x_ready, tile_done, first=True):
            (xh, xl), units = x, []
            while state["used"] < len(stream) and stream[state["used"]]["name"] == name:
                u = state["used"]
                queue_splits(u + 1)
                unit, i = stream[u], u % RING
                for kk in range(unit["per"]):
                    at = slice(kk * unit["cols"], (kk + 1) * unit["cols"])
                    units.append((WH[i][:, at], WL[i][:, at], unit["split"], i, kk == unit["per"] - 1))
                state["used"] += 1
            for t, b in enumerate(banks):
                if first:
                    pe.wait(*bank_free[b])
                for k, (wh, wl, split, i, unit_ends) in enumerate(units):
                    pe.wait(*split)
                    pe.wait(*x_ready[k])
                    xt, xlt = xh[:, k, t * P:(t + 1) * P], xl[:, k, t * P:(t + 1) * P]
                    last = k == len(units) - 1
                    mm(bank[b][:, :], xt, wh, first and k == 0, False, signal=False)
                    mm(bank[b][:, :], xt, wl, False, False, signal=False)
                    mark = mm(bank[b][:, :], xlt, wh, False, last, signal=unit_ends)
                    if unit_ends:
                        ring_free[i] = [mark]
                tile_done(t, mark)

        turn_bank = {"ring": list(range(8)), "at": 0, "now": [0, 1, 2, 3]}

        def four():
            ring, at = turn_bank["ring"], turn_bank["at"]
            turn_bank["now"] = [ring[(at + i) % len(ring)] for i in range(4)]
            turn_bank["at"] = (at + 4) % len(ring)
            return turn_bank["now"]

        def others():
            return [b for b in range(8) if b not in turn_bank["now"]]

        def product_banks(ring, at=0):
            turn_bank["ring"], turn_bank["at"] = ring, at

        def mm(o, l, r, start, stop, after=(), signal=True):
            return pe.do(lambda e: e.matmul(o, l, r, start=start, stop=stop), after, signal)

        def turn(o, i, after=(), signal=True, small=False):
            eye = ident[0:i.shape[0], 0:i.shape[0]] if small else ident
            return pe.do(lambda e: e.transpose(o, i, eye), list(after) + [con_in], signal)

        def gone():
            return [lane.last() for lane in (pe, act, dve, pool)]

        def settle(marks, *lanes):
            for lane in lanes:
                lane.wait(*marks)

        final_even = sb("final_even_gain", [P, KD])
        gains_in = dve.do(lambda e: e.tensor_tensor(final_even[:, :], V("final_g", 0, KD), V("even_g", 0, KD),
                                                    ALU.mult), [vec_in])
        spare_free = [[]]

        def split_bank(b, src, hi, lo, scale, after):
            if scale is None:
                h = act.do(lambda e: e.activation(hi, src, ACT.Copy), after)
                l = dve.do(lambda e: e.tensor_tensor(lo, src, hi.bitcast(F32), ALU.subtract), [h])
            else:
                h = act.do(lambda e: e.activation(hi, src, ACT.Copy, scale=scale), after)
                l = dve.do(lambda e: e.scalar_tensor_tensor(
                    out=lo, in0=src, scalar=scale, in1=hi.bitcast(F32), op0=ALU.mult, op1=ALU.subtract), [h])
            bank_free[b] = [h, l]
            return [h, l]

        def split_sbuf(src, hi, lo, after):
            h = act.do(lambda e: e.activation(hi, src, ACT.Copy), after)
            l = dve.do(lambda e: e.tensor_tensor(lo, src, hi.bitcast(F32), ALU.subtract), [h])
            return [h, l]

        def turn_and_split(src, k, marks, gain, x_free, x_ready):
            b = others()[turned_count[0] % 4]
            turned_count[0] += 1
            for t in range(T):
                m = turn(bank[b][:, t * P:(t + 1) * P], src[:, t, k * P:(k + 1) * P],
                         list(marks[t]) + bank_free[b], signal=(t == T - 1))
            assert len(x_ready) == k
            x_ready.append(split_bank(b, bank[b][:, :], XH[:, k, :], XL[:, k, :], gain, [m, gains_in] + x_free))

        turned_count = [0]

        def squares(src, out, after):
            junk = spare[:, 0:src.shape[-1] // P, :].rearrange("p t n -> p (t n)")
            m = act.do(lambda e: e.activation(junk, src, ACT.Square, accum_out=out), list(after) + spare_free[0])
            spare_free[0] = [m]
            return m

        def inverse_root(out, total, width, after):
            root = act.do(lambda e: e.activation(out, total, ACT.Sqrt, bias=epsc[:, 0:1], scale=1.0 / width),
                          list(after) + [eps_set])
            return dve.do(lambda e: e.reciprocal(out, out), [root])

        def broadcast(column, out, after, b=None):
            marks = [dve.do(lambda e, t=t: e.tensor_scalar(
                spare[:, t, :], ident, column[:, t:t + 1], None, ALU.mult), list(after) + [con_in] + spare_free[0])
                for t in range(T)]
            b = others()[turned_count[0] % 4] if b is None else b
            turned_count[0] += 1
            m = mm(bank[b][:, :], mean_ones, spare[:, :, :].rearrange("p t n -> p (t n)"), True, True,
                   marks + bank_free[b])
            spare_free[0] = [m]
            r = act.do(lambda e: e.activation(out, bank[b][:, :], ACT.Copy, scale=float(D)), [m, dve.last()])
            bank_free[b] = [r]
            return r

        class Norm:
            count = 0

            def __init__(self, gain, x_free):
                self.at, self.gain, self.x_free = Norm.count, gain, x_free
                Norm.count += 1
                self.x_ready, self.sums = [], []

            def col(self, c):
                return norm_stat[:, self.at, c, :]

            def r(self, t):
                return norm_stat[:, self.at, 2, t:t + 1]

            def rr(self, t):
                return norm_stat[:, self.at, 3, t:t + 1]

            def turn(self, k):
                turn_and_split(H, k, self.marks[k // 4], self.gain(k), self.x_free, self.x_ready)

            def add_squares(self, half):
                for t in range(T):
                    self.sums.append(squares(H[:, t, half * 512:(half + 1) * 512],
                                             norm_stat[:, self.at, half, t:t + 1], self.marks[half][t]))

            def roots(self):
                both = dve.do(lambda e: e.tensor_tensor(self.col(2), self.col(0), self.col(1), ALU.add), self.sums)
                self.r_ready = inverse_root(self.col(2), self.col(2), D, [both])
                self.rr_ready = dve.do(lambda e: e.tensor_tensor(self.col(3), self.col(2), self.col(2), ALU.mult),
                                       [self.r_ready])

            def row(self):
                self.row_ready = broadcast(self.col(2), rrow[:, :], [self.r_ready])

            marks = None

            def half(self, n, marks):
                self.marks = (self.marks or []) + [marks]
                if n == 0:
                    for k in range(4):
                        slots.append(lambda k=k: self.turn(k))
                    slots.append(lambda: self.add_squares(0))
                else:
                    self.add_squares(1)
                    slots.append(lambda: [self.turn(4), self.turn(5)])
                    slots.append(lambda: [self.turn(6), self.turn(7)])
                    slots.append(self.roots)

        def start_norm():
            norm = Norm(lambda k: V("mix_g0", k), [])
            norm.marks = [[[x_in[1]]] * T, [[x_in[3]]] * T]
            queue_splits(1)
            for k in range(KD):
                for t in range(T):
                    m = turn(bank[k][:, t * P:(t + 1) * P], H[:, t, k * P:(k + 1) * P], [x_in[k // 2]])
                norm.x_ready.append(split_bank(k, bank[k][:, :], XH[:, k, :], XL[:, k, :], norm.gain(k),
                                               [m, gains_in]))
            queue_splits(3)
            norm.add_squares(0)
            return norm

        def close(names, x, x_ready, evacuate, norm):
            for n in range(2):
                banks = four()
                m = product(names[n], 0, banks, x, x_ready, False)
                all_slots()
                norm.half(n, evacuate(n, banks, m))
            return norm

        def add_to_residual(n, banks, m, scale=None, after=()):
            marks = []
            for t, b in enumerate(banks):
                hh = H[:, t, n * 512:(n + 1) * 512]
                if scale is None:
                    d = dve.do(lambda e, b=b, hh=hh: e.tensor_tensor(hh, bank[b][:, :], hh, ALU.add), [m] + list(after))
                else:
                    d = dve.do(lambda e, b=b, hh=hh, t=t: e.scalar_tensor_tensor(
                        out=hh, in0=bank[b][:, :], scalar=scale(t), in1=hh, op0=ALU.mult, op1=ALU.add),
                        [m] + list(after))
                bank_free[b] = [d]
                marks.append([d])
            return marks

        def times_row(b, m, dst, row, after=()):
            d = dve.do(lambda e: e.tensor_tensor(dst, bank[b][:, :], row, ALU.mult), [m] + list(after))
            bank_free[b] = [d]
            return d

        X = (XH, XL)

        def dsa_stage(norm):
            scope = ExitStack()
            with scope:
                vT = sb("v_tok", [P, T, D], scope=scope)
                qT = sb("q_feat", [P, HEADS, S], scope=scope)
                kT = sb("k_feat", [P, HEADS, S], scope=scope)
                bias = sb("score_then_bias", [P, T, S], scope=scope)
                att = sb("att_stats", [P, 4, 2], scope=scope)
                index = ExitStack()
                qi = sb("qi_hi_and_lo", [P, HEADS, S], F32R, scope=index)
                kiH = sb("ki_hi", [P, S], F32R, scope=index)
                kiL = sb("ki_lo", [P, S], F32R, scope=index)
                ki = sb("ki_tok", [P, T, P], scope=index)
                kiT = sb("ki_feat", [P, S], scope=index)
                narrow = sb("narrow_feat", [IDX_DIM + HEADS, S], scope=index)
                wi = sb("wi_tok", [P, T, HEADS], scope=index)
                bn = sb("ki_stats", [P, T, 6], scope=index)
                mv = sb("ki_meanvar", [P, T, 2], scope=index)
                relu = [sb(f"relu{i}", [P, S], scope=index) for i in range(2)]
                top8 = sb("top8", [P, T, 8], scope=index)
                x_ready = norm.x_ready

                banks = four()
                m = product("idx_narrow", 0, banks[:1], X, x_ready, True)
                nar = act.do(lambda e, b=banks[0]: e.activation(narrow[:, :], bank[b][0:IDX_DIM + HEADS, :], ACT.Copy), [m])
                bank_free[banks[0]] = [nar]
                norm.add_squares(1)
                norm.roots()

                def turn_narrow():
                    b = banks[1]
                    for t in range(T):
                        m = turn(bank[b][:, t * P:t * P + IDX_DIM + HEADS], narrow[:, t * P:(t + 1) * P],
                                 [nar] + bank_free[b], small=True)
                    index_norm(b, m)

                sc = dve.do(lambda e: e.tensor_scalar(norm.col(4), norm.col(2), P ** -0.5, None, ALU.mult),
                            [norm.r_ready])
                nsc_ready = dve.do(lambda e: e.tensor_scalar(norm.col(5), norm.col(4), -1.0, None, ALU.mult), [sc])
                wi_ready, kn = [], []

                def index_norm(b, m):
                    ln = []
                    for t in range(T):
                        at = t * P
                        w = dve.do(lambda e, t=t, at=at: e.tensor_scalar(
                            wi[:, t, :], bank[b][:, at + IDX_DIM:at + IDX_DIM + HEADS], norm.rr(t),
                            HEADS ** -0.5 * IDX_DIM ** -0.5, ALU.mult, ALU.mult), [m, norm.rr_ready])
                        c = dve.do(lambda e, t=t, at=at: e.tensor_scalar(
                            ki[:, t, 0:IDX_DIM], bank[b][:, at:at + IDX_DIM], norm.r(t), None, ALU.mult),
                            [m, norm.r_ready])
                        bank_free[b] = [w, c]
                        wi_ready.append(w)
                        s = dve.do(lambda e, t=t: e.bn_stats(bn[:, t, :], ki[:, t, 0:IDX_DIM]), [c])
                        ln.append(dve.do(lambda e, t=t: e.bn_aggr(mv[:, t, :], bn[:, t, :]), [s]))
                    root = act.do(lambda e: e.activation(norm.col(6), mv[:, :, 1], ACT.Sqrt, bias=epsc[:, 0:1]),
                                  ln + [eps_set])
                    rs = dve.do(lambda e: e.reciprocal(norm.col(6), norm.col(6)), [root])
                    for t in range(T):
                        for c in (1, 0):
                            kn.append(dve.do(lambda e, t=t, c=c: e.tensor_scalar(
                                ki[:, t, c * IDX_DIM:(c + 1) * IDX_DIM], ki[:, t, 0:IDX_DIM], mv[:, t, 0:1],
                                norm_stat[:, norm.at, 6, t:t + 1], ALU.subtract, ALU.mult), [rs] + kn[-1:]))

                ki_ready = []

                def turn_ki():
                    b = others()[0]
                    for t in range(T):
                        m = turn(bank[b][:, t * P:(t + 1) * P], ki[:, t, :], [kn[-1]] + bank_free[b])
                    ki_ready.append(dve.do(lambda e: e.tensor_scalar(
                        kiT[:, :], bank[b][:, :], V("idx_g"), V("idx_b"), ALU.mult, ALU.add), [m]))
                    bank_free[b] = [ki_ready[0]]
                    ki_ready.extend(split_sbuf(kiT[:, :], kiH[:, :], kiL[:, :], [ki_ready[0]]))

                def feature(name, dst, t0, row=None):
                    banks = four()
                    m = product(name, 0, banks, X, x_ready, True)
                    marks = []
                    for j, b in enumerate(banks):
                        if row is None:
                            d = act.do(lambda e, j=j, b=b: e.activation(dst[:, t0 + j, :], bank[b][:, :], ACT.Copy), [m])
                            bank_free[b] = [d]
                        else:
                            d = times_row(b, m, dst[:, t0 + j, :], row, [norm.row_ready])
                        marks.append(d)
                    return marks

                slots.extend([None, None, turn_narrow, None, norm.row, turn_ki])
                qi_banks = four()
                m = product("qi", 0, qi_banks, X, x_ready, True)
                qi_ready = {}
                for j, b in enumerate(qi_banks):
                    for half in range(2):
                        h, at, other = 2 * j + half, half * IDX_DIM, (1 - half) * IDX_DIM
                        hi = qi[at:at + IDX_DIM, h, :]
                        hm = act.do(lambda e, b=b, at=at, hi=hi: e.activation(
                            hi, bank[b][at:at + IDX_DIM, :], ACT.Copy), [m] + bank_free[b] * half)
                        lm = dve.do(lambda e, b=b, at=at, hi=hi, h=h, other=other: e.tensor_tensor(
                            qi[other:other + IDX_DIM, h, :], bank[b][at:at + IDX_DIM, :], hi.bitcast(F32),
                            ALU.subtract), [hm])
                        bank_free[b] = [lm]
                        qi_ready[h] = [hm, lm]

                assert TOPK == P
                score_ready, bias_ready = [None] * T, [None] * T
                relu_free = [[], []]
                uses = [0]
                bias_ready[0] = dve.do(lambda e: e.tensor_copy(bias[:, 0, 0:P], C("causal")), [con2_in])

                def score_task(t, h):
                    n = (t + 1) * P
                    b, i, p0 = others()[uses[0] % 4], uses[0] % 2, IDX_DIM * (h % 2)
                    uses[0] += 1
                    mm(bank[b][:, 0:n], qi[:, h, t * P:(t + 1) * P], kiH[:, 0:n], True, False,
                       qi_ready[h] + ki_ready + bank_free[b])
                    m = mm(bank[b][:, 0:n], qi[p0:p0 + IDX_DIM, h, t * P:(t + 1) * P],
                           kiL[p0:p0 + IDX_DIM, 0:n], False, True)
                    r = act.do(lambda e: e.activation(relu[i][:, 0:n], bank[b][:, 0:n], ACT.Relu), [m] + relu_free[i])
                    bank_free[b] = [r]
                    w = wi[:, t, h:h + 1]
                    if h == 0:
                        acc = dve.do(lambda e: e.tensor_scalar(
                            bias[:, t, 0:n], relu[i][:, 0:n], w, None, ALU.mult), [r, wi_ready[t]])
                    else:
                        acc = dve.do(lambda e: e.scalar_tensor_tensor(
                            out=bias[:, t, 0:n], in0=relu[i][:, 0:n], scalar=w, in1=bias[:, t, 0:n],
                            op0=ALU.mult, op1=ALU.add), [r, score_ready[t]])
                    relu_free[i] = [acc]
                    score_ready[t] = acc
                    if h == HEADS - 1:
                        c = bias[:, t, t * P:n]
                        score_ready[t] = pool.do(lambda e: e.affine_select(
                            out=c, in_=c, compare_op=ALU.is_ge, fill=CAUSAL_FILL, base=0,
                            pattern=[[-1, P]], channel_multiplier=1), [acc])

                def top_round(t, r):
                    n = (t + 1) * P
                    m8 = dve.do(lambda e: e.max(top8[:, t, :], bias[:, t, 0:n]), [score_ready[t]])
                    score_ready[t] = dve.do(lambda e: e.match_replace(
                        out=bias[:, t, 0:n], in_to_replace=top8[:, t, :], in_values=bias[:, t, 0:n],
                        imm_value=TAKEN), [m8])
                    if r == TOPK // 8 - 1:
                        bias_ready[t] = dve.do(lambda e: e.tensor_scalar(
                            bias[:, t, 0:n], bias[:, t, 0:n], TAKEN, -BIG, ALU.not_equal, ALU.mult),
                            [score_ready[t]])

                scoring = [(score_task, t, h) for t in range(1, T) for h in range(HEADS)]
                rounds = [(top_round, t, r) for r in range(TOPK // 8) for t in range(1, T)]
                all_slots()
                slots.extend([None, None])
                in_slots(scoring, 4)
                in_slots(rounds, 3)

                v_ready = []
                for n in range(2):
                    banks = four()
                    m = product(f"v{n}", 0, banks, X, x_ready, False)
                    for t, b in enumerate(banks):
                        d = act.do(lambda e, t=t, n=n, b=b: e.activation(
                            vT[:, t, n * 512:(n + 1) * 512], bank[b][:, :], ACT.Copy, scale=norm.r(t)), [m])
                        bank_free[b] = [d]
                        v_ready.append(d)
                q_ready = feature("q0", qT, 0)
                k_ready = feature("k0", kT, 0, rrow[:, :])
                all_slots()
                index.close()
                left = gone()
                settle(left, act, dve)
                YH = sb("att_hi", [P, HEADS, S], F32R, scope=scope)
                YL = sb("att_lo", [P, HEADS, S], F32R, scope=scope)
                lg = [sb(f"prob{i}", [P, S], scope=scope) for i in range(4)]
                PT = [sb(f"prob_turned{i}", [P, S], scope=scope) for i in range(3)]

                product_banks([0, 1, 2, 3])
                items = [(h, t) for h in range(HEADS) for t in range(T)]
                logit_mark, prob_mark = {}, {}
                turned_mark, copied = {}, {}
                value_mark = {}
                o_ready = []

                def logits(i):
                    h, t = items[i]
                    n, b = (t + 1) * P, 4 + i % 2
                    logit_mark[i] = mm(bank[b][:, 0:n], qT[:, h, t * P:(t + 1) * P], kT[:, h, 0:n], True, True,
                                       [q_ready[h], k_ready[h]] + bank_free[b])

                def softmax(i):
                    h, t = items[i]
                    n, b, p = (t + 1) * P, 4 + i % 2, lg[i % 4]
                    mx, sm = att[:, i % 4, 0:1], att[:, i % 4, 1:2]
                    m1 = dve.do(lambda e: e.tensor_tensor_reduce(
                        out=p[:, 0:n], in0=bank[b][:, 0:n], in1=bias[:, t, 0:n], scale=1.0,
                        scalar=-3e38, op0=ALU.add, op1=ALU.max, accum_out=mx),
                        [logit_mark[i], bias_ready[t], turned_mark.get(i - 4), prob_mark.get(i - 4)])
                    bank_free[b] = [m1]
                    m2 = dve.do(lambda e: e.tensor_scalar(
                        mx, mx, norm_stat[:, norm.at, 5, t:t + 1], None, ALU.mult), [m1, nsc_ready])
                    ex = act.do(lambda e: e.activation(
                        p[:, 0:n], p[:, 0:n], ACT.Exp, bias=mx, scale=norm_stat[:, norm.at, 4, t:t + 1],
                        accum_out=sm), [m2])
                    rc = dve.do(lambda e: e.reciprocal(sm, sm), [ex])
                    prob_mark[i] = dve.do(lambda e: e.tensor_scalar(p[:, 0:n], p[:, 0:n], sm, None, ALU.mult), [rc])

                def turn_probs(i):
                    h, t = items[i]
                    n, p, o = (t + 1) * P, lg[i % 4], PT[i % 3]
                    for s in range(t + 1):
                        m = turn(bank[6][:, s * P:(s + 1) * P], p[:, s * P:(s + 1) * P],
                                 [prob_mark[i]] + bank_free[6])
                    turned_mark[i] = m
                    after = [m, value_mark.get(i - 3)]
                    if i % 2:
                        c = act.do(lambda e: e.activation(o[:, 0:n], bank[6][:, 0:n], ACT.Copy), after)
                    else:
                        c = dve.do(lambda e: e.tensor_copy(o[:, 0:n], bank[6][:, 0:n]), after)
                    bank_free[6] = [c]
                    copied[i] = c

                def values(i):
                    h, t = items[i]
                    p = PT[i % 3]
                    for s in range(t + 1):
                        m = mm(bank[7][:, t * P:(t + 1) * P], vT[:, s, h * P:(h + 1) * P],
                               p[:, s * P:(s + 1) * P], s == 0, s == t, [copied[i]] + v_ready + bank_free[7])
                    value_mark[i] = m
                    if t == T - 1:
                        o_ready.append(split_bank(7, bank[7][:, :], YH[:, h, :], YL[:, h, :], None, [m]))

                def step(i):
                    if i < len(items):
                        logits(i)
                    if 0 <= i - 2 < len(items):
                        turn_probs(i - 2)
                    if 0 <= i - 3 < len(items):
                        values(i - 3)
                    if i < len(items):
                        softmax(i)

                steps = [(step, i) for i in range(len(items) + 3)]
                in_slots(steps[:14], 1)
                q_ready += feature("q1", qT, 4)
                k_ready += feature("k1", kT, 4, rrow[:, :])
                x_free = [pe.last()]
                all_slots()
                in_slots(steps[14:], 2)

                nxt = Norm(lambda k: V("mlp_g0", k), x_free)
                banks = four()
                m = product("dsa_out0", 0, banks, (YH, YL), o_ready, False)
                all_slots()
                product_banks(list(range(8)), 4)
                nxt.half(0, add_to_residual(0, banks, m))
                banks = four()
                m = product("dsa_out1", 0, banks, (YH, YL), o_ready, False)
                all_slots()
                nxt.half(1, add_to_residual(1, banks, m))
            nxt.left = gone()
            return nxt

        def mlp_stage(layer, norm, next_gain):
            scope = ExitStack()
            with scope:
                FH = sb(f"f_hi{layer}", [P, 16, S], F32R, scope=scope)
                FL = sb(f"f_lo{layer}", [P, 16, S], F32R, scope=scope)
                relu = [sb(f"f_relu{layer}_{i}", [P, S], scope=scope) for i in range(4)]
                square = [sb(f"f_square{layer}_{i}", [P, S], scope=scope) for i in range(4)]
                relu_free, square_free = [[] for _ in range(4)], [[] for _ in range(4)]
                f_free = []
                for half in range(2):
                    f_ready = []
                    for g in range(4):
                        banks = four()
                        m = product(f"up{layer}{half}{g}", 0, banks, X, norm.x_ready, True)
                        all_slots()
                        if half == 0 and g == 0:
                            settle(norm.left, act, dve)
                        rs = []
                        for j, b in enumerate(banks):
                            r = act.do(lambda e, j=j, b=b: e.activation(relu[j][:, :], bank[b][:, :], ACT.Relu),
                                       [m] + relu_free[j])
                            bank_free[b] = [r]
                            rs.append(r)
                        ss = [dve.do(lambda e, j=j: e.tensor_tensor(square[j][:, :], relu[j][:, :], relu[j][:, :],
                                                                    ALU.mult), [rs[j]] + square_free[j]) for j in range(4)]
                        for j in range(4):
                            relu_free[j] = [ss[j]]
                            k = g * 4 + j
                            f = split_sbuf(square[j][:, :], FH[:, k, :], FL[:, k, :], [ss[j]] + f_free)
                            square_free[j] = f
                            f_ready.append(f)
                    def evacuate(n, banks, m):
                        return add_to_residual(n, banks, m, norm.rr, [norm.rr_ready])

                    if half == 0:
                        for n in range(2):
                            banks = four()
                            m = product(f"down{layer}{half}{n}", 0, banks, (FH, FL), f_ready, False)
                            evacuate(n, banks, m)
                        f_free = [m]
                    else:
                        nxt = close([f"down{layer}10", f"down{layer}11"], (FH, FL), f_ready, evacuate,
                                    Norm(next_gain, [m]))
            nxt.left = gone()
            return nxt

        def conv_stage(norm):
            scope = ExitStack()
            with scope:
                PAD = CONV_W - 1
                every = list(range(CONV_W))
                PE_TAPS = {7: every, 6: every[14:]}
                POOL_TAPS = {0: every[:6], 1: every, 3: every[:11]}
                DVE_TAPS = {0: every[6:], 2: every, 3: every[11:], 4: every, 5: every, 6: every[:14]}
                u = sb("conv_u", [P, KD, PAD + S], scope=scope)
                c = sb("conv_c", [P, KD, S], scope=scope)
                odd = [sb(f"conv_sum{i}", [P, S], scope=scope) for i in range(2)]
                mean = sb("conv_mean_then_rstd", [P, S], scope=scope)
                taps = ExitStack()
                diag = sb("conv_diag", [P, sum(len(v) for v in PE_TAPS.values()), P], scope=taps)
                lin = [sb(f"conv_lin{i}", [P, S], scope=taps) for i in range(2)]
                gate = [sb(f"conv_gate{i}", [P, S], scope=taps) for i in range(2)]
                part = [sb(f"conv_product{i}", [P, S], scope=taps) for i in range(3)]
                u_ready = [None] * KD
                parts_done = {k: [] for k in range(KD)}
                odd_free, part_free = [[], []], [[], [], []]

                def window(k, i):
                    return u[:, k, i:i + S], V("dw_w", k * CONV_W + i)

                def dve_tap(k, i):
                    n = DVE_TAPS[k].index(i)
                    (src, w), side = window(k, i), n % 2
                    dst = c[:, k, :] if side == 0 and k not in POOL_TAPS else odd[side][:, :]
                    if n == 0 and k not in POOL_TAPS:
                        m = dve.do(lambda e: e.tensor_scalar(dst, src, w, V("dw_b", k), ALU.mult, ALU.add), [u_ready[k]])
                    elif n < 2:
                        m = dve.do(lambda e: e.tensor_scalar(dst, src, w, None, ALU.mult), [u_ready[k]] + odd_free[side])
                    else:
                        m = dve.do(lambda e: e.scalar_tensor_tensor(
                            out=dst, in0=src, scalar=w, in1=dst, op0=ALU.mult, op1=ALU.add), [dve_mark[side]])
                    dve_mark[side] = m
                    if n == len(DVE_TAPS[k]) - 1:
                        while k in POOL_TAPS and not parts_done[k]:
                            pool_tap(*pool_due.pop(0))
                        for side in ((0, 1) if k in POOL_TAPS else (1,)):
                            d = dve.do(lambda e, side=side: e.tensor_tensor(
                                c[:, k, :], c[:, k, :], odd[side][:, :], ALU.add), dve_mark + parts_done[k])
                            parts_done[k] = [d]
                            odd_free[side] = [d]

                def pool_tap(k, i):
                    (src, w), p = window(k, i), pool_count[0] % 3
                    if i == POOL_TAPS[k][0]:
                        m = act.do(lambda e: e.activation(c[:, k, :], src, ACT.Identity, scale=w, bias=V("dw_b", k)),
                                   [u_ready[k]])
                    else:
                        m = act.do(lambda e: e.activation(part[p][:, :], src, ACT.Copy, scale=w),
                                   [u_ready[k]] + part_free[p])
                        m = pool.do(lambda e: e.tensor_tensor(c[:, k, :], c[:, k, :], part[p][:, :], ALU.add),
                                    [m, pool_mark[0]])
                        part_free[p] = [m]
                        pool_count[0] += 1
                    pool_mark[0] = m
                    if i == POOL_TAPS[k][-1]:
                        parts_done[k] = [m]

                pool_count, pool_mark, dve_mark = [0], [None], [None, None]
                diag_at, diag_marks = {}, {}
                for k in PE_TAPS:
                    for i in PE_TAPS[k]:
                        diag_at[k, i] = len(diag_at)

                def make_diag(k, i):
                    diag_marks[k, i] = act.do(lambda e: e.activation(
                        diag[:, diag_at[k, i], :], ident, ACT.Copy, scale=V("dw_w", k * CONV_W + i)), [con_in])

                slots.append(norm.row)
                dve_due, pool_due, diag_due = [], [], list(diag_at)

                def some(n_dve, n_pool, n_diag=0):
                    for n, due, take in ((n_dve, dve_due, dve_tap), (n_pool, pool_due, pool_tap),
                                         (n_diag, diag_due, make_diag)):
                        for _ in range(min(n, len(due))):
                            take(*due.pop(0))

                lin_free, gate_free = [[], []], [[], []]
                x_ready = norm.x_ready
                for k in range(KD):
                    banks = four()
                    m = product(f"pw1{k}", 0, banks[:2], X, x_ready, True)
                    all_slots()
                    if k == 0:
                        settle(norm.left, act, dve, pool)
                        row_in = load_gain_row("b_pw2", [])
                        padded = dve.do(lambda e: e.memset(u[:, :, 0:PAD], 0.0))
                    j = k % 2
                    g2 = times_row(banks[1], m, gate[j][:, :], rrow[:, :], [norm.row_ready] + gate_free[j])
                    g1 = times_row(banks[0], m, lin[j][:, :], rrow[:, :], lin_free[j])
                    s = act.do(lambda e, j=j, k=k: e.activation(
                        gate[j][:, :], gate[j][:, :], ACT.Sigmoid, bias=V("pw1_b", KD + k)), [g2])
                    u_ready[k] = dve.do(lambda e, j=j, k=k: e.scalar_tensor_tensor(
                        out=u[:, k, PAD:PAD + S], in0=lin[j][:, :], scalar=V("pw1_b", k), in1=gate[j][:, :],
                        op0=ALU.add, op1=ALU.mult), [s, g1, padded])
                    lin_free[j] = gate_free[j] = [u_ready[k]]
                    pool_due += [(k, i) for i in POOL_TAPS.get(k, [])]
                    if k != 3:
                        dve_due += [(k, i) for i in DVE_TAPS.get(k, [])]
                    if k < KD - 1:
                        for n in range(7):
                            in_slots([(some, 2, n % 2, 1)], 1)
                x_free = [pe.last()]
                split_ahead()
                while pool_due:
                    some(2, 1, 2)
                dve_due += [(3, i) for i in DVE_TAPS[3]]
                some(len(dve_due), 0, len(diag_due))
                load_table("sqrt_and_others")

                bm, bv, b7, b6 = four()
                for k, b in ((6, b6), (7, b7)):
                    for i in PE_TAPS[k]:
                        m = mm(bank[b][:, :], diag[:, diag_at[k, i], :], u[:, k, i:i + S], i == PE_TAPS[k][0],
                               i == PE_TAPS[k][-1], [diag_marks[k, i], u_ready[k], padded] + bank_free[b])
                    if k in DVE_TAPS:
                        d = dve.do(lambda e, k=k, b=b: e.tensor_tensor(c[:, k, :], bank[b][:, :], c[:, k, :], ALU.add),
                                   [m] + parts_done[k])
                    else:
                        d = act.do(lambda e, k=k, b=b: e.activation(
                            c[:, k, :], bank[b][:, :], ACT.Identity, bias=V("dw_b", k)), [m])
                    bank_free[b] = parts_done[k] = [d]
                order = [0, 1, 2, 7, 4, 5, 3, 6]
                for k in order:
                    m = mm(bank[bm][:, :], mean_ones, c[:, k, :], k == order[0], k == order[-1],
                           parts_done[k] + bank_free[bm])
                taps.close()
                after_taps = gone()
                YH = sb("conv_hi", [P, KD, S], F32R, scope=scope)
                YL = sb("conv_lo", [P, KD, S], F32R, scope=scope)
                mean_ready = act.do(lambda e: e.activation(mean[:, :], bank[bm][:, :], ACT.Copy), [m])
                bank_free[bm] = [mean_ready]
                sq_free = [[], []]
                sq = odd
                cents = []
                for n, k in enumerate(order):
                    i = n % 2
                    lane = pool if n in (2, 5) else dve
                    cent = lane.do(lambda e, k=k: e.tensor_tensor(
                        c[:, k, :], c[:, k, :], mean[:, :], ALU.subtract), [mean_ready])
                    cents.append(cent)
                    s = act.do(lambda e, k=k, i=i: e.activation(sq[i][:, :], c[:, k, :], ACT.Square),
                               [cent] + odd_free[i] + sq_free[i])
                    m = mm(bank[bv][:, :], mean_ones, sq[i][:, :], n == 0, n == KD - 1, [s] + bank_free[bv])
                    sq_free[i] = [m]
                rs = act.do(lambda e: e.activation(mean[:, :], bank[bv][:, :], ACT.Sqrt, bias=epsc[:, 0:1]), [m] + cents)
                bank_free[bv] = [rs]
                load_table("silu_and_others")
                settle(after_taps, act, dve)

                def normalised(k, at, rs):
                    o = c[:, k, at]
                    n = dve.do(lambda e: e.tensor_tensor(o, o, mean[:, at], ALU.mult), [rs])
                    return act.do(lambda e: e.activation(o, o, ACT.Silu, bias=V("ln_b", k), scale=V("ln_g", k)), [n])

                at0, at1 = slice(0, S // 2), slice(S // 2, S)
                rh = dve.do(lambda e: e.reciprocal(mean[:, at0], mean[:, at0]), [rs])
                s0 = normalised(0, at0, rh)
                rh = dve.do(lambda e: e.reciprocal(mean[:, at1], mean[:, at1]), [rs])
                y0 = split_sbuf(c[:, 0, at0], YH[:, 0, at0], YL[:, 0, at0], [s0])
                s1 = normalised(0, at1, rh)
                y_ready = [(y0, split_sbuf(c[:, 0, at1], YH[:, 0, at1], YL[:, 0, at1], [s1]))]
                for k in range(1, KD):
                    s = normalised(k, slice(0, S), rh)
                    y_ready.append(split_sbuf(c[:, k, :], YH[:, k, :], YL[:, k, :], [s]))
                biased = [[None] * T for _ in range(2)]

                def add_bias(n):
                    for t in range(T):
                        hh = H[:, t, n * 512:(n + 1) * 512]
                        biased[n][t] = pool.do(lambda e, hh=hh: e.tensor_tensor(
                            hh, hh, gain_row[:, n * 512:(n + 1) * 512], ALU.add), [row_in])

                slots.extend([lambda: add_bias(0), None, None, lambda: add_bias(1)])

                def evacuate(n, banks, m):
                    return add_to_residual(n, banks, m, None, biased[n])

                nxt = close(["pw20", "pw21"], (YH, YL), y_ready, evacuate, Norm(lambda k: V("mlp_g1", k), x_free))
            nxt.left = gone()
            return nxt

        def load_table(name):
            act.queue.append(lambda e: e.preload_act_table_set(name))

        def in_slots(tasks, per):
            for i in range(0, len(tasks), per):
                slots.append(lambda group=tasks[i:i + per]: [f(*args) for f, *args in group])

        def even_stage(norm):
            scope = ExitStack()
            with scope:
                YBH = sb("yb_hi", [P, KD, S], F32R, scope=scope)
                YBL = sb("yb_lo", [P, KD, S], F32R, scope=scope)
                ya = sb("rg_y", [P, KD, S], scope=scope)
                ua = sb("rg_u", [P, 4, S], scope=scope)
                R = sb("rg_r", [P, 4, S], scope=scope)
                I = sb("rg_i", [P, 4, S], scope=scope)
                Q = sb("rg_t", [P, 4, S], scope=scope)
                xpad = sb("conv_in", [P, 4, S + 3], scope=scope)
                sc = sb("sc_acc", [P, 4, S], scope=scope)
                silu = [sb(f"even_silu{i}", [P, S], scope=scope) for i in range(2)]
                sqr = [sb(f"rg_sq{i}", [P, S], scope=scope) for i in range(1)]
                gw = sb("gate_w", [P, 8, P], scope=scope)
                coef = sb("rg_coef", [P, 2 * KD], scope=scope)
                sp1 = sb("sp_z", [P, 2 * KD], scope=scope)
                sp2 = sb("sp_w", [P, 2 * KD], scope=scope)
                sp3 = sb("sp_s", [P, 2 * KD], scope=scope)
                load_gw = Landing(sem("gate_w_landed"))
                x_ready = norm.x_ready
                got = {}

                def finish_norm():
                    h1 = []
                    for t in range(T):
                        m = dve.do(lambda e, t=t: e.scalar_tensor_tensor(
                            out=H[:, t, :], in0=H[:, t, :], scalar=norm.r(t), in1=gain_row[:, :],
                            op0=ALU.mult, op1=ALU.mult), [norm.r_ready, got["final_g"], got["turned"]])
                        for n in range(2):
                            h1.append(squares(H[:, t, n * 512:(n + 1) * 512],
                                              norm_stat[:, norm.at, 4 + n, t:t + 1], [m]))
                    got["h1"] = h1

                def second_root():
                    c4, c5, c6 = norm.col(4), norm.col(5), norm.col(6)
                    both = dve.do(lambda e: e.tensor_tensor(c6, c4, c5, ALU.add), got["h1"])
                    r2 = inverse_root(c6, c6, D, [both])
                    both = dve.do(lambda e: e.tensor_tensor(c4, c6, norm.col(2), ALU.mult), [r2])
                    sq = dve.do(lambda e: e.tensor_tensor(c5, c4, c4, ALU.mult), [both])
                    got["r"], got["r2"] = both, sq
                    got["row"] = load_gain_row("even_post", got["h1"])

                def rows():
                    norm.row_ready = broadcast(norm.col(4), rrow[:, :], [got["r"]])
                    norm.row2_ready = broadcast(norm.col(5), rrow2[:, :], [got["r2"]])

                def load_gates(direction, g, after):
                    for which in range(2):
                        landed = load_gw.start(sp, gw[:, 4 * which:4 * which + 4, :],
                                               a["rg_gate_w_2"][0, direction, which, 4 * g:4 * g + 4]
                                               .rearrange("h i j -> i h j"), after)
                    got["gates"] = landed

                got["final_g"] = load_gain_row("final_g", [dve.last(), pool.last()])
                slots.insert(2, lambda: got.update(turned=pe.last()))
                slots.extend([finish_norm, second_root, None, rows])

                def make_coef():
                    lam = V("lam", 0, 2 * KD)
                    m = act.do(lambda e: e.activation(sp1[:, :], lam, ACT.Abs), [vec_in])
                    m = act.do(lambda e: e.activation(sp1[:, :], sp1[:, :], ACT.Exp, scale=-1.0), [m])
                    m = dve.do(lambda e: e.tensor_scalar(sp2[:, :], sp1[:, :], 2.0, None, ALU.add), [m])
                    m = dve.do(lambda e: e.reciprocal(sp2[:, :], sp2[:, :]), [m])
                    m = dve.do(lambda e: e.tensor_tensor(sp1[:, :], sp1[:, :], sp2[:, :], ALU.mult), [m])
                    m = dve.do(lambda e: e.tensor_tensor(sp2[:, :], sp1[:, :], sp1[:, :], ALU.mult), [m])
                    m = dve.do(lambda e: e.memset(sp3[:, :], 1.0 / 19), [m])
                    for d in range(17, 0, -2):
                        m = dve.do(lambda e: e.tensor_tensor(sp3[:, :], sp3[:, :], sp2[:, :], ALU.mult), [m])
                        m = dve.do(lambda e, d=d: e.tensor_scalar(sp3[:, :], sp3[:, :], 1.0 / d, None, ALU.add), [m])
                    m = dve.do(lambda e: e.scalar_tensor_tensor(
                        out=sp3[:, :], in0=sp3[:, :], scalar=2.0, in1=sp1[:, :], op0=ALU.mult, op1=ALU.mult), [m])
                    m = dve.do(lambda e: e.tensor_scalar(sp2[:, :], lam, -1.0, 0.0, ALU.mult, ALU.max), [m])
                    m = dve.do(lambda e: e.tensor_tensor(sp3[:, :], sp3[:, :], sp2[:, :], ALU.add), [m])
                    got["coef"] = dve.do(lambda e: e.tensor_scalar(coef[:, :], sp3[:, :], -RG_C, None, ALU.mult), [m])

                ua_ready, ya_ready, yb_ready = [None] * KD, [None] * KD, [None] * KD
                state = {"pad_free": [], "ua_free": [], "rg_free": [], "gw_free": [], "sqr_free": []}

                def long_conv(g, banks, m):
                    edges = [dve.do(lambda e: e.memset(xpad[:, :, 0:2], 0.0), state["pad_free"]),
                             dve.do(lambda e: e.memset(xpad[:, :, S + 2:S + 3], 0.0), state["pad_free"])]
                    xs = [times_row(b, m, xpad[:, j, 2:2 + S], rrow[:, :], [norm.row_ready] + state["pad_free"])
                          for j, b in enumerate(banks)]
                    pad_free = []
                    for j in range(4):
                        k = g * 4 + j
                        d = dve.do(lambda e, j=j, k=k: e.tensor_scalar(
                            ua[:, j, :], xpad[:, j, 0:S], V("rg_w", k * RG_W), V("rg_b", k), ALU.mult, ALU.add),
                            [xs[j]] + edges + state["ua_free"])
                        for i in range(1, RG_W):
                            d = dve.do(lambda e, j=j, k=k, i=i: e.scalar_tensor_tensor(
                                out=ua[:, j, :], in0=xpad[:, j, i:i + S], scalar=V("rg_w", k * RG_W + i),
                                in1=ua[:, j, :], op0=ALU.mult, op1=ALU.add), [d])
                        ua_ready[k] = d
                        pad_free.append(d)
                    state["pad_free"] = pad_free

                gates, root = {}, {}

                def gate_task(direction, g, which, j):
                    dst, k, b = (R, I)[which], 4 * g + j, others()[j]
                    m = mm(bank[b][:, :], gw[:, 4 * which + j, :], ua[:, j, :], True, True,
                           [got["gates"], ua_ready[k]] + bank_free[b])
                    gates[which, j] = act.do(lambda e: e.activation(
                        dst[:, j, :], bank[b][:, :], ACT.Sigmoid,
                        bias=V("gate_b", (2 * direction + which) * KD + k)), [m] + state["rg_free"])
                    bank_free[b] = [gates[which, j]]
                    state["gw_free"] = [m]

                def decay_task(direction, g):
                    cf = [coef[:, direction * KD + 4 * g + j:direction * KD + 4 * g + j + 1] for j in range(4)]
                    th = [act.do(lambda e, j=j: e.activation(Q[:, j, :], R[:, j, :], ACT.Tanh, scale=cf[j]),
                                 [gates[0, j], got["coef"]] + state["rg_free"]) for j in range(4)]
                    state["ex"] = [act.do(lambda e, j=j: e.activation(R[:, j, :], R[:, j, :], ACT.Exp, scale=cf[j]),
                                          [th[j]]) for j in range(4)]
                    state["iu"] = [dve.do(lambda e, j=j: e.tensor_tensor(I[:, j, :], I[:, j, :], ua[:, j, :], ALU.mult),
                                          [gates[1, j]]) for j in range(4)]
                    state["ua_free"] = state["gw_free"] + state["iu"]

                def root_task(j):
                    s = sqr[0]
                    d = dve.do(lambda e: e.tensor_tensor(s[:, :], R[:, j, :], R[:, j, :], ALU.mult),
                               [state["ex"][j]] + state["sqr_free"])
                    d = dve.do(lambda e: e.scalar_tensor_tensor(
                        out=Q[:, j, :], in0=s[:, :], scalar=1.0, in1=Q[:, j, :], op0=ALU.add, op1=ALU.mult), [d])
                    state["sqr_free"] = [d]
                    root[j] = act.do(lambda e: e.activation(Q[:, j, :], Q[:, j, :], ACT.Sqrt, scale=-1.0), [d])

                def scan_task(direction, g, j):
                    k = 4 * g + j
                    if j == 0:
                        state["rg_free"] = []
                    d = dve.do(lambda e: e.tensor_tensor(I[:, j, :], I[:, j, :], Q[:, j, :], ALU.mult),
                               [root[j], state["iu"][j]])
                    if direction == 0:
                        d = dve.do(lambda e: e.tensor_tensor_scan(
                            ya[:, k, :], R[:, j, :], I[:, j, :], 0.0, ALU.mult, ALU.add), [d])
                    else:
                        s = dve.do(lambda e: e.tensor_tensor_scan(
                            Q[:, j, ::-1], R[:, j, ::-1], I[:, j, ::-1], 0.0, ALU.mult, ALU.add), [d])
                        d = dve.do(lambda e: e.tensor_tensor(ya[:, k, :], ya[:, k, :], Q[:, j, :], ALU.add),
                                   [s, ya_ready[k]])
                    ya_ready[k] = d
                    state["rg_free"].append(d)

                def lru(direction, g):
                    in_slots([(gate_task, direction, g, w, j) for w in range(2) for j in range(4)], 2)
                    in_slots([(decay_task, direction, g)], 1)
                    in_slots([(root_task, j) for j in range(4)], 2)
                    in_slots([(scan_task, direction, g, j) for j in range(4)], 1)
                    slots.append(lambda: load_gates(*following[direction, g], state["gw_free"])
                                 if (direction, g) in following else None)

                following = {(0, 0): (1, 0), (1, 0): (0, 1), (0, 1): (1, 1)}
                silu_free = [[], []]

                def silu_of(banks, m, j):
                    s, i = silu[j % 2], j % 2
                    z = times_row(banks[j], m, s[:, :], rrow[:, :], silu_free[i])
                    return act.do(lambda e: e.activation(s[:, :], s[:, :], ACT.Silu), [z])

                sc_free = []
                for g in range(2):
                    banks = four()
                    m = product(f"xa{g}", 0, banks, X, x_ready, True)
                    all_slots()
                    if g == 0:
                        settle(norm.left, act, dve, sp)
                        load_gates(0, 0, [])
                    long_conv(g, banks, m)

                    slots.append(make_coef if g == 0 else None)
                    slots.extend([None] * 3)
                    lru(0, g)
                    lru(1, g)
                    banks = four()
                    m = product(f"gc{g}", 0, banks, X, x_ready, True)
                    edges = [dve.do(lambda e: e.memset(xpad[:, :, 0:1], 0.0), state["pad_free"]),
                             dve.do(lambda e: e.memset(xpad[:, :, S + 1:S + 2], 0.0), state["pad_free"])]
                    cs = [times_row(b, m, xpad[:, j, 1:1 + S], rrow2[:, :], [norm.row2_ready] + state["pad_free"])
                          for j, b in enumerate(banks)]
                    banks = four()
                    m = product(f"xb{g}", 0, banks, X, x_ready, True)
                    acc, pad_free = [], []
                    for j, b in enumerate(banks):
                        k = 4 * g + j
                        d = dve.do(lambda e, j=j, b=b: e.tensor_tensor(
                            xpad[:, j, 1:1 + S], bank[b][:, :], xpad[:, j, 1:1 + S], ALU.mult), [m, cs[j]])
                        bank_free[b] = [d]
                        acc.append(d)
                    for j in range(4):
                        k = 4 * g + j
                        d = dve.do(lambda e, j=j, k=k: e.tensor_scalar(
                            sc[:, j, :], xpad[:, j, 0:S], V("sc_w", k * SC_W), None, ALU.mult),
                            [acc[j]] + edges + sc_free)
                        for i in range(1, SC_W):
                            d = dve.do(lambda e, j=j, k=k, i=i: e.scalar_tensor_tensor(
                                out=sc[:, j, :], in0=xpad[:, j, i:i + S], scalar=V("sc_w", k * SC_W + i),
                                in1=sc[:, j, :], op0=ALU.mult, op1=ALU.add), [d])
                        pad_free.append(d)
                        acc[j] = d
                    state["pad_free"] = pad_free
                    banks = four()
                    m = product(f"gb{g}", 0, banks, X, x_ready, True)
                    for j, b in enumerate(banks):
                        d = dve.do(lambda e, j=j, b=b: e.tensor_tensor(
                            sc[:, j, :], bank[b][:, :], sc[:, j, :], ALU.mult), [m, acc[j]])
                        bank_free[b] = [d]
                        acc[j] = pool.do(lambda e, j=j: e.tensor_tensor(
                            sc[:, j, :], sc[:, j, :], rrow[:, :], ALU.mult), [d])
                    banks = four()
                    m = product(f"zb{g}", 0, banks, X, x_ready, True)
                    sc_free = []
                    for j in range(4):
                        k = 4 * g + j
                        s = silu_of(banks, m, j)
                        d = dve.do(lambda e, j=j: e.tensor_tensor(sc[:, j, :], sc[:, j, :], silu[j % 2][:, :], ALU.mult),
                                   [s, acc[j]])
                        silu_free[j % 2] = [d]
                        yb_ready[k] = split_sbuf(sc[:, j, :], YBH[:, k, :], YBL[:, k, :], [d])
                        sc_free += yb_ready[k]
                    if g == 0:
                        all_slots()

                za_marks = []
                for g in range(2):
                    banks = four()
                    m = product(f"za{g}", 0, banks, X, x_ready, True)
                    all_slots()
                    for j in range(4):
                        k = 4 * g + j
                        s = silu_of(banks, m, j)
                        d = dve.do(lambda e, j=j, k=k: e.tensor_tensor(
                            ya[:, k, :], ya[:, k, :], silu[j % 2][:, :], ALU.mult), [s, ya_ready[k]])
                        silu_free[j % 2] = [d]
                        za_marks.append(d)
                yax = [split_sbuf(ya[:, k, :], XH[:, k, :], XL[:, k, :], [za_marks[k], m]) for k in range(KD)]
                load_table("sqrt_and_others")
                post = Post([R, I], norm.at, got["row"], state["rg_free"])
                b0 = four()
                product("eout_b0", 0, b0, (YBH, YBL), yb_ready, False, True, False)
                m0 = product("eout_a0", 0, b0, X, yax, False, False, True)
                slots.extend([lambda t=t: post.take(0, t, b0, m0) for t in range(T)])
                b1 = four()
                m1 = product("eout_a1", 0, b1, X, yax, False, True, False)
                nxt = Norm(lambda k: V("odd_g", k), [m1])
                all_slots()
                split_ahead()
                ahead, updated = others(), [[], []]

                def turn_tile(t):
                    for k, b in enumerate(ahead):
                        turned[k] = turn(bank[b][:, t * P:(t + 1) * P], H[:, t, k * P:(k + 1) * P],
                                         updated[0][t] + bank_free[b])

                def tile_done(t, mark):
                    if t == T - 1:
                        split_ahead(2)
                    post.take(1, t, b1, mark)
                    post.root(t)
                    for n in range(2):
                        updated[n].append([post.add(t, n, shared=t == T - 1 and n == 1)])
                    if t:
                        turn_tile(t - 1)

                turned = [None] * 4
                product_by_tokens("eout_b1", b1, (YBH, YBL), yb_ready, tile_done, first=False)
                turn_tile(T - 1)
                for k, b in enumerate(ahead):
                    nxt.x_ready.append(split_bank(b, bank[b][:, :], XH[:, k, :], XL[:, k, :], nxt.gain(k),
                                                  [turned[k], gains_in, m1]))
                split_ahead()
                nxt.marks = [updated[0]]
                nxt.add_squares(0)
                nxt.half(1, updated[1])
            nxt.left = gone()
            return nxt

        class Post:

            def __init__(self, buffers, at, gain_in, free):
                self.buf, self.at, self.gain_in, self.free = buffers, at, gain_in, free
                self.sums, self.taken = [], {}

            def take(self, n, t, banks, m):
                b = banks[t]
                s = squares(bank[b][:, :], norm_stat[:, self.at, 4 + n, t:t + 1], [m])
                d = dve.do(lambda e: e.tensor_tensor(self.buf[n][:, t, :], bank[b][:, :],
                                                     gain_row[:, n * 512:(n + 1) * 512], ALU.mult),
                           [s, self.gain_in] + self.free)
                bank_free[b] = [d]
                self.sums.append(s)
                self.taken[n, t] = d

            def root(self, t=None):
                at = slice(0, T) if t is None else slice(t, t + 1)
                c4, c5, c6 = (norm_stat[:, self.at, c, at] for c in (4, 5, 6))
                both = dve.do(lambda e: e.tensor_tensor(c6, c4, c5, ALU.add), self.sums)
                self.ready = inverse_root(c6, c6, D, [both])

            def add(self, t, n, shared=None):
                hh = H[:, t, n * 512:(n + 1) * 512]
                z, r = self.buf[n][:, t, :], norm_stat[:, self.at, 6, t:t + 1]
                if shared if shared is not None else t == T - 1:
                    m = act.do(lambda e: e.activation(z, z, ACT.Copy, scale=r), [self.ready, self.taken[n, t]])
                    return pool.do(lambda e: e.tensor_tensor(hh, hh, z, ALU.add), [m])
                return dve.do(lambda e: e.scalar_tensor_tensor(
                    out=hh, in0=z, scalar=r, in1=hh, op0=ALU.mult, op1=ALU.add), [self.ready, self.taken[n, t]])

        def odd_stage(norm):
            scope = ExitStack()
            with scope:
                qT = sb("gla_q", [P, GLA_HEADS, S], scope=scope)
                kT = sb("gla_k", [P, GLA_HEADS, S], scope=scope)
                v = sb("gla_v", [P, T, D], scope=scope)
                r = sb("gla_r", [P, T, D], scope=scope)
                G = sb("gla_g", [P, 2, GLA_HEADS, S], scope=scope)
                e1 = [[sb(f"gla_e1{d}{i}", [P, S], scope=scope) for d in range(2)] for i in range(2)]
                e2 = [[sb(f"gla_e2{d}{i}", [P, S], scope=scope) for d in range(2)] for i in range(2)]
                kst = [sb(f"gla_kst{d}", [P, T, P], scope=scope) for d in range(2)]
                stm = [sb(f"gla_stm{d}", [P, T, P], scope=scope) for d in range(2)]
                stt = sb("gla_state", [P, 2, NCH, GLA_DV], scope=scope)
                dec = sb("gla_decay", [P, 2, 2, NCH], scope=scope)
                ssq = sb("gla_ssq", [P, GLA_HEADS, T], scope=scope)
                head_g = sb("gla_head_gain", [P, GLA_DV], scope=scope)
                lrT = kst[0][0:2 * GLA_RANK, :, :].rearrange("p t n -> p (t n)")
                wg = stt[0:2 * GLA_RANK, :, 0:2, :]
                load_wg, load_head = Landing(sem("wg_landed")), Landing(sem("head_gain_landed"))
                masks = [C("fwd_mask"), C("bwd_mask")]
                keeps = [C("fwd_keep"), C("bwd_keep")]
                x_ready = norm.x_ready
                got, g_ready, q_ready, k_ready, v_ready, r_ready = {}, {}, [], [], [], []
                slots.append(norm.row)

                def feature(name, dst):
                    banks = four()
                    m = product(name, 0, banks, X, x_ready, True)
                    return banks, m, lambda: [times_row(b, m, dst[:, j, :], rrow[:, :], [norm.row_ready])
                                              for j, b in enumerate(banks)]

                _, _, take = feature("gq", qT)
                all_slots()
                settle(norm.left, act, dve, pool, sp)
                q_ready += take()
                head_in = load_head.start(sp, head_g[:, :], a["gla_norm_g"].partition_broadcast(P))
                row_in = load_gain_row("odd_post", [dve.last()])
                zeroed = dve.do(lambda e: e.memset(wg, 0.0))
                for d in range(2):
                    wg_in = load_wg.start(sp, stt[d * GLA_RANK:(d + 1) * GLA_RANK, d, 0:2, :],
                                          a["gla_w_gate_lr_2"][0, d].rearrange("r (c n) -> r c n", n=GLA_DV), [zeroed])

                banks = four()
                m = product("lr", 0, banks[:1], X, x_ready, True)
                b = banks[0]
                lr_ready = dve.do(lambda e: e.tensor_tensor(
                    lrT, bank[b][0:2 * GLA_RANK, :], rrow[0:2 * GLA_RANK, :], ALU.mult), [m, norm.row_ready])
                bank_free[b] = [lr_ready]
                load_table("natural_log_exp_and_others")
                z_done = [[], []]
                tmp = [e1[0][0], e1[0][1]]

                def z_task(h, d):
                    b, i, z = others()[(2 * h + d) % 4], d, G[:, d, h, :]
                    wz = stt[0:2 * GLA_RANK, d, h // 2, (h % 2) * P:(h % 2 + 1) * P]
                    m = mm(bank[b][:, :], wz, lrT, True, True, [wg_in, lr_ready] + bank_free[b])
                    m1 = dve.do(lambda e: e.tensor_scalar(
                        z, bank[b][:, :], V("gla_b", d * GLA_HEADS + h), None, ALU.add), [m])
                    bank_free[b] = [m1]
                    m2 = act.do(lambda e: e.activation(tmp[i][:, :], z, ACT.Abs), [m1] + z_done[i])
                    m2 = act.do(lambda e: e.activation(tmp[i][:, :], tmp[i][:, :], ACT.Exp, scale=-1.0), [m2])
                    m2 = act.do(lambda e: e.activation(tmp[i][:, :], tmp[i][:, :], ACT.Ln, bias=1.0), [m2])
                    m3 = dve.do(lambda e: e.scalar_tensor_tensor(
                        out=z, in0=z, scalar=0.0, in1=tmp[i][:, :], op0=ALU.min, op1=ALU.subtract), [m2])
                    z_done[i] = [m3]
                    g_ready[d, h] = dve.do(lambda e: e.tensor_scalar(z, z, 1.0 / GLA_NORM, None, ALU.mult), [m3])
                    got["z"] = [m, m3]

                def chunks(ap):
                    return ap.rearrange("p (c n) -> p c n", n=CHUNK)

                dk_scale = GLA_DK ** -0.5
                free = {}
                ready = {}
                y_marks = [[] for _ in range(T)]

                def decays(h, d):
                    i, g = h % 2, G[:, d, h, :]
                    a1, a2 = e1[i][d], e2[i][d]
                    before = free.get(("e", i, d), got["z"])
                    sl = (lambda x: x) if d == 0 else (lambda x: x[:, ::-1])
                    at = CHUNK - 1 if d == 0 else 0
                    m = dve.do(lambda e: e.tensor_tensor_scan(sl(g), sl(keeps[d]), sl(g), 0.0, ALU.mult, ALU.add),
                               [g_ready[d, h], con2_in])
                    x1 = act.do(lambda e: e.activation(a1[:, :], g, ACT.Exp), [m] + before)
                    x2 = act.do(lambda e: e.activation(a2[:, :], g, ACT.Exp, scale=-1.0), [m] + before)
                    ready["dec", h, d] = dve.do(lambda e: e.tensor_copy(dec[:, i, d, :], chunks(a1[:, :])[:, :, at]),
                                                [x1] + before)
                    total = dve.do(lambda e: e.tensor_copy(tot[:, d, :], chunks(g)[:, :, at]), [m] + free.get(("tot", d), []))
                    df = dve.do(lambda e: e.tensor_tensor(
                        chunks(g), tot[:, d, :].unsqueeze(2).broadcast_to([P, NCH, CHUNK]), chunks(g), ALU.subtract),
                        [total, x1, x2])
                    free["tot", d] = [df]
                    x3 = act.do(lambda e: e.activation(g, g, ACT.Exp), [df])
                    ready["q", h, d] = dve.do(lambda e: e.scalar_tensor_tensor(
                        out=a1[:, :], in0=qT[:, h, :], scalar=dk_scale, in1=a1[:, :], op0=ALU.mult, op1=ALU.mult),
                        [ready["dec", h, d], q_ready[h]])
                    ready["k", h, d] = dve.do(lambda e: e.tensor_tensor(a2[:, :], kT[:, h, :], a2[:, :], ALU.mult),
                                              [x2, k_ready[h]])
                    ready["s", h, d] = dve.do(lambda e: e.tensor_tensor(g, kT[:, h, :], g, ALU.mult), [x3])

                tot = sb("gla_total", [P, 2, NCH], scope=scope)

                def intra(h, d):
                    i, b, b2 = h % 2, 4 + d, 6 + d
                    for t in range(T):
                        m = mm(bank[b][:, t * P:(t + 1) * P], e2[i][d][:, t * P:(t + 1) * P],
                               e1[i][d][:, t * P:(t + 1) * P], True, True,
                               [ready["q", h, d], ready["k", h, d]] + bank_free[b])
                    for t in range(T):
                        m2 = turn(bank[b2][:, t * P:(t + 1) * P], G[:, d, h, t * P:(t + 1) * P],
                                  [ready["s", h, d]] + bank_free[b2])
                    ready["stm", d] = dve.do(lambda e: e.tensor_tensor(
                        stm[d][:, :, :], bank[b][:, :].rearrange("p (t n) -> p t n", n=P),
                        masks[d].unsqueeze(1).broadcast_to([P, T, P]), ALU.mult), [m, con2_in] + free.get("out", []))
                    bank_free[b] = [ready["stm", d]]
                    if d == 1:
                        ready["sum"] = dve.do(lambda e: e.tensor_tensor(
                            stm[0][:, :, :], stm[0][:, :, :], stm[1][:, :, :], ALU.add),
                            [ready["stm", 0], ready["stm", 1]])
                    ready["kst", d] = act.do(lambda e: e.activation(
                        kst[d][:, :, :].rearrange("p t n -> p (t n)"), bank[b2][:, :], ACT.Copy),
                        [m2] + free.get("out", got["z"]))
                    bank_free[b2] = [ready["kst", d]]

                def states(h, d, quad):
                    i = h % 2
                    order = list(range(NCH)) if d == 0 else list(range(NCH - 1, -1, -1))
                    four_n = [n for n in range(4 * quad, 4 * quad + 4) if n < NCH - 1]
                    pair, place = (4, 5) if (quad + d) % 2 == 0 else (6, 7), {}
                    for n in four_n:
                        c = order[n]
                        b, col, p0 = pair[n % 2], (n // 2) % 2 * GLA_DV, (c % 2) * CHUNK
                        place[n] = bank[b][:, col:col + GLA_DV]
                        m = mm(place[n], kst[d][p0:p0 + CHUNK, c // 2, :],
                               v[p0:p0 + CHUNK, c // 2, h * GLA_DV:(h + 1) * GLA_DV], True, True,
                               [ready["kst", d]] + v_ready[(h // 2) * T:(h // 2 + 1) * T] + bank_free[b])
                    reads = []
                    for n in four_n:
                        dst, c = stt[:, d, order[n + 1], :], order[n]
                        after = [m] + free.get("out", got["z"])
                        if n == 0:
                            s = dve.do(lambda e, src=place[n], dst=dst: e.tensor_copy(dst, src), after)
                        else:
                            s = dve.do(lambda e, src=place[n], dst=dst, c=c: e.scalar_tensor_tensor(
                                out=dst, in0=stt[:, d, c, :], scalar=dec[:, i, d, c:c + 1], in1=src,
                                op0=ALU.mult, op1=ALU.add), after + [ready["st", d, c], ready["dec", h, d]])
                        ready["st", d, order[n + 1]] = s
                        reads.append(s)
                    for b in pair:
                        bank_free[b] = list(reads)

                def outputs(h, t):
                    i, b = h % 2, 4 + t
                    o, vv = bank[b][:, 0:GLA_DV], v[:, t, h * GLA_DV:(h + 1) * GLA_DV]
                    mm(o, stm[0][:, t, :], vv, True, False, [ready["sum"]] + bank_free[b])
                    for c in (2 * t, 2 * t + 1):
                        both = [d for d in range(2) if c != (0 if d == 0 else NCH - 1)]
                        p0 = (c % 2) * CHUNK
                        for d in both:
                            m = mm(bank[b][p0:p0 + CHUNK, 0:GLA_DV], e1[i][d][:, c * CHUNK:(c + 1) * CHUNK],
                                   stt[:, d, c, :], False, d == both[-1], [ready["st", d, c]])
                    ready["out", t] = m
                    if t == T - 1:
                        free["out"] = free["e", i, 0] = free["e", i, 1] = [m]

                def head_out(h, t):
                    b, rr, ss = 4 + t, r[:, t, h * GLA_DV:(h + 1) * GLA_DV], ssq[:, h, t:t + 1]
                    m = squares(bank[b][:, 0:GLA_DV], ss, [ready["out", t]])
                    m = inverse_root(ss, ss, GLA_DV, [m])
                    m = dve.do(lambda e: e.scalar_tensor_tensor(
                        out=rr, in0=bank[b][:, 0:GLA_DV], scalar=ss, in1=rr, op0=ALU.mult, op1=ALU.mult),
                        [m, r_ready[(h // 2) * T + t]])
                    bank_free[b] = [m]
                    y_marks[t].append(m)

                def tokens(name, n, dst, func, marks):
                    banks = four()
                    m = product(name, 0, banks, X, x_ready, False)
                    for t, b in enumerate(banks):
                        o = dst[:, t, n * 512:(n + 1) * 512]
                        d = act.do(lambda e, t=t, b=b, o=o: e.activation(o, bank[b][:, :], func, scale=norm.r(t)), [m])
                        bank_free[b] = [d]
                        if dst is r:
                            oo = o.rearrange("p (h n) -> p h n", n=GLA_DV)
                            d = dve.do(lambda e, oo=oo: e.tensor_tensor(
                                oo, oo, head_g[:, :].unsqueeze(1).broadcast_to([P, 2, GLA_DV]), ALU.mult), [d, head_in])
                        marks.append(d)
                    return m

                zs = [(z_task, h, d) for h in range(GLA_HEADS) for d in range(2)]
                slots.extend([None, None])
                in_slots(zs, 1)
                _, _, take = feature("gk", kT)
                k_ready += take()
                tokens("gr0", 0, r, ACT.Silu, r_ready)
                all_slots()
                load_table("natural_log_exp_and_others")

                product_banks([0, 1, 2, 3])
                core = {h: ([(intra, h, 0), (intra, h, 1)]
                            + [(states, h, d, quad) for quad in range(2) for d in range(2)]
                            + [(f, h, t) for t in range(T) for f in (outputs, head_out)]) for h in range(GLA_HEADS)}
                pre = {h: [(decays, h, d) for d in range(2)] for h in range(GLA_HEADS)}
                slots.extend([None, None])
                in_slots(pre[0] + core[0][:2], 1)
                tokens("gv0", 0, v, ACT.Copy, v_ready)
                all_slots()
                in_slots(core[0][2:6] + pre[1] + core[0][6:] + core[1][:2], 2)
                tokens("gv1", 1, v, ACT.Copy, v_ready)
                all_slots()
                in_slots(core[1][2:6] + pre[2] + core[1][6:] + core[2][:6], 3)
                x_free = [tokens("gr1", 1, r, ACT.Silu, r_ready)]
                all_slots()
                y_ready = []

                def turn_y(k):
                    turn_and_split(r, k, [[y_marks[t][k // 2]] for t in range(T)], None, x_free, y_ready)

                for k in range(4):
                    turn_y(k)
                in_slots(pre[3] + core[2][6:] + [(turn_y, 4), (turn_y, 5)], 4)
                in_slots(core[3] + [(turn_y, 6), (turn_y, 7)], 4)
                b0 = four()
                m0 = product("oout0", 0, b0, X, y_ready, False)
                all_slots()
                product_banks(list(range(8)), 4)
                post = Post([qT, kT], norm.at, row_in, [dve.last()])
                queue_splits(len(stream))
                for t in range(T):
                    post.take(0, t, b0, m0)
                out_landed = Landing(sem("out_landed"))
                b1 = four()

                def tile_done(t, mark):
                    post.take(1, t, b1, mark)
                    post.root(t)
                    marks = [post.add(t, n, shared=t == T - 1 and n == 1) for n in range(2)]
                    out_landed.start(sp, out[0, t * P:(t + 1) * P, :], H[:, t, :], marks)

                product_by_tokens("oout1", b1, X, y_ready, tile_done)
                sp.wait((out_landed.sem, out_landed.count))

        queue_loads(1)
        for _ in range(3):
            load_x_quarter()
        queue_loads(RAW)
        con2_in = load_con2.start(sp, con[:, 2 * P:], a["constants"][:, 2 * P:])
        norm = start_norm()
        norm = dsa_stage(norm)
        norm = mlp_stage(0, norm, lambda k: V("mix_g1", k))
        norm = conv_stage(norm)
        norm = mlp_stage(1, norm, lambda k: final_even[:, k:k + 1])
        norm = even_stage(norm)
        odd_stage(norm)
        assert state["used"] == len(stream)

        block = ctx.enter_context(nc.Block())

        @block.sync
        def _(e):
            sp.play(e)

        @block.scalar
        def _(e):
            act.play(e)

        @block.gpsimd
        def _(e):
            pool.play(e)

        @block.vector
        def _(e):
            dve.play(e)

        @block.tensor
        def _(e):
            pe.play(e)


def constants():
    i = np.arange(P)
    same = (i[:, None] // CHUNK) == (i[None, :] // CHUNK)
    parts = {
        "ident": np.eye(P),
        "mean": np.full((P, P), 1.0 / D),
        "fwd_mask": same & (i[None, :] >= i[:, None]),
        "bwd_mask": same & (i[None, :] <= i[:, None]),
        "causal": np.where(i[None, :] <= i[:, None], 0.0, -BIG),
        "fwd_keep": np.tile((np.arange(S) % CHUNK != 0)[None], (P, 1)),
        "bwd_keep": np.tile((np.arange(S) % CHUNK != CHUNK - 1)[None], (P, 1)),
    }
    return np.concatenate([parts[n].astype(np.float32) for n, _ in CON_SIZES], axis=1)


def columns(x):
    return np.ascontiguousarray(np.asarray(x).reshape(-1, P).T)


def taps(w):
    w = np.asarray(w)
    return np.ascontiguousarray(w.reshape(w.shape[0], -1, P).transpose(2, 1, 0)).reshape(P, -1)


def kernel(**inputs):
    import concourse.bacc as bacc
    from concourse.bass_utils import run_bass_kernel_spmd

    x = {k: np.asarray(v) for k, v in inputs.items()}
    vectors = {
        "mix_g0": columns(x["norm_mix_g"][0]), "mix_g1": columns(x["norm_mix_g"][1]),
        "mlp_g0": columns(x["norm_mlp_g"][0]), "mlp_g1": columns(x["norm_mlp_g"][1]),
        "pw1_b": columns(x["conv_b_pw1"][0]), "dw_w": taps(x["conv_w_dw"][0]),
        "dw_b": columns(x["conv_b_dw"][0]), "ln_g": columns(x["conv_ln_g"][0]),
        "ln_b": columns(x["conv_ln_b"][0]),
        "idx_g": columns(np.concatenate([x["dsa_idx_k_g"][0]] * 2)),
        "idx_b": columns(np.concatenate([x["dsa_idx_k_b"][0]] * 2)),
        "even_g": columns(x["even_norm_pre_2"][0]), "rg_w": taps(x["rg_conv_w_2"][0]),
        "rg_b": columns(x["rg_conv_b_2"][0]), "gate_b": columns(x["rg_gate_b_2"][0]),
        "lam": columns(x["rg_lambda_2"][0]), "sc_w": taps(x["sc_conv_w_2"][0]),
        "final_g": columns(x["final_g"]),
        "odd_g": columns(x["odd_norm_pre_2"][0]), "gla_b": columns(x["gla_b_gate_2"][0]),
    }
    arrays = {
        "x": x["x"],
        "vectors": np.concatenate([vectors[n] for n, _ in VEC_SIZES], axis=1),
        "constants": constants(),
        "b_pw2": x["conv_b_pw2"][0], "final_g": x["final_g"], "even_post": x["even_norm_post_2"][0],
        "odd_post": x["odd_norm_post_2"][0], "gla_norm_g": x["gla_norm_g_2"][0],
    }
    for name in ("dsa_w_in", "dsa_w_out", "mlp_w1", "mlp_w2", "conv_w_pw1", "conv_w_pw2", "even_w_in_2",
                 "even_w_out_2", "rg_gate_w_2", "odd_w_in_2", "odd_w_out_2", "gla_w_gate_lr_2"):
        arrays[name] = x[name]
    arrays = {k: np.ascontiguousarray(v) for k, v in arrays.items()}

    nc = bacc.Bacc("TRN2", target_bir_lowering=False, num_devices=1,
                   dynamic_dma_scratch_size=1024)
    a = {k: nc.dram_tensor(f"in_{k}", v.shape, mybir.dt.from_np(v.dtype), kind="ExternalInput").ap()
         for k, v in arrays.items()}
    out = nc.dram_tensor("out", (1, S, D), F32, kind="ExternalOutput").ap()
    build(nc, a, out)
    result = run_bass_kernel_spmd(nc, [{f"in_{k}": v for k, v in arrays.items()}], core_ids=[0])
    return result.results[0]["out"]
```
